# Optimizing a Trainium2 kernel written in Bass

```python
import math
import jax
import jax.numpy as jnp
from jax import lax
import numpy as np

D_MODEL = 1024
BATCH = 1
SEQ = 256
DEPTH = 1
DEC_BATCH = 8
DEC_SEQ = 16
PAST_LEN = 512

CHUNK = 64
DK_A = 128
DV_A = 128
H_A = (D_MODEL // 2) // DV_A
QK_A = H_A * DK_A
V_A = H_A * DV_A
QKV_A = 2 * QK_A + V_A
CONV_W = 4
N_B = 64
H_B = (D_MODEL // 2) // N_B
D_B = H_B * N_B
W_LORA = 64
A_LORA = 64
G_LORA = 128
SHIFT_W = 3 * D_B + W_LORA + A_LORA + G_LORA
OFF_ALPHA = QKV_A
OFF_BETA = OFF_ALPHA + H_A
OFF_Z = OFF_BETA + H_A
OFF_RWKV = OFF_Z + V_A
OFF_MERGE = OFF_RWKV + SHIFT_W
IN_W = OFF_MERGE + 2 * D_MODEL
N_EXPERTS = 64
TOP_K = 8
N_GROUPS = 8
TOPK_GROUPS = 4
D_EXPERT = 256
D_SHARED = 256
ROUTED_SCALE = 2.5
DN_ALPHA = (2 * DEPTH) ** 0.25
DN_BETA = (8 * DEPTH) ** -0.25
LN_EPS = 1e-5
GN_EPS = 64e-5
RMS_EPS = 1e-6

kernel_name = 'hybrid_gdn_rwkv7_moe_stream_step'

def _layernorm(x, g, b):
    xf = x.astype(jnp.float32)
    mu = jnp.mean(xf, -1, keepdims=True)
    var = jnp.mean(jnp.square(xf - mu), -1, keepdims=True)
    return ((xf - mu) * lax.rsqrt(var + LN_EPS) * g + b).astype(x.dtype)

def _l2norm(x):
    return x * lax.rsqrt(jnp.sum(x * x, -1, keepdims=True) + 1e-6)

def _causal_conv(u, buf, w):
    up = jnp.concatenate([buf, u], axis=1)
    out = lax.conv_general_dilated(up, w[:, None, :], window_strides=(1,), padding='VALID',
                                   dimension_numbers=('NWC', 'WIO', 'NWC'),
                                   feature_group_count=u.shape[-1])
    return out, up[:, -(CONV_W - 1):]

def _gated_delta_chunked(q, k, v, g, beta, S0):
    B, L, H, DK = q.shape
    DV = v.shape[-1]
    C = CHUNK if L % CHUNK == 0 else L
    N = L // C

    def blocks(t):
        return t.reshape(B, N, C, H, -1).transpose(1, 0, 3, 2, 4)

    qc = blocks(q * DK ** -0.5)
    kc = blocks(k)
    vc = blocks(v)
    gc = blocks(g[..., None])[..., 0]
    bc = blocks(beta[..., None])[..., 0]
    G = jnp.cumsum(gc, axis=-1)
    incl = jnp.tril(jnp.ones((C, C), bool))
    strict = jnp.tril(jnp.ones((C, C), bool), -1)
    diff = G[..., :, None] - G[..., None, :]
    decay = jnp.where(incl, jnp.exp(jnp.where(incl, diff, 0.0)), 0.0)
    kk = jnp.einsum('nbhid,nbhjd->nbhij', kc, kc)
    lower = jnp.where(strict, bc[..., :, None] * kk * decay, 0.0) + jnp.eye(C, dtype=jnp.float32)
    rhs = jnp.concatenate([vc * bc[..., None], kc * (bc * jnp.exp(G))[..., None]], axis=-1)
    sol = lax.linalg.triangular_solve(lower, rhs, left_side=True, lower=True, unit_diagonal=True)
    u, w = sol[..., :DV], sol[..., DV:]
    qk = jnp.einsum('nbhid,nbhjd->nbhij', qc, kc) * decay
    qg = qc * jnp.exp(G)[..., None]
    kd = kc * jnp.exp(G[..., -1:] - G)[..., None]
    gl = jnp.exp(G[..., -1])

    def step(S, xs):
        u_n, w_n, qk_n, qg_n, kd_n, gl_n = xs
        v_new = u_n - jnp.einsum('bhck,bhkv->bhcv', w_n, S)
        o_n = jnp.einsum('bhck,bhkv->bhcv', qg_n, S) + jnp.einsum('bhij,bhjv->bhiv', qk_n, v_new)
        S = S * gl_n[..., None, None] + jnp.einsum('bhck,bhcv->bhkv', kd_n, v_new)
        return S, o_n

    S, o = lax.scan(step, S0, (u, w, qk, qg, kd, gl))
    return o.transpose(1, 0, 3, 2, 4).reshape(B, L, H, DV), S

def _rwkv7_scan(r, decay, k, v, kk, a, S0):
    def step(S, xs):
        r_t, d_t, k_t, v_t, kk_t, a_t = xs
        sa = jnp.einsum('bhvk,bhk->bhv', S, -kk_t)
        S = (S * d_t[:, :, None, :] + sa[..., None] * (kk_t * a_t)[:, :, None, :]
             + v_t[..., None] * k_t[:, :, None, :])
        return S, jnp.einsum('bhvk,bhk->bhv', S, r_t)

    xs = tuple(jnp.swapaxes(t, 0, 1) for t in (r, decay, k, v, kk, a))
    S, y = lax.scan(step, S0, xs)
    return jnp.swapaxes(y, 0, 1), S

def _gdn_branch(proj, conv_buf, S0, p):
    B, L, _ = proj.shape
    qkv, conv_new = _causal_conv(proj[..., :OFF_ALPHA], conv_buf.astype(jnp.float32),
                                 p['conv_w'].astype(jnp.float32))
    qkv = jax.nn.silu(qkv)
    q = _l2norm(qkv[..., :QK_A].reshape(B, L, H_A, DK_A))
    k = _l2norm(qkv[..., QK_A:2 * QK_A].reshape(B, L, H_A, DK_A))
    v = qkv[..., 2 * QK_A:].reshape(B, L, H_A, DV_A)
    g = -jnp.exp(p['a_log'].astype(jnp.float32)) * jax.nn.softplus(proj[..., OFF_ALPHA:OFF_BETA] + p['dt_bias'])
    beta = jax.nn.sigmoid(proj[..., OFF_BETA:OFF_Z])
    o, S = _gated_delta_chunked(q, k, v, g, beta, S0.astype(jnp.float32))
    z = proj[..., OFF_Z:OFF_RWKV].reshape(B, L, H_A, DV_A)
    o = o * lax.rsqrt(jnp.mean(o * o, -1, keepdims=True) + RMS_EPS) * p['gdn_norm_w'] * jax.nn.silu(z)
    return o.reshape(B, L, V_A), conv_new, S

def _rwkv7_branch(proj, shift_buf, S0, p):
    B, L, _ = proj.shape
    cur = proj[..., OFF_RWKV:OFF_MERGE]
    seq = jnp.concatenate([shift_buf.astype(jnp.float32), cur], axis=1)
    mixed = cur + (seq[:, :-1] - cur) * p['mu_shift']
    shift_new = seq[:, -1:]
    r, k, v, wl, al, gl = jnp.split(
        mixed, [D_B, 2 * D_B, 3 * D_B, 3 * D_B + W_LORA, 3 * D_B + W_LORA + A_LORA], axis=-1)
    w = -jax.nn.softplus(-(p['w0'] + jnp.tanh(wl) @ p['w2'])) - 0.5
    decay = jnp.exp(-jnp.exp(w))
    a = jax.nn.sigmoid(p['a0'] + al @ p['a2'])
    gate = jax.nn.sigmoid(gl) @ p['g2']

    def heads(t):
        return t.reshape(B, L, H_B, N_B)

    kk = _l2norm(heads(k * p['k_k']))
    k = k * (1.0 + (a - 1.0) * p['k_a'])
    rh, kh, vh = heads(r), heads(k), heads(v)
    y, S = _rwkv7_scan(rh, heads(decay), kh, vh, kk, heads(a), S0.astype(jnp.float32))
    mu = jnp.mean(y, -1, keepdims=True)
    var = jnp.mean(jnp.square(y - mu), -1, keepdims=True)
    y = ((y - mu) * lax.rsqrt(var + GN_EPS)).reshape(B, L, D_B) * p['lnx_g'] + p['lnx_b']
    y = y + (jnp.sum(rh * kh * p['r_k'], -1, keepdims=True) * vh).reshape(B, L, D_B)
    return y * gate, shift_new, S

def _moe(h, p):
    B, L, D = h.shape
    scores = jax.nn.sigmoid((h @ p['router_w']).astype(jnp.float32))
    choice = scores + p['router_bias'].astype(jnp.float32)
    grp = choice.reshape(B, L, N_GROUPS, N_EXPERTS // N_GROUPS)
    grp_score = jnp.sum(lax.top_k(grp, 2)[0], -1)
    _, gidx = lax.top_k(grp_score, TOPK_GROUPS)
    gmask = jnp.sum(jax.nn.one_hot(gidx, N_GROUPS, dtype=jnp.float32), -2) > 0
    emask = jnp.repeat(gmask, N_EXPERTS // N_GROUPS, axis=-1)
    _, eidx = lax.top_k(jnp.where(emask, choice, -jnp.inf), TOP_K)
    wsel = jnp.take_along_axis(scores, eidx, axis=-1)
    wsel = ROUTED_SCALE * wsel / (jnp.sum(wsel, -1, keepdims=True) + 1e-20)
    gates = jnp.einsum('blk,blke->ble', wsel,
                       jax.nn.one_hot(eidx, N_EXPERTS, dtype=jnp.float32)).astype(h.dtype)

    def routed(args):
        hs, gs = args
        act = (jax.nn.silu(jnp.einsum('ld,edf->lef', hs, p['we_gate']))
               * jnp.einsum('ld,edf->lef', hs, p['we_up']))
        return jnp.einsum('lef,efd->ld', act * gs[..., None], p['we_down'])

    y = lax.map(routed, (h, gates))
    shared = (jax.nn.silu(h @ p['ws_gate']) * (h @ p['ws_up'])) @ p['ws_down']
    return y + shared

def _layer(x, c, conv_buf, gdn_S, shift_buf, rwkv_S, p):
    D = x.shape[-1]
    mod = jax.nn.silu(c) @ p['w_ada'] + p['b_ada']
    sh1, sc1, ga1, sh2, sc2, ga2 = jnp.split(mod[:, None, :], 6, axis=-1)
    h = x * (1.0 + sc1) + sh1
    proj = (h @ p['w_in']).astype(jnp.float32)
    ya, conv_new, gdn_new = _gdn_branch(proj, conv_buf, gdn_S, p)
    yb, shift_new, rwkv_new = _rwkv7_branch(proj, shift_buf, rwkv_S, p)
    mg = jax.nn.sigmoid(proj[..., OFF_MERGE:])
    merged = (mg[..., :D] * (ya.astype(x.dtype) @ p['p_a'])
              + mg[..., D:] * (yb.astype(x.dtype) @ p['p_b']))
    mix = merged.astype(x.dtype) @ p['w_o']
    x = _layernorm(DN_ALPHA * x + (1.0 + ga1) * mix, p['ln1_g'], p['ln1_b'])
    h2 = x * (1.0 + sc2) + sh2
    x = _layernorm(DN_ALPHA * x + (1.0 + ga2) * _moe(h2, p), p['ln2_g'], p['ln2_b'])
    return (x, conv_new.astype(conv_buf.dtype), gdn_new.astype(gdn_S.dtype),
            shift_new.astype(shift_buf.dtype), rwkv_new.astype(rwkv_S.dtype))

def setup_inputs(seed: int = 0) -> dict:
    key = jax.random.key(seed)
    keys = iter(jax.random.split(key, 64))
    f32 = jnp.float32

    def nrm(shape, scale):
        return scale * jax.random.normal(next(keys), shape, f32)

    def unif(shape, lo, hi):
        return jax.random.uniform(next(keys), shape, f32, lo, hi)

    L, D = DEPTH, D_MODEL
    dt = jnp.exp(unif((L, H_A), math.log(1e-3), math.log(1e-1)))
    w0_base = jnp.broadcast_to(jnp.linspace(-6.0, -1.0, N_B, dtype=f32), (L, H_B, N_B)).reshape(L, D_B)
    return {
        'x_prompt': nrm((BATCH, SEQ, D), 1.0),
        'x_sample': nrm((DEC_BATCH, DEC_SEQ, D), 1.0),
        'c_prompt': nrm((BATCH, D), 1.0),
        'c_sample': nrm((DEC_BATCH, D), 1.0),
        'state_gdn_conv': nrm((L, DEC_BATCH, CONV_W - 1, QKV_A), 1.0),
        'state_gdn': nrm((L, DEC_BATCH, H_A, DK_A, DV_A), 0.1),
        'state_rwkv_shift': nrm((L, DEC_BATCH, 1, SHIFT_W), 1.0),
        'state_rwkv': nrm((L, DEC_BATCH, H_B, N_B, N_B), 0.1),
        'w_ada': nrm((L, D, 6 * D), 0.1 * D ** -0.5),
        'b_ada': nrm((L, 6 * D), 0.02),
        'w_in': nrm((L, D, IN_W), D ** -0.5),
        'conv_w': nrm((L, CONV_W, QKV_A), CONV_W ** -0.5),
        'a_log': jnp.log(unif((L, H_A), 1.0, 16.0)),
        'dt_bias': dt + jnp.log(-jnp.expm1(-dt)),
        'gdn_norm_w': 1.0 + nrm((L, DV_A), 0.02),
        'mu_shift': unif((L, SHIFT_W), 0.0, 1.0),
        'w0': w0_base + nrm((L, D_B), 0.1),
        'w2': nrm((L, W_LORA, D_B), 0.1 * W_LORA ** -0.5),
        'a0': nrm((L, D_B), 0.1),
        'a2': nrm((L, A_LORA, D_B), 0.1 * A_LORA ** -0.5),
        'g2': nrm((L, G_LORA, D_B), G_LORA ** -0.5),
        'k_k': 0.85 + nrm((L, D_B), 0.02),
        'k_a': 1.0 + nrm((L, D_B), 0.02),
        'r_k': nrm((L, H_B, N_B), 0.1),
        'lnx_g': 1.0 + nrm((L, D_B), 0.02),
        'lnx_b': nrm((L, D_B), 0.02),
        'p_a': nrm((L, V_A, D), DN_BETA * V_A ** -0.5),
        'p_b': nrm((L, D_B, D), DN_BETA * D_B ** -0.5),
        'w_o': nrm((L, D, D), DN_BETA * D ** -0.5),
        'ln1_g': 1.0 + nrm((L, D), 0.02),
        'ln1_b': nrm((L, D), 0.02),
        'router_w': nrm((L, D, N_EXPERTS), D ** -0.5),
        'router_bias': nrm((L, N_EXPERTS), 0.01),
        'we_gate': nrm((L, N_EXPERTS, D, D_EXPERT), D ** -0.5),
        'we_up': nrm((L, N_EXPERTS, D, D_EXPERT), D ** -0.5),
        'we_down': nrm((L, N_EXPERTS, D_EXPERT, D), DN_BETA * D_EXPERT ** -0.5),
        'ws_gate': nrm((L, D, D_SHARED), D ** -0.5),
        'ws_up': nrm((L, D, D_SHARED), D ** -0.5),
        'ws_down': nrm((L, D_SHARED, D), DN_BETA * D_SHARED ** -0.5),
        'ln2_g': 1.0 + nrm((L, D), 0.02),
        'ln2_b': nrm((L, D), 0.02),
    }

def reference(x_prompt, x_sample, c_prompt, c_sample, state_gdn_conv, state_gdn, state_rwkv_shift,
              state_rwkv, w_ada, b_ada, w_in, conv_w, a_log, dt_bias, gdn_norm_w, mu_shift, w0, w2,
              a0, a2, g2, k_k, k_a, r_k, lnx_g, lnx_b, p_a, p_b, w_o, ln1_g, ln1_b, router_w,
              router_bias, we_gate, we_up, we_down, ws_gate, ws_up, ws_down, ln2_g, ln2_b):
    bp = x_prompt.shape[0]
    dtp = x_prompt.dtype
    yp, ys = x_prompt, x_sample
    new_p = ([], [], [], [])
    new_s = ([], [], [], [])
    for l in range(DEPTH):
        p = {'w_ada': w_ada[l], 'b_ada': b_ada[l], 'w_in': w_in[l], 'conv_w': conv_w[l],
             'a_log': a_log[l], 'dt_bias': dt_bias[l], 'gdn_norm_w': gdn_norm_w[l],
             'mu_shift': mu_shift[l], 'w0': w0[l], 'w2': w2[l], 'a0': a0[l], 'a2': a2[l],
             'g2': g2[l], 'k_k': k_k[l], 'k_a': k_a[l], 'r_k': r_k[l], 'lnx_g': lnx_g[l],
             'lnx_b': lnx_b[l], 'p_a': p_a[l], 'p_b': p_b[l], 'w_o': w_o[l], 'ln1_g': ln1_g[l],
             'ln1_b': ln1_b[l], 'router_w': router_w[l], 'router_bias': router_bias[l],
             'we_gate': we_gate[l], 'we_up': we_up[l], 'we_down': we_down[l],
             'ws_gate': ws_gate[l], 'ws_up': ws_up[l], 'ws_down': ws_down[l],
             'ln2_g': ln2_g[l], 'ln2_b': ln2_b[l]}
        yp, *sp = _layer(yp, c_prompt,
                         jnp.zeros((bp, CONV_W - 1, QKV_A), dtp),
                         jnp.zeros((bp, H_A, DK_A, DV_A), dtp),
                         jnp.zeros((bp, 1, SHIFT_W), dtp),
                         jnp.zeros((bp, H_B, N_B, N_B), dtp), p)
        ys, *ss = _layer(ys, c_sample, state_gdn_conv[l], state_gdn[l], state_rwkv_shift[l],
                         state_rwkv[l], p)
        for lst, val in zip(new_p, sp):
            lst.append(val)
        for lst, val in zip(new_s, ss):
            lst.append(val)
    conv_p, gdn_p, shift_p, rwkv_p = [jnp.stack(t, 0) for t in new_p]
    conv_s, gdn_s, shift_s, rwkv_s = [jnp.stack(t, 0) for t in new_s]
    return (yp, ys, conv_p, gdn_p, shift_p, rwkv_p, conv_s, gdn_s, shift_s, rwkv_s)


_drawn_inputs = setup_inputs


def setup_inputs(seed=0):
    import zlib

    import numpy as np

    out = dict(_drawn_inputs(seed))
    spreads = {}
    factors = {'gdn_norm_w': 5.864,
     'w2': 8.0,
     'k_k': 3.155,
     'k_a': 2.668,
     'lnx_g': 3.717,
     'lnx_b': 3.574,
     'ln2_g': 2.735}
    for name, (base, spread) in spreads.items():
        noise = np.random.default_rng([zlib.crc32(name.encode()), seed]).standard_normal(out[name].shape)
        drawn = base * np.exp(spread * noise) if base else spread * noise
        out[name] = jnp.asarray(drawn.astype(out[name].dtype))
    for name, factor in factors.items():
        out[name] = (out[name] * factor).astype(out[name].dtype)
    return out
```

```python
import concourse.bass as bass
from concourse import mybir
from contextlib import ExitStack

F32 = mybir.dt.float32
I32 = mybir.dt.int32
ALU = mybir.AluOpType
ACT = mybir.ActivationFunctionType
AX = mybir.AxisListType

P = 128
D = 1024
KC = D // P
SEQ = 256
NSEQ, LS = 8, 16
TILES = 3
T = TILES * P
HA = 4
HB, NB = 8, 64
PAIRS = HB // 2
DB = HB * NB
QKV = 3 * HA * P
QB = QKV // P
SHIFT_W = 3 * DB + 64 + 64 + 128
RB = SHIFT_W // P
OFF_ALPHA = QKV
OFF_Z = QKV + 2 * HA
OFF_RWKV = OFF_Z + HA * P
OFF_MERGE = OFF_RWKV + SHIFT_W
NE, NG, TG, DE = 64, 8, 4, 256
GE = NE // NG
ROUTED_SCALE = 2.5
DN_ALPHA = 2 ** 0.25
LN_EPS, GN_EPS, RMS_EPS, L2_EPS = 1e-5, 64e-5, 1e-6, 1e-6
EXP_NEG_HALF = 0.6065306597126334
QW = 3 + SEQ + NSEQ * (LS + 3)
RW = 1 + SEQ + NSEQ * (LS + 1)
ORDER = [2, 0, 1]
LEVELS = [4, 7, 7]
INV0 = [0, 12, 33]
RING = 3
BIG = 1e30
NOWHERE = 65536
N_ACT = 8
ROUND = 6
C_ADA, C_CONV, C_MU, C_W0, C_A0, C_KK, C_KA, C_RK = 0, 48, 96, 110, 114, 118, 122, 126


def hybrid_kernel(nc, x_prompt, x_sample, c_prompt, c_sample, state_gdn_conv, state_gdn,
                  state_rwkv_shift, state_rwkv, w_ada, b_ada, w_in, conv_w, a_log, dt_bias,
                  gdn_norm_w, mu_shift, w0, w2, a0, a2, g2, k_k, k_a, r_k, lnx_g, lnx_b, p_a, p_b,
                  w_o, ln1_g, ln1_b, router_w, router_bias, we_gate, we_up, we_down, ws_gate,
                  ws_up, ws_down, ln2_g, ln2_b,
                  y_p, y_s, conv_p, gdn_p, shift_p, rwkv_p, conv_s, gdn_s, shift_s, rwkv_s):
    ctx = ExitStack()
    with ctx:
        def sb(name, shape):
            return ctx.enter_context(nc.sbuf_tensor(name, shape, F32))

        sems = {}

        def S(name):
            if name not in sems:
                sems[name] = ctx.enter_context(nc.semaphore(name))
            return sems[name]

        class Steps:

            def __init__(self, eng, own):
                self.eng, self.own, self.n = eng, own, {}

            def do(self, ins, name=None, hold=True):
                name = name or self.own
                self.n[name] = self.n.get(name, 0) + 1
                ins.then_inc(S(name), 1)
                if hold:
                    self.eng.wait_ge(S(name), self.n[name])

        def flat(t, n, off=0):
            names = "abcd"[:len(t.shape) - 1]
            ap = t[tuple([slice(None)] * len(t.shape))]
            if len(names) > 1:
                ap = ap.rearrange(f"p {' '.join(names)} -> p ({' '.join(names)})")
            return ap[:, off:off + n]

        ident = sb("ident", [P, P])
        ones = sb("ones", [P, P])
        blk64 = sb("blk64", [P, P])
        lvl = sb("lvl", [P, 7, P])
        masks = sb("masks", [P, 2, 2, P])
        same_seq = sb("same_seq", [P, P])
        seq_cols = sb("seq_cols", [P, NSEQ, P])
        seq_rows = sb("seq_rows", [P, NSEQ])
        head_sel = sb("head_sel", [P, 2])
        req_rows = sb("req_rows", [9, 2, P])
        par = sb("par", [P, 130])
        a_neg = sb("a_neg", [P, HA])
        dtb = sb("dtb", [P, HA])
        gnw = sb("gnw", [P, P])
        lnx = sb("lnx", [P, 2, DB])
        w_ab = sb("w_ab", [P, KC, 2 * HA])
        hT = sb("hT", [P, KC, T])
        cT = sb("cT", [P, KC, 9])
        modT = sb("modT", [P, 48, 9])
        qkv = sb("qkv", [P, QB, QW])
        rwp = sb("rwp", [P, RB, RW])
        zs = sb("zs", [P, TILES, DB])
        gate = sb("gate", [P, TILES, DB])
        ring = sb("ring", [P, RING, KC, 512])
        last_q = sb("last_q", [P, QB, 9, 3])
        last_r = sb("last_r", [P, RB, 9])
        ab = sb("ab", [P, TILES, 2 * HA])
        g_log = sb("g_log", [P, TILES, HA])
        beta = sb("beta", [P, TILES, HA])
        sp_tmp = sb("sp_tmp", [P, 3, TILES, HA])
        F13 = sb("F13", [P, 2, PAIRS, T])
        F1, F3 = F13[:, 0], F13[:, 1]
        c_mid = sb("c_mid", [P, PAIRS, 2])
        e_mid = sb("e_mid", [P, PAIRS, 2])
        e_tot = sb("e_tot", [P, PAIRS, 2])
        e_seq = sb("e_seq", [P, PAIRS, NSEQ])
        bonus = sb("bonus", [P, TILES, HB])
        NT = sb("NT", [P, 512])
        aT = sb("aT", [P, 512])
        MT = sb("MT", [P, HB, 512])
        inv = sb("inv", [P, 4, 3, 512])
        X, XT, T1, NL = inv[:, 0], inv[:, 1], inv[:, 2], inv[:, 3]
        xs = sb("xs", [P, TILES, D])
        states = sb("states", [P, 1024])
        Sg = states[:, 0:512]
        Zb = states[:, 512:1024]
        gc = sb("gc", [P, 40])
        eg = sb("eg", [P, 40])
        neg_eg = sb("neg_eg", [P, HA])
        stat = sb("stat", [P, 3, 16])
        slot_ids = ctx.enter_context(nc.sbuf_tensor("slot_ids", [P, ROUND, 2], I32))
        slot_gate = sb("slot_gate", [P, ROUND])
        most = ctx.enter_context(nc.sbuf_tensor("most", [P, 1], I32))
        tok_id = sb("tok_id", [P, TILES, 2])
        h_rows = nc.dram_tensor("h_rows", [T, D], F32).ap()
        y_rows = nc.dram_tensor("y_rows", [T * N_ACT, D], F32).ap()

        c_sb = flat(MT, D, 1024)[0:9, :]
        mod_row = flat(MT, RING * 512, 1024)[0:9, :].rearrange("p (u n) -> p u n", u=RING)
        col_sel = flat(MT, 15, 896)
        half_sel = flat(MT, 14, 912)
        past_r = flat(MT, P)[0:112, :]
        past_q = flat(MT, 3 * P, P).rearrange("p (a c) -> p a c", a=3)[0:96]
        conv_acc = flat(MT, 2 * T, 1024).rearrange("p (a t) -> p a t", a=2)
        shift_tmp = flat(MT, T)
        keep = flat(MT, T, 512)
        par_a = flat(MT, P, 3584)[0:110, :]
        par_b = flat(MT, P, 3712)[0:20, :]
        cum = flat(inv, PAIRS * T).rearrange("p (b t) -> p b t", b=PAIRS)
        kkn = flat(inv, PAIRS * T, PAIRS * T).rearrange("p (b t) -> p b t", b=PAIRS)
        sq = flat(inv, 2 * PAIRS * T, 2 * PAIRS * T).rearrange("p (b t) -> p b t", b=8)
        w2a2 = flat(MT, DB, 2560)
        g2_sb = flat(MT, DB, 3072)
        rs_tmp = flat(MT, 2 * T, 1792).rearrange("p (a t) -> p a t", a=2)
        DT = flat(xs, 512)
        Vt, R, vn, Kd, Ot = [flat(xs, 512, 512 * i) for i in range(1, 6)]
        gb = Ot
        vt, F3t, F4t, Zp, W1n, sp = [flat(xs, 512, 512 * i) for i in range(6)]
        Ss = flat(ring, 4096).rearrange("p (s h v) -> p s h v", s=NSEQ, h=HA)
        Zs = flat(ring, 4096, 4096).rearrange("p (s b v) -> p s b v", s=NSEQ, b=PAIRS)
        Zraw = flat(ring, 4096, 8192).rearrange("p (s b v) -> p s b v", s=NSEQ, b=PAIRS)
        sm = flat(ring, 4096, 8192).rearrange("p (a w s c) -> p a w s c", a=2, w=2, s=NSEQ)
        zout = flat(MT, 512)
        head_rows = NT[0:8, :]
        len_rows = flat(MT, T, 1792 + T)[0:8, :]
        last_out = flat(inv, 512, 4096)
        yT = flat(inv, 2 * PAIRS * T).rearrange("p (w b t) -> p w b t", w=2, b=4)
        ga_rows = flat(inv, 2048, 3072)[0:9, :]
        sgA = flat(qkv, 8 * T).rearrange("p (b t) -> p b t", b=8)
        sgB = flat(rwp, 8 * T).rearrange("p (b t) -> p b t", b=8)
        merged = flat(MT, 8 * T).rearrange("p (b t) -> p b t", b=8)
        mtmp = flat(MT, 2 * T, 8 * T).rearrange("p (a t) -> p a t", a=2)
        ga_tok = flat(qkv, 4096).rearrange("p (k n) -> p k n", k=2)
        ln_rows = flat(rwp, 4096).rearrange("p (a n) -> p a n", a=4)
        rw_sb = flat(rwp, 512, 4096).rearrange("p (a n) -> p a n", a=KC)
        r_bias = flat(rwp, NE, 4608)
        lt = flat(MT, 1024)
        wd_ring = flat(inv, 6144).rearrange("p (a k n) -> p a k n", a=3, k=2)
        h2_tok = flat(MT, 3 * D).rearrange("p (t n) -> p t n", t=3)
        xt = flat(MT, 2 * D).rearrange("p (a n) -> p a n", a=2)
        hgT = flat(MT, 2 * D, 2 * D).rearrange("p (a k c) -> p a k c", a=2, k=KC)
        obuf = [flat(zs, D), flat(gate, D)]
        sil = flat(zs, 2 * DE, D).rearrange("p (a n) -> p a n", a=2)
        act_t = flat(gate, 2 * DE, D).rearrange("p (a n) -> p a n", a=2)
        actT = flat(rwp, 2 * DE, 4672).rearrange("p (a n) -> p a n", a=2)
        onehot = flat(qkv, 2 * TILES * P, 4096).rearrange("p (a t c) -> p a t c", a=2, t=TILES)
        slot_rows = flat(states, TILES * NE * 3).rearrange("p (t e c) -> p t e c", t=TILES, c=3)
        pos = flat(states, TILES * NE, 576).rearrange("p (t e) -> p t e", t=TILES)
        count_up = flat(states, P, 768)
        rt = flat(NT, 5 * NE).rearrange("p (a e) -> p a e", a=5)
        r8 = flat(NT, 64, 5 * NE)
        g8 = flat(NT, 32, 5 * NE + 64)
        chosen = flat(aT, TILES * NE).rearrange("p (t e) -> p t e", t=TILES)
        y_sh = flat(F13, 3 * D).rearrange("p (t n) -> p t n", t=TILES)
        y_in = flat(ring, 3 * 4096).rearrange("p (a j n) -> p a j n", a=3, j=4)

        bank = [ctx.enter_context(nc.psum_tensor(f"bank{i}", [P, 512], F32)) for i in range(8)]

        def upd_bank(h, j):
            return (6 if h % 2 == 0 else 2) + j

        def seqs(ap, n=LS):
            return ap.rearrange("p (s t) -> p s t", s=NSEQ)

        def tok(t):
            return slice(t * P, (t + 1) * P)

        def col(c):
            return par[:, c:c + 1]

        w_in_v = w_in[0].rearrange("(k p) n -> p k n", p=P)
        w_ada_v = w_ada[0].rearrange("(k p) n -> p k n", p=P)
        w_o_v = w_o[0].rearrange("(k p) n -> p k n", p=P)
        RING_IN = [(OFF_RWKV, 512), (OFF_RWKV + 512, 512), (OFF_RWKV + 1024, 512), (OFF_RWKV + 1536, 256),
                   (OFF_Z, 512), (0, 512), (512, 512), (1024, 512)]
        MERGE_IN = [(OFF_MERGE + 512 * i, 512) for i in range(4)]
        N_ADA = 12
        N_RING = N_ADA + len(RING_IN) + len(MERGE_IN) + 4
        NP_Z, NP_QKV, NP_MG, NP_END = RB, RB + 3, RB + QB + 3, RB + QB + 3 + 16

        def rounds(eng, task, n_task):
            full = (n_task - 3) // ROUND
            for u in range(ROUND):
                task(0, u)
            with eng.Fori(1, full) as i:
                for u in range(ROUND):
                    task(i, u)
            for n in range(full * ROUND, n_task):
                task(n // ROUND, n % ROUND)

        def expert_of(pre, i, u):
            return i * ROUND + u if pre == "a" else i * (ROUND // 2) + u // 2

        def first_slot(pre, u):
            return 0 if pre == "a" else P * (1 + u % 2)

        def weight_slot(pre, u):
            return (u + 1) % 3 if pre == "a" else u % 3

        def done(pre, name, k=0):
            shared = {"gu": 32, "wd": 16}.get(name, 0) if k == 0 else 0
            if pre == "a":
                return shared
            if name in ("xg", "sc"):
                return 16 * NE // 2
            if name in ("gu", "wd"):
                return shared + {"gu": 32, "wd": 16}[name] * sum(weight_slot("a", n) == k for n in range(NE))
            return NE

        block = ctx.enter_context(nc.Block())
        n_const, n_ident = [0], [0]

        @block.gpsimd
        def _(pool):
            st = Steps(pool, "pool_chain")

            def fill(ap, value):
                st.do(pool.memset(ap, value))

            def where(ap, pattern, base, cm, op=ALU.is_ge, other=0.0):
                st.do(pool.affine_select(out=ap, in_=ap, compare_op=op, fill=other, base=base,
                                         pattern=pattern, channel_multiplier=cm))

            def diagonal(ap, lead, n, width):
                where(ap, lead + [[-width, n], [0, width]], 0, 1)
                where(ap, lead + [[width, n], [0, width]], width - 1, -1)

            fill(ident[:, :], 0.0)
            where(ident[:, :], [[-1, P]], 0, 1, ALU.not_equal, 1.0)
            n_ident[0] = st.n["pool_chain"]
            fill(ones[:, :], 1.0)
            fill(blk64[:, :], 1.0)
            diagonal(blk64[:, :].rearrange("p (a b) -> p a b", a=2), [], 2, 64)
            fill(qkv[:, :, 0:3], 0.0)
            fill(rwp[:, :, 0:1], 0.0)
            fill(req_rows[:, :, :], 1.0)
            where(req_rows[:, 0, :], [[0, P]], 0, -1)
            where(req_rows[:, 1, :], [[1, P]], LS, -LS)
            where(req_rows[:, 1, :], [[-1, P]], -1, LS)
            fill(keep, 1.0)
            fill(keep[:, 0:SEQ:P], 0.0)
            fill(keep[:, SEQ:T:LS], 0.0)
            fill(head_sel[:, :], 1.0)
            where(head_sel[:, :], [[-64, 2]], 0, 1)
            where(head_sel[:, :], [[64, 2]], 63, -1)
            fill(flat(MT, 32, 896), 0.0)
            fill(col_sel[:, 7:8], 1.0)
            fill(head_rows, 0.0)
            where(head_rows.rearrange("p (h c) -> p h c", h=HB), [[-1, HB], [0, NB]], 0, 1, ALU.not_equal, 1.0)
            fill(half_sel[:, 6:8], 1.0)
            where(half_sel[:, 6:8], [[-64, 2]], 0, 1)
            where(half_sel[:, 6:8], [[64, 2]], 63, -1)
            fill(lvl[:, :, :], 1.0)
            for i in range(7):
                n = 1 << i
                v = lvl[:, i, :].rearrange("p (b two x) -> p b two x", two=2, x=n)
                fill(v[:, :, 0, :], 0.0)
                where(v[:, :, 1, :], [[-2 * n, 64 // n], [0, n]], 0, 1)
                where(v[:, :, 1, :], [[2 * n, 64 // n], [0, n]], n - 1, -1)
            fill(masks[:, :, :, :], 1.0)
            for kind in range(2):
                where(masks[:, kind, 0, :], [[1, P]], 0, -1, ALU.is_gt)
                where(masks[:, kind, 1, :], [[1, P]], 0, -1)
            diagonal(masks[:, 1, :, :].rearrange("p a (b c) -> p a b c", b=NSEQ), [[0, 2]], NSEQ, LS)
            fill(same_seq[:, :], 1.0)
            diagonal(same_seq[:, :].rearrange("p (b c) -> p b c", b=NSEQ), [], NSEQ, LS)
            fill(seq_cols[:, :, :], 1.0)
            where(seq_cols[:, :, :], [[-LS, NSEQ], [1, P]], 0, 0)
            where(seq_cols[:, :, :], [[LS, NSEQ], [-1, P]], LS - 1, 0)
            fill(seq_rows[:, :], 1.0)
            where(seq_rows[:, :], [[-LS, NSEQ]], 0, 1)
            where(seq_rows[:, :], [[LS, NSEQ]], LS - 1, -1)
            fill(Sg[:, :], 0.0)
            fill(Zb[:, :], 0.0)
            n_const[0] = st.n["pool_chain"]
            pool.wait_ge(S("proj_mm"), NP_MG)
            pool.wait_ge(S("ab_mm"), 1)
            st.do(pool.memset(flat(ring, 4096, 8192), 0.0), "zraw_clear")
            for q in range(3):
                for l in range(LEVELS[q]):
                    for g in range(3):
                        n = INV0[q] + 3 * l + g
                        if l == 0 and g == 0:
                            pool.wait_ge(S("gdn_mat"), q + 1)
                        if l == 0 and g > 0:
                            pool.wait_ge(S("rw_mat"), HB * q + 4 * g)
                        if n >= 3:
                            pool.wait_ge(S("inv_t1"), n - 2)
                        if l == 1:
                            pool.wait_ge(S("inv_x"), n - 2)
                        src = NT[:, :] if g == 0 else MT[:, 4 * (g - 1):4 * g, 0:P]
                        if g == 0:
                            src = src.rearrange("p (h i) -> p h i", h=4)
                        st.do(pool.tensor_tensor(NL[:, g].rearrange("p (h i) -> p h i", h=4), src,
                                                 lvl[:, l, :].unsqueeze(1).broadcast_to([P, 4, P]),
                                                 ALU.mult), "inv_nl", hold=False)

            pool.wait_ge(S("h_out"), 32 + 16)
            st.do(pool.memset(flat(MT, 2 * D), 0.0))

            def mark():
                pool.sem_inc(S("dma_go"))

            def routed(pre, n_task):
                def gather(i, u):
                    pool.wait_ge(S("r_ids"), i * ROUND + u + 1 + done(pre, "ids"))
                    if not (isinstance(i, int) and i * ROUND + u < 2):
                        pool.wait_ge(S("r_turn"), i * ROUND + u - 1 + done(pre, "turn"))
                    mark()
                    pool.indirect_dma_start(xt[:, u % 2, :], None, h_rows,
                                            bass.IndirectOffsetOnAxis(slot_ids[:, u % ROUND, 0:1], 0),
                                            bounds_check=T - 1, oob_is_err=False
                                            ).then_inc(S(f"r_xg{u % 2}"), 16)

                def scatter(i, u):
                    pool.wait_ge(S("r_oA"), i * ROUND + u + 1 + done(pre, "oA"))
                    pool.wait_ge(S("r_oD"), i * ROUND + u + 1 + done(pre, "oD"))
                    mark()
                    pool.indirect_dma_start(y_rows, bass.IndirectOffsetOnAxis(slot_ids[:, u % ROUND, 1:2], 0),
                                            obuf[u % 2], None, bounds_check=N_ACT * T - 1, oob_is_err=False
                                            ).then_inc(S(f"r_sc{u % 2}"), 16)

                def task(i, u):
                    n = i * ROUND + u if isinstance(i, int) else None
                    if n is None or n + 3 < n_task:
                        gather(i, u + 3)
                    if n is None or n >= 1:
                        scatter(i, u - 1)

                for u in range(3):
                    gather(0, u)
                rounds(pool, task, n_task)
                scatter((n_task - 1) // ROUND, (n_task - 1) % ROUND)
                for par_ in range(2):
                    pool.wait_ge(S(f"r_sc{par_}"), 16 * (n_task // 2) + done(pre, "sc", par_))

            routed("a", NE)
            pool.wait_ge(S("most"), 1)
            with pool.If(pool.value_load(most[0:1, 0:1], min_val=0, max_val=T) > P):
                for i in range(2):
                    pool.wait_ge(S(f"r_sc{i}"), 16 * NE // 2)
                routed("b", 2 * NE)
            st.do(pool.memset(stat[:, 2, 0:1], 0.0), "routed")

        @block.sync
        def _(sp_):
            def load(dst, src, name):
                sp_.dma_start(dst, src).then_inc(S(name), 16)

            load(c_sb[0:1, :], c_prompt, "c_in")
            load(c_sb[1:9, :], c_sample, "c_in")

            for u in range(RING):
                load(ring[:, u], w_ada_v[:, :, 512 * u:512 * (u + 1)], f"ring{u}")
            load(xs[:, 0:2, :], x_prompt[0].rearrange("(t p) d -> p t d", p=P), "x_in")
            load(xs[:, 2, :], x_sample.rearrange("s t d -> (s t) d"), "x_in")
            for b in range(RB):
                load(past_r[NSEQ * b:NSEQ * (b + 1), :], state_rwkv_shift[0, :, 0, tok(b)], "past_in")
            for b in range(QB):
                load(past_q[24 * (b % 4):24 * (b % 4 + 1), b // 4, :],
                     state_gdn_conv[0, :, :, tok(b)].rearrange("s w c -> (s w) c"), "past_in")
            with sp_.Fori(1, N_ADA // RING) as i:
                for u in range(RING):
                    sp_.wait_ge(S("ada_mm"), (i - 1) * RING + u + 1)
                    sp_.dma_start(ring[:, u], w_ada_v[:, :, bass.ds(i * (512 * RING) + 512 * u, 512)]
                                  ).then_inc(S(f"ring{u}"), 16)
            for j, (c0, w) in enumerate(RING_IN):
                n = N_ADA + j
                if j < RING:
                    sp_.wait_ge(S("ada_mm"), n - RING + 1)
                else:
                    sp_.wait_ge(S("proj_mm"), [4, 8, 12, 14, 17][j - RING])
                load(ring[:, n % RING, :, 0:w], w_in_v[:, :, c0:c0 + w], f"ring{n % RING}")

            sp_.wait_ge(S("proj_mm"), NP_MG)
            load(Ss, state_gdn[0].rearrange("s h k v -> k s h v"), "gdn_in")
            sp_.wait_ge(S("zraw_clear"), 1)
            for h in range(2):
                for s in range(NSEQ):
                    load(Zraw[64 * h:64 * h + 64, s, :, 64 * h:64 * h + 64],
                         state_rwkv[0, s, h:HB:2].rearrange("b v k -> v b k"), "rwkv_in")
            for w in range(4):
                sp_.wait_ge(S("last_ev"), w + 1)
                if w < 3:
                    for j in range(4):
                        b, r = 4 * w + j, 27 * j
                        sp_.dma_start(conv_p[0, 0, :, tok(b)], last_out[r:r + 3, tok(w)]).then_inc(S("out"), 16)
                        sp_.dma_start(conv_s[0, :, :, tok(b)].rearrange("s w c -> (s w) c"),
                                      last_out[r + 3:r + 27, tok(w)]).then_inc(S("out"), 16)
                else:
                    for b in range(RB):
                        sp_.dma_start(shift_p[0, 0, :, tok(b)], last_out[9 * b:9 * b + 1, tok(w)]).then_inc(S("out"), 16)
                        sp_.dma_start(shift_s[0, :, 0, tok(b)], last_out[9 * b + 1:9 * b + 9, tok(w)]).then_inc(S("out"), 16)
            n_out = 16 * (24 + 28)
            sp_.wait_ge(S("out"), n_out)
            sp_.wait_ge(S("seq_ev"), HA)
            sp_.dma_start(gdn_s[0].rearrange("s h k v -> k s h v"), Ss).then_inc(S("out"), 16)
            sp_.wait_ge(S("z_ev"), 16)
            for h in range(2):
                for s in range(NSEQ):
                    sp_.dma_start(rwkv_s[0, s, h:HB:2].rearrange("b v k -> v b k"),
                                  Zraw[64 * h:64 * h + 64, s, :, 64 * h:64 * h + 64]).then_inc(S("out"), 16)
            n_out += 16 * 17
            sp_.wait_ge(S("out"), n_out)
            merge_src = [(w_in_v[:, :, c0:c0 + w], None) for c0, w in MERGE_IN]
            merge_src += [(w[0].rearrange("(k p) n -> p k n", p=P), 4) for w in (p_a, p_b)]
            merge_src += [(w_o_v[:, :, 512 * i:512 * i + 512], None) for i in range(2)]
            free = [None, None, None, ("proj_mm", NP_MG + 4), ("proj_mm", NP_MG + 8), ("proj_mm", NP_MG + 12),
                    ("proj_mm", NP_MG + 16), ("pab_mm", 15)]
            for j, (src, k) in enumerate(merge_src):
                n = N_ADA + len(RING_IN) + j
                if j == RING:
                    sp_.wait_ge(S("branch_done"), 3)
                    sp_.dma_start(gdn_p[0, 0].rearrange("h k v -> k h v"),
                                  Sg[:, :].rearrange("p (h v) -> p h v", h=4)).then_inc(S("out"), 16)
                    load(xs[:, 0:2, :], x_prompt[0].rearrange("(t p) d -> p t d", p=P), "x_in")
                    load(xs[:, 2, :], x_sample.rearrange("s t d -> (s t) d"), "x_in")
                    sp_.wait_ge(S("z_ev"), 17)
                    for h in range(2):
                        sp_.dma_start(rwkv_p[0, 0, h:HB:2].rearrange("b v k -> v b k"),
                                      zout.rearrange("p (b k) -> p b k", b=4)[64 * h:64 * h + 64, :, 64 * h:64 * h + 64]
                                      ).then_inc(S("out"), 16)
                    n_out += 48
                if free[j]:
                    sp_.wait_ge(S(free[j][0]), free[j][1])
                dst = ring[:, n % RING]
                if k:
                    dst = flat(ring, 4096, 4096 * (n % RING)).rearrange("p (k n) -> p k n", k=k)
                load(dst, src, f"ring{n % RING}")
            sp_.wait_ge(S("merged"), 8)
            for i, v in enumerate((ln1_g, ln1_b, ln2_g, ln2_b)):
                load(ln_rows[:, i, :], v[0].partition_broadcast(P), "ln_in")
            load(r_bias, router_bias[0].partition_broadcast(P), "ln_in")
            load(rw_sb, router_w[0].rearrange("(k p) n -> p k n", p=P), "ln_in")

            def col_w(w):
                return w.rearrange("(k p) n -> p k n", p=P)

            def dyn(w, e):
                return w[0, bass.ds(e, 1)].rearrange("e (k p) n -> p (e k) n", p=P)

            sp_.wait_ge(S("wo_mm"), 6)
            load(ring[:, 0, :, 0:DE], col_w(ws_gate[0]), "r_gu0")
            load(ring[:, 0, :, DE:2 * DE], col_w(ws_up[0]), "r_gu0")
            load(wd_ring[:, 0], col_w(ws_down[0]), "r_wd0")

            def routed(pre, n_task):
                def task(i, u):
                    n = i * ROUND + u if isinstance(i, int) else None
                    slot, e = weight_slot(pre, u), expert_of(pre, i, u)
                    if n is None or n >= 3:
                        sp_.wait_ge(S("r_gu_mm"), i * ROUND + u - 2 + done(pre, "gu_mm"))
                    elif pre == "a" and n == 2:
                        sp_.wait_ge(S("sgu_mm"), 3)
                    elif pre == "b":
                        sp_.wait_ge(S("r_gu_mm"), NE)
                    sp_.dma_start(ring[:, slot, :, 0:DE], dyn(we_gate, e)).then_inc(S(f"r_gu{slot}"), 16)
                    sp_.dma_start(ring[:, slot, :, DE:2 * DE], dyn(we_up, e)).then_inc(S(f"r_gu{slot}"), 16)
                    if n is None or n >= 3:
                        sp_.wait_ge(S("r_dn_mm"), i * ROUND + u - 2 + done(pre, "dn_mm"))
                    elif pre == "a" and n == 2:
                        sp_.wait_ge(S("sdn_mm"), 3)
                    elif pre == "b":
                        sp_.wait_ge(S("r_dn_mm"), NE)
                    sp_.dma_start(wd_ring[:, slot], dyn(we_down, e)).then_inc(S(f"r_wd{slot}"), 16)

                rounds(sp_, task, n_task)

            routed("a", NE)
            sp_.wait_ge(S("most"), 1)
            with sp_.If(sp_.value_load(most[0:1, 0:1], min_val=0, max_val=T) > P):
                for i in range(2):
                    sp_.wait_ge(S(f"r_sc{i}"), 16 * NE // 2)
                routed("b", 2 * NE)
            sp_.wait_ge(S("routed"), 1)
            y_v = y_rows.rearrange("(t p j) d -> t p j d", p=P, j=N_ACT)
            for j in range(2 * TILES):
                if j >= 3:
                    sp_.wait_ge(S("y_used"), j - 2)
                load(y_in[:, j % 3], y_v[j // 2][:, 4 * (j % 2):4 * (j % 2) + 4, :], f"ring{j % 3}")
            for t in range(TILES):
                sp_.wait_ge(S("y_ready"), t + 1)
                dst = y_p[0, tok(t), :] if t < 2 else y_s.rearrange("s t d -> (s t) d")
                sp_.dma_start(dst, xs[:, t, :]).then_inc(S("out"), 16)
            sp_.wait_ge(S("out"), n_out + 48)

        @block.scalar
        def _(act):
            st = Steps(act, "act_chain")

            def load(dst, src, name):
                act.dma_start(dst, src).then_inc(S(name), 16)

            def f(out, in_, func, name=None, hold=True, **kw):
                st.do(act.activation(out, in_, func, **kw), name, hold)

            def lengths(n):
                act.wait_ge(S("len_mm"), n)
                f(len_rows, bank[n - 1][0:8, 0:T], ACT.Sqrt, "len_ev", hold=False, bias=L2_EPS)

            def root(ap, k):
                act.wait_ge(S("var_in"), k)
                f(ap, ap, ACT.Sqrt, "var_root", hold=False)

            act.wait_ge(S("c_in"), 32)
            f(c_sb, c_sb, ACT.Silu, "c_silu")
            load(par_a[C_ADA:C_ADA + 48, :], b_ada[0].rearrange("(b c) -> b c", c=P), "par_in")
            load(par_a[C_CONV:C_CONV + 48, :], conv_w[0].rearrange("w (b c) -> (w b) c", c=P), "par_in")
            load(par_a[C_MU:C_MU + RB, :], mu_shift[0].rearrange("(b c) -> b c", c=P), "par_in")
            for i, v in enumerate((w0[0], a0[0], k_k[0], k_a[0], r_k[0].rearrange("h n -> (h n)"))):
                load(par_b[4 * i:4 * i + 4, :], v.rearrange("(b c) -> b c", c=P), "par_in")
            load(a_neg[:, :], a_log[0].partition_broadcast(P), "row_in")
            load(dtb[:, :], dt_bias[0].partition_broadcast(P), "row_in")
            load(gnw[:, :], gdn_norm_w[0].partition_broadcast(P), "row_in")
            load(lnx[:, 0, :], lnx_g[0].partition_broadcast(P), "row_in")
            load(lnx[:, 1, :], lnx_b[0].partition_broadcast(P), "row_in")
            for n in range(N_ADA):
                act.wait_ge(S("ada_mm"), n + 1)
                if n >= RING:
                    act.wait_ge(S("ada_t"), n - RING + 1)
                f(mod_row[:, n % RING, :], bank[[3, 4, 6][n % RING]][0:9, :], ACT.Copy, "ada_row", hold=False)
            load(w2a2[0:64, :], w2[0], "row_in")
            load(w2a2[64:128, :], a2[0], "row_in")
            load(g2_sb, g2[0], "row_in")
            load(w_ab[:, :, :], w_in_v[:, :, OFF_ALPHA:OFF_Z], "row_in")
            def projected(n):
                act.wait_ge(S("proj_mm"), n + 1)
                b = bank[4 + n % 4]
                row, pad = (rwp[:, n, :], 1) if n < RB else (qkv[:, n - NP_QKV, :], 3)
                f(row[:, pad:pad + SEQ], b[:, 0:SEQ], ACT.Copy, hold=False)
                f(row[:, pad + SEQ:].rearrange("p (s t) -> p s t", s=NSEQ)[:, :, pad:], seqs(b[:, SEQ:T]),
                  ACT.Copy, "proj_ev", hold=False)

            def conv_silu(j):
                act.wait_ge(S("conv_sum"), j + 1)
                f(qkv[:, j, 0:T], conv_acc[:, j % 2, :], ACT.Silu, "conv_silu", hold=False)

            act.wait_ge(S("past_ev"), 2)
            for n in range(RB):
                projected(n)
            act.wait_ge(S("mixed"), RB)
            f(rwp[0:64, 12, 0:T], rwp[0:64, 12, 0:T], ACT.Tanh)
            f(rwp[:, 13, 0:T], rwp[:, 13, 0:T], ACT.Sigmoid, "lora_in")
            for b in range(PAIRS):
                for w, (dst, c) in enumerate(((F1, C_W0), (F3, C_A0))):
                    act.wait_ge(S("lora_mm"), 2 * b + w + 1)
                    f(dst[:, b, :], bank[2 * (b % 2) + w][:, 0:T], ACT.Sigmoid, "lora_ev", hold=False,
                      bias=col(c + b))
            lengths(1)
            for t in range(3):
                act.wait_ge(S("proj_mm"), NP_Z + t + 1)
                f(zs[:, t, :], bank[4 + (NP_Z + t) % 4][:, :], ACT.Silu, "proj_ev", hold=False)
                if t == 0:
                    act.wait_ge(S("decay"), 1)
                    f(e_mid[:, :, :], c_mid[:, :, :], ACT.Exp)
                    f(e_tot[:, :, :], e_tot[:, :, :], ACT.Exp)
                    f(e_seq[:, :, :], e_seq[:, :, :], ACT.Exp, None)
                    f(F1[:, :, :], F1[:, :, :], ACT.Exp, "e_factor")
            for t in range(3):
                act.wait_ge(S("gate_mm"), t + 1)
                f(gate[:, t, :], bank[1 + t][:, :], ACT.Copy, "gate_ev", hold=False)
            act.wait_ge(S("ab_ev"), 2)
            f(beta[:, :, :], ab[:, :, HA:2 * HA], ACT.Sigmoid, "beta")
            act.wait_ge(S("row_in"), 16 * 9)
            f(a_neg[:, :], a_neg[:, :], ACT.Exp)
            f(sp_tmp[:, 2], sp_tmp[:, 1], ACT.Exp)
            f(sp_tmp[:, 2], sp_tmp[:, 2], ACT.Ln, "sp_ln", bias=1.0)
            act.wait_ge(S("kb"), 1)
            f(sq[:, 0:4, :], cum, ACT.Exp, scale=-1.0, name="e_factor")
            f(cum, cum, ACT.Exp, "e_factor")
            for j in range(QB):
                projected(NP_QKV + j)
                if j >= 2:
                    conv_silu(j - 2)
            lengths(2)
            conv_silu(QB - 2)
            conv_silu(QB - 1)
            for w in range(4):
                act.wait_ge(S("last_t"), w + 1)
                f(last_out[0:[108, 108, 108, 126][w], tok(w)], bank[w][0:[108, 108, 108, 126][w], 0:P],
                  ACT.Copy, "last_ev", hold=False)
            for i in range(8):
                act.wait_ge(S("z_turned"), i + 1)
                f(flat(ring, 512, 4096 + 512 * i), bank[4 + i % 4][:, :], ACT.Copy, "z_ev", hold=False)

            for q, t in enumerate(ORDER):
                act.wait_ge(S("gc"), q + 1)
                f(eg[:, :], gc[:, :], ACT.Exp, "decay_exp", hold=False)
                act.wait_ge(S("dt"), q + 1)
                f(DT, DT, ACT.Exp, "decay_exp", hold=False)
                for l in range(1, LEVELS[q]):
                    for g in range(3):
                        n = INV0[q] + 3 * l + g
                        act.wait_ge(S("inv_t1"), n + 1)
                        if (q, l, g) == (0, 1, 2):
                            act.wait_ge(S("out"), 16 * 52)
                        f(T1[:, g], bank[g][:, :], ACT.Copy, "inv_t1e", hold=False)
                act.wait_ge(S("kv_t"), q + 1)
                f(Vt, bank[2][:, :], ACT.Copy, "vt_a", hold=False)
                root(stat[:, 0, 0:4], 2 * q + 1)
                for i, dst in enumerate((vt, F3t, F4t)):
                    act.wait_ge(S("rt_t"), 3 * q + i + 1)
                    f(dst, bank[[7, 0, 1][i]][:, :], ACT.Copy, "rtok", hold=False)
                act.wait_ge(S("w1_mm"), q + 1)
                f(W1n, bank[2][:, :], ACT.Copy, "w1n", hold=False, scale=-1.0)
                act.wait_ge(S("sp_mm"), q + 1)
                f(sp, bank[3][:, :], ACT.Copy, "sp", hold=False)
                root(stat[:, 1, 0:8], 2 * q + 2)
                if t == 2:
                    for i in range(8):
                        act.wait_ge(S("z_turned"), 8 + i + 1)
                        f(flat(ring, 512, 8192 + 512 * i), bank[i % 4][:, :], ACT.Copy, "z_ev", hold=False)
            act.wait_ge(S("z_turned"), 17)
            f(zout, bank[0][:, :], ACT.Copy, "z_ev", hold=False)
            for n in range(NP_MG, NP_END):
                act.wait_ge(S("proj_mm"), n + 1)
                b = n - NP_MG
                f((sgA if b < 8 else sgB)[:, b % 8, :], bank[4 + n % 4][:, 0:T], ACT.Sigmoid, "proj_ev", hold=False)
            for i in range(4):
                act.wait_ge(S("ga_t"), i + 1)
                f(ga_rows[:, 512 * i:512 * i + 512], bank[4 + i][0:9, :], ACT.Copy, "ga_r", hold=False)
            act.wait_ge(S("merged"), 8)
            for i in range(8):
                act.wait_ge(S("gat_mm"), i + 1)
                f(ga_tok[:, i // 4, 512 * (i % 4):512 * (i % 4) + 512], bank[i % 4][:, :], ACT.Copy, "gat_ev", hold=False)
            for t in range(3):
                root(stat[:, 1, 1:2], 7 + t)
            act.wait_ge(S("route_mm"), 1)
            f(rt[:, 0:3, :], bank[6][:, 0:3 * NE].rearrange("p (t e) -> p t e", t=3), ACT.Sigmoid, "scores", hold=False)

            for i in range(6):
                act.wait_ge(S("x_turned"), 12 + i + 1)
                f(h2_tok[:, i // 2, 512 * (i % 2):512 * (i % 2) + 512], bank[i][:, :], ACT.Copy, "h2_tok", hold=False)
            act.wait_ge(S("h2_tok"), 6)
            for t in range(3):
                load(h_rows[tok(t), :], h2_tok[:, t, :], "h_out")
            for j in range(3):
                act.wait_ge(S("sgu_mm"), j + 1)
                f(sil[:, j % 2, :], bank[6 + j % 2][:, 0:DE], ACT.Silu, "s_silu", hold=False)
                if j:
                    act.wait_ge(S("s_turn"), j)
                    f(actT[:, (j - 1) % 2, :], bank[6 + (j - 1) % 2][:, 0:2 * P], ACT.Copy, "s_actT", hold=False)
                    if j == 2:
                        act.wait_ge(S("sdn_mm"), 1)
                        for i in range(2):
                            f(y_sh[:, 0, 512 * i:512 * i + 512], bank[2 + i][:, :], ACT.Copy, "y_sh", hold=False)
            act.wait_ge(S("s_turn"), 3)
            f(actT[:, 0, :], bank[6][:, 0:2 * P], ACT.Copy, "s_actT", hold=False)
            for t in range(1, 3):
                act.wait_ge(S("sdn_mm"), t + 1)
                for i in range(2):
                    f(y_sh[:, t, 512 * i:512 * i + 512], bank[2 * (1 + t % 2) + i][:, :], ACT.Copy, "y_sh", hold=False)

            def routed(pre, n_task):
                def turned(i, u):
                    act.wait_ge(S("r_turn"), i * ROUND + u + 1 + done(pre, "turn"))
                    act.activation(hgT[:, u % 2, 0:4, :].rearrange("p k c -> p (k c)"), bank[0][:, :], ACT.Copy
                                   ).then_inc(S("r_hgA"), 1)

                def out_half(i, u):
                    act.wait_ge(S("r_dn_mm"), i * ROUND + u + 1 + done(pre, "dn_mm"))
                    if not (isinstance(i, int) and i * ROUND + u < 2):
                        act.wait_ge(S(f"r_sc{u % 2}"), i * 48 + 16 * ((u - 2) // 2 + 1) + done(pre, "sc", u % 2))
                    act.activation(obuf[u % 2][:, 0:512], bank[4][:, :], ACT.Copy).then_inc(S("r_oA"), 1)

                def task(i, u):
                    n = i * ROUND + u if isinstance(i, int) else None
                    if n is None or n + 1 < n_task:
                        turned(i, u + 1)
                    act.wait_ge(S("r_gu_mm"), i * ROUND + u + 1 + done(pre, "gu_mm"))
                    act.activation(sil[:, u % 2, :], bank[[2, 3, 7][u % 3]][:, 0:DE], ACT.Silu
                                   ).then_inc(S("r_silu"), 1)
                    if n is None or n >= 1:
                        out_half(i, u - 1)
                    act.wait_ge(S("r_ta"), i * ROUND + u + 1 + done(pre, "ta"))
                    act.activation(actT[:, u % 2, :], bank[[2, 3, 7][u % 3]][:, 0:2 * P], ACT.Copy
                                   ).then_inc(S("r_actT"), 1)

                turned(0, 0)
                rounds(act, task, n_task)
                out_half((n_task - 1) // ROUND, (n_task - 1) % ROUND)

            routed("a", NE)
            act.wait_ge(S("most"), 1)
            with act.If(act.value_load(most[0:1, 0:1], min_val=0, max_val=T) > P):
                for i in range(2):
                    act.wait_ge(S(f"r_sc{i}"), 16 * NE // 2)
                routed("b", 2 * NE)
            for t in range(3):
                root(stat[:, 1, 1:2], 10 + t)

        @block.vector
        def _(dve):
            st = Steps(dve, "dve_chain")
            V = nc.vector

            def tt(out, a, b, op, name=None, hold=True):
                st.do(V.tensor_tensor(out, a, b, op), name, hold)

            def ts(out, a, s1, s2, op0, op1=None, name=None, hold=True):
                if op1 is None:
                    st.do(V.tensor_scalar(out, a, s1, None, op0), name, hold)
                else:
                    st.do(V.tensor_scalar(out, a, s1, s2, op0, op1), name, hold)

            def stt(out, a, s, b, op0, op1, name=None, hold=True):
                st.do(V.scalar_tensor_tensor(out=out, in0=a, scalar=s, in1=b, op0=op0, op1=op1), name, hold)

            def cp(out, a, name=None, hold=True):
                st.do(V.tensor_copy(out, a), name, hold)

            def rsum(out, a, name=None):
                st.do(V.tensor_reduce(out, a, AX.X, ALU.add), name)

            def over(ap, n):
                return ap.unsqueeze(2).broadcast_to([P, ap.shape[1], n])

            def inv_root(ap, scale, eps, k):
                ts(ap, ap, scale, eps, ALU.mult, ALU.add, "var_in")
                dve.wait_ge(S("var_root"), k)
                st.do(V.reciprocal(ap, ap))

            dve.wait_ge(S("start_t"), 1)
            cp(cT[:, :, :], bank[1][:, 0:72].rearrange("p (k r) -> p k r", r=9), "start_ev")
            dve.wait_ge(S("pool_chain"), n_const[0])
            dve.wait_ge(S("start_t"), 2)
            cp(par[:, :], bank[0][:, 0:130], "start_ev")
            dve.wait_ge(S("start_t"), 3)
            cp(rwp[:, :, 1 + SEQ:].rearrange("p b (s t) -> p b s t", s=NSEQ)[:, :, :, 0],
               bank[2][:, 0:112].rearrange("p (b s) -> p b s", s=NSEQ), "past_ev")
            qs = qkv[:, :, 3 + SEQ:].rearrange("p b (s t) -> p b s t", s=NSEQ)
            for w in range(3):
                cp(qs[:, :, :, w], bank[2][:, 112:400].rearrange("p (b s w) -> p b s w", s=NSEQ, w=3)[:, :, :, w],
                   "past_ev" if w == 2 else None)
            dve.wait_ge(S("ada_t"), N_ADA)
            tt(modT[:, :, :], bank[5][:, 0:432].rearrange("p (b r) -> p b r", r=9), over(par[:, 0:48], 9), ALU.add)
            for b in (8, 16, 32, 40):
                ts(modT[:, b:b + 8, :], modT[:, b:b + 8, :], 1.0, None, ALU.add)

            def modulate(before, shift, scale, banks):
                for i in range(6):
                    t, k0 = i // 2, 4 * (i % 2)
                    dve.wait_ge(S("x_turned"), before + i + 1)
                    src = bank[banks[i]][:, :].rearrange("p (k t) -> p k t", k=4)
                    out = hT[:, k0:k0 + 4, tok(t)]
                    sc, sh = modT[:, scale + k0:scale + k0 + 4, :], modT[:, shift + k0:shift + k0 + 4, :]
                    if t < 2:
                        tt(out, src, over(sc[:, :, 0], P), ALU.mult)
                        tt(out, out, over(sh[:, :, 0], P), ALU.add, "hT")
                    else:
                        for k in range(4):
                            o = seqs(out[:, k, :])
                            tt(o, seqs(src[:, k, :]), over(sc[:, k, 1:9], LS), ALU.mult)
                            tt(o, o, over(sh[:, k, 1:9], LS), ALU.add, "hT" if k == 3 else None)

            modulate(0, 0, 8, [0, 2, 3, 4, 6, 7])

            for b in range(RB):
                dve.wait_ge(S("proj_ev"), b + 1)
                row = rwp[:, b, :]
                srow = row[:, 1 + SEQ:].rearrange("p (s t) -> p s t", s=NSEQ)
                cp(last_r[:, b, 0:1], row[:, SEQ:SEQ + 1])
                cp(last_r[:, b, 1:9], srow[:, :, LS])
                tt(shift_tmp[:, 0:SEQ], row[:, 0:SEQ], row[:, 1:1 + SEQ], ALU.subtract)
                tt(seqs(shift_tmp[:, SEQ:T]), srow[:, :, 0:LS], srow[:, :, 1:], ALU.subtract)
                ts(shift_tmp, shift_tmp, col(C_MU + b), None, ALU.mult)
                tt(shift_tmp[:, 0:SEQ], shift_tmp[:, 0:SEQ], row[:, 1:1 + SEQ], ALU.add)
                tt(seqs(shift_tmp[:, SEQ:T]), seqs(shift_tmp[:, SEQ:T]), srow[:, :, 1:], ALU.add)
                cp(row[:, 0:T], shift_tmp, "mixed")
            dve.wait_ge(S("ab_mm"), 1)
            cp(ab[:, :, :], bank[3][:, 0:24].rearrange("p (t c) -> p t c", t=3))
            dve.wait_ge(S("row_in"), 16 * 9)
            tt(sp_tmp[:, 0], ab[:, :, 0:HA], dtb[:, :].unsqueeze(1).broadcast_to([P, 3, HA]), ALU.add)
            ts(sp_tmp[:, 1], sp_tmp[:, 0], -1.0, None, ALU.mult)
            tt(sp_tmp[:, 1], sp_tmp[:, 0], sp_tmp[:, 1], ALU.min, "ab_ev")
            st.do(V.memset(stat[:, 0, 0:1], 0.0), "ab_ev")
            r_, k_ = rwp[:, 0:4, 0:T], rwp[:, 4:8, 0:T]
            for b in range(PAIRS):
                ts(kkn[:, b, :], k_[:, b, :], col(C_KK + b), None, ALU.mult)
            tt(sq[:, 0:4, :], kkn, kkn, ALU.mult, "sq")
            dve.wait_ge(S("lora_ev"), 8)
            ts(F1[:, :, :], F1[:, :, :], -EXP_NEG_HALF, None, ALU.mult)
            for b in range(PAIRS):
                st.do(V.tensor_tensor_scan(cum[:, b, :], keep, F1[:, b, :], 0.0, ALU.mult, ALU.add))
            cp(e_seq[:, :, :], cum[:, :, SEQ + LS - 1:T:LS])
            cp(c_mid[:, :, :], cum[:, :, 63:SEQ:P])
            tt(e_tot[:, :, :], cum[:, :, P - 1:SEQ:P], c_mid[:, :, :], ALU.subtract)
            for t in range(2):
                tt(cum[:, :, tok(t)], cum[:, :, tok(t)], over(c_mid[:, :, t], P), ALU.subtract)
            tt(F1[:, :, :], cum, F1[:, :, :], ALU.subtract, "decay")
            dve.wait_ge(S("len_ev"), 1)
            st.do(V.reciprocal(len_rows, len_rows), "len_inv")
            for b in range(PAIRS):
                dve.wait_ge(S("len_all"), b + 1)
                tt(kkn[:, b, :], kkn[:, b, :], bank[b][:, 0:T], ALU.mult, "len_used")
            for b in range(PAIRS):
                tmp = rs_tmp[:, 0, :]
                ts(tmp, F3[:, b, :], 1.0, col(C_KA + b), ALU.subtract, ALU.mult)
                stt(k_[:, b, :], tmp, 1.0, k_[:, b, :], ALU.add, ALU.mult)
            tt(F3[:, :, :], F3[:, :, :], kkn, ALU.mult)
            for b in range(PAIRS):
                stt(sq[:, 4 + b, :], r_[:, b, :], col(C_RK + b), k_[:, b, :], ALU.mult, ALU.mult,
                    "bonus_in" if b == 3 else None)
            dve.wait_ge(S("e_factor"), 1)
            tt(F1[:, :, :], F1[:, :, :], kkn, ALU.mult, "kb")
            dve.wait_ge(S("e_factor"), 2)
            tt(F3[:, :, :], F3[:, :, :], sq[:, 0:4, :], ALU.mult)
            tt(k_, k_, sq[:, 0:4, :], ALU.mult)
            dve.wait_ge(S("e_factor"), 3)
            tt(r_, r_, cum, ALU.mult, "F_ready")
            for b in range(QB):
                if b == 9:
                    dve.wait_ge(S("bonus_mm"), 1)
                    cp(bonus[:, :, :], bank[0][:, 0:24].rearrange("p (t h) -> p t h", t=3), "bonus_ev")
                    dve.wait_ge(S("conv_silu"), 8)
                    tt(sq, qkv[:, 0:8, 0:T], qkv[:, 0:8, 0:T], ALU.mult, "sq")
                dve.wait_ge(S("proj_ev"), NP_QKV + b + 1)
                row = qkv[:, b, :]
                srow = row[:, 3 + SEQ:].rearrange("p (s t) -> p s t", s=NSEQ)
                cp(last_q[:, b, 0, :], row[:, SEQ:SEQ + 3])
                cp(last_q[:, b, 1:9, :], srow[:, :, LS:LS + 3], "last_q")
                acc = conv_acc[:, b % 2, :]
                if b >= 2:
                    dve.wait_ge(S("conv_silu"), b - 1)
                for w in range(4):
                    c = col(C_CONV + QB * w + b)
                    if w == 0:
                        ts(acc[:, 0:SEQ], row[:, w:w + SEQ], c, None, ALU.mult)
                        ts(seqs(acc[:, SEQ:T]), srow[:, :, w:w + LS], c, None, ALU.mult)
                    else:
                        stt(acc[:, 0:SEQ], row[:, w:w + SEQ], c, acc[:, 0:SEQ], ALU.mult, ALU.add)
                        stt(seqs(acc[:, SEQ:T]), srow[:, :, w:w + LS], c, seqs(acc[:, SEQ:T]), ALU.mult, ALU.add,
                            "conv_sum" if w == 3 else None)
            dve.wait_ge(S("len_ev"), 2)
            st.do(V.reciprocal(len_rows, len_rows), "len_inv")
            for b in range(8):
                dve.wait_ge(S("len_all"), PAIRS + b + 1)
                stt(qkv[:, b, 0:T], qkv[:, b, 0:T], P ** -0.5 if b < 4 else 1.0, bank[b % 4][:, 0:T],
                    ALU.mult, ALU.mult, "len_used")
            dve.wait_ge(S("sp_ln"), 1)
            ts(sp_tmp[:, 0], sp_tmp[:, 0], 0.0, None, ALU.max)
            tt(sp_tmp[:, 0], sp_tmp[:, 0], sp_tmp[:, 2], ALU.add)
            tt(g_log[:, :, :], sp_tmp[:, 0], a_neg[:, :].unsqueeze(1).broadcast_to([P, 3, HA]), ALU.mult)
            ts(g_log[:, :, :], g_log[:, :, :], -1.0, None, ALU.mult)

            for q, t in enumerate(ORDER):
                kind = int(t == 2)
                cp(gb.rearrange("p (h i) -> p h i", h=4), over(g_log[:, t, :], P), "gb")
                dve.wait_ge(S("g_mm"), q + 1)
                cp(gc[:, 0:4], bank[7][:, 0:4])
                tt(gc[:, 4:8], bank[7][:, 4:8], gc[:, 0:4], ALU.subtract)
                cp(gc[:, 8:40], bank[7][:, 8:40], "gc")
                for h in range(4):
                    ts(DT[:, tok(h)], bank[6][:, tok(h)], gc[:, h:h + 1], 0.0, ALU.subtract, ALU.min,
                       "dt" if h == 3 else None)
                dve.wait_ge(S("decay_exp"), 2 * q + 2)
                dve.wait_ge(S("decay_exp"), 2 * q + 1)
                ts(neg_eg[:, :], eg[:, 0:4], -1.0, None, ALU.mult)
                dve.wait_ge(S("kq_mm"), q + 1)
                dve.wait_ge(S("beta"), 1)
                tt(NT[:, :].rearrange("p (h i) -> p h i", h=4), bank[6][:, :].rearrange("p (h i) -> p h i", h=4),
                   over(beta[:, t, :], P), ALU.mult)
                tt(NT[:, :], NT[:, :], DT, ALU.mult)
                tt(aT[:, :], bank[7][:, :], DT, ALU.mult)
                a4 = aT[:, :].rearrange("p (h i) -> p h i", h=4)
                tt(a4, a4, masks[:, kind, 1, :].unsqueeze(1).broadcast_to([P, 4, P]), ALU.mult, "gdn_mat")
                for h in range(HB):
                    dve.wait_ge(S("rw_mm"), HB * q + h + 1)
                    tt(MT[:, h, :].rearrange("p (a i) -> p a i", a=2),
                       bank[6 + h % 2][:, :].rearrange("p (a i) -> p a i", a=2),
                       masks[:, kind].rearrange("p a i -> p (a i)").unsqueeze(1).broadcast_to([P, 2, 2 * P]),
                       ALU.mult, "rw_mat", hold=False)
                for l in range(LEVELS[q]):
                    for g in range(3):
                        n = INV0[q] + 3 * l + g
                        four = "p (h i) -> p h i"
                        x_g, xt_g = X[:, g].rearrange(four, h=4), XT[:, g].rearrange(four, h=4)
                        if l == 0:
                            idb = ident[:, :].unsqueeze(1).broadcast_to([P, 4, P])
                            dve.wait_ge(S("inv_t1"), n + 1)
                            tt(x_g, idb, bank[g][:, :].rearrange(four, h=4), ALU.subtract, hold=False)
                            dve.wait_ge(S("inv_nl"), n + 1)
                            tt(xt_g, idb, NL[:, g].rearrange(four, h=4), ALU.subtract, "inv_x", hold=False)
                            continue
                        dve.wait_ge(S("inv_p"), n + 1 - 3 * (q + 1))
                        if l < LEVELS[q] - 1:
                            tt(x_g, x_g, bank[3 + g][:, :].rearrange(four, h=4), ALU.subtract, hold=False)
                        tt(xt_g, xt_g, bank[g][:, :].rearrange(four, h=4), ALU.subtract, "inv_x", hold=False)
                if t == 2:
                    for h in range(HA):
                        if h >= 2:
                            dve.wait_ge(S("seq_mm"), h - 1)
                        for w in range(2):
                            src = qkv[:, 4 * (1 - w) + h, tok(2)]
                            tt(sm[:, h % 2, w], src.unsqueeze(1).broadcast_to([P, NSEQ, P]), seq_cols[:, :, :],
                               ALU.mult, "seq_in" if w else None, hold=False)
                dve.wait_ge(S("kv_t"), q + 1)
                four = "p (h i) -> p h i"
                tt(Kd.rearrange(four, h=4), bank[3][:, :].rearrange(four, h=4), over(eg[:, 4:8], P), ALU.mult)
                tt(Ot.rearrange(four, h=4), bank[1][:, :].rearrange(four, h=4), over(eg[:, 0:4], P), ALU.mult)
                dve.wait_ge(S("vt_a"), q + 1)
                for h in range(4):
                    stt(R[:, tok(h)], bank[0][:, tok(h)], neg_eg[:, h:h + 1], Vt[:, tok(h)], ALU.mult, ALU.add,
                        "R" if h == 3 else None)
                dve.wait_ge(S("yr_mm"), q + 1)
                tt(vn.rearrange(four, h=4), bank[4][:, :].rearrange(four, h=4), over(beta[:, t, :], P), ALU.mult, "vn")
                dve.wait_ge(S("av_mm"), q + 1)
                tt(Ot, Ot, bank[5][:, :], ALU.add)
                if t < 2:
                    for h in range(4):
                        stt(Sg[:, tok(h)], Sg[:, tok(h)], eg[:, 8 + 8 * h:9 + 8 * h], bank[6][:, tok(h)],
                            ALU.mult, ALU.add)
                else:
                    def by_seq(h):
                        if h >= 2:
                            dve.wait_ge(S("seq_upd"), h - 1)
                        tt(sm[:, h % 2, 0], vn[:, tok(h)].unsqueeze(1).broadcast_to([P, NSEQ, P]),
                           over(seq_rows[:, :], P), ALU.mult, "seq_rhs", hold=False)

                    by_seq(0)
                    for h in range(4):
                        if h < 3:
                            by_seq(h + 1)
                        tt(Ss[:, :, h, :], Ss[:, :, h, :], over(eg[:, 8 + 8 * h:16 + 8 * h], P), ALU.mult)
                        dve.wait_ge(S("seq_upd"), h + 1)
                        for j in range(2):
                            sl = Ss[:, 4 * j:4 * j + 4, h, :]
                            tt(sl, sl, bank[upd_bank(h, j)][:, :].rearrange("p (s v) -> p s v", s=4), ALU.add,
                               "seq_ev" if j else None, hold=False)
                tt(R, Ot, Ot, ALU.mult)
                rsum(stat[:, 0, 0:4], R.rearrange(four, h=4))
                inv_root(stat[:, 0, 0:4], 1.0 / P, RMS_EPS, 2 * q + 1)
                tt(Ot.rearrange(four, h=4), Ot.rearrange(four, h=4), over(stat[:, 0, 0:4], P), ALU.mult)
                tt(Ot.rearrange(four, h=4), Ot.rearrange(four, h=4),
                   gnw[:, :].unsqueeze(1).broadcast_to([P, 4, P]), ALU.mult)
                tt(zs[:, t, :], zs[:, t, :], Ot, ALU.mult, "gdn_done")
                if t < 2:
                    tt(Zp.rearrange(four, h=4), Zb[:, :].rearrange(four, h=4), over(e_mid[:, :, t], P), ALU.mult, "zp")
                else:
                    for b in range(PAIRS):
                        if b >= 2:
                            dve.wait_ge(S("seq_mm"), HA + b - 1)
                        for w, src in enumerate((F1[:, b, tok(2)], rwp[:, b, tok(2)])):
                            tt(sm[:, b % 2, w], src.unsqueeze(1).broadcast_to([P, NSEQ, P]), seq_cols[:, :, :],
                               ALU.mult, "seq_in" if w else None, hold=False)
                dve.wait_ge(S("ry_mm"), q + 1)
                Y, Y2 = T1[:, 0], T1[:, 1]
                cp(Y, bank[4][:, :])
                if t < 2:
                    tt(Zb[:, :].rearrange(four, h=4), bank[5][:, :].rearrange(four, h=4),
                       blk64[:, :].unsqueeze(1).broadcast_to([P, 4, P]), ALU.mult)
                    tt(Zb[:, :], Zb[:, :], Zp, ALU.add)
                    tt(Zb[:, :].rearrange(four, h=4), Zb[:, :].rearrange(four, h=4), over(e_tot[:, :, t], P),
                       ALU.mult)
                else:
                    tt(Y, Y, bank[0][:, :], ALU.add)
                    def pair_by_seq(b):
                        if b >= 2:
                            dve.wait_ge(S("seq_upd"), HA + b - 1)
                        for w, src in enumerate((sp, vt)):
                            tt(sm[:, b % 2, w], src[:, tok(b)].unsqueeze(1).broadcast_to([P, NSEQ, P]),
                               over(seq_rows[:, :], P), ALU.mult, "seq_rhs" if w else None, hold=False)

                    upd = flat(inv, 1024).rearrange("p (s v) -> p s v", s=NSEQ)
                    pair_by_seq(0)
                    for b in range(PAIRS):
                        if b < PAIRS - 1:
                            pair_by_seq(b + 1)
                        dve.wait_ge(S("seq_upd"), HA + b + 1)
                        for j in range(2):
                            tt(upd[:, 4 * j:4 * j + 4, :],
                               bank[upd_bank(b, j)][:, :].rearrange("p (s v) -> p s v", s=4),
                               blk64[:, :].unsqueeze(1).broadcast_to([P, 4, P]), ALU.mult)
                        tt(upd, upd, Zs[:, :, b, :], ALU.add)
                        tt(Zs[:, :, b, :], upd, over(e_seq[:, b, :], P), ALU.mult, "seq_ev")
                eight = "p (h v) -> p h v"
                Yh, Y2h = Y.rearrange(eight, h=8), Y2.rearrange(eight, h=8)
                mu8, rs8 = stat[:, 0, 0:8], stat[:, 1, 0:8]
                rsum(mu8, Yh)
                ts(mu8, mu8, 1.0 / NB, None, ALU.mult)
                tt(Yh, Yh, over(mu8, NB), ALU.subtract)
                tt(Y2, Y, Y, ALU.mult)
                rsum(rs8, Y2h)
                inv_root(rs8, 1.0 / NB, GN_EPS, 2 * q + 2)
                tt(Yh, Yh, over(rs8, NB), ALU.mult)
                tt(Y, Y, lnx[:, 0, :], ALU.mult)
                tt(Y, Y, lnx[:, 1, :], ALU.add)
                tt(Y2h, vt.rearrange(eight, h=8), over(bonus[:, t, :], NB), ALU.mult)
                tt(Y, Y, Y2, ALU.add)
                dve.wait_ge(S("gate_ev"), 3)
                tt(gate[:, t, :], gate[:, t, :], Y, ALU.mult, "branch_done")

            for i in range(6):
                dve.wait_ge(S("y_t"), i + 1)
                cp(yT[:, i // 3, :, tok(i % 3)], bank[1 + i % 3][:, :].rearrange("p (b t) -> p b t", b=4), "yT")
            dve.wait_ge(S("proj_ev"), NP_END)
            dve.wait_ge(S("out"), 16 * (52 + 17 + 3))
            for c in range(8):
                dve.wait_ge(S("pab_mm"), 2 * c + 1)
                tt(mtmp[:, 0], bank[c % 2][:, 0:T], sgA[:, c, :], ALU.mult)
                dve.wait_ge(S("pab_mm"), 2 * c + 2)
                tt(mtmp[:, 1], bank[2 + c % 2][:, 0:T], sgB[:, c, :], ALU.mult)
                tt(merged[:, c, :], mtmp[:, 0], mtmp[:, 1], ALU.add, "merged")

            def layernorm(t, src_banks, which, name):
                kind = int(t == 2)
                for j in range(2):
                    half = slice(512 * j, 512 * j + 512)
                    tt(lt[:, half], src_banks[j], ga_tok[:, kind, 1024 * which + 512 * j:1024 * which + 512 * j + 512],
                       ALU.mult)
                    stt(xs[:, t, half], xs[:, t, half], DN_ALPHA, lt[:, half], ALU.mult, ALU.add)
                    st.do(V.bn_stats(stat[:, 0, 6 * j:6 * j + 6], xs[:, t, half]))
                st.do(V.bn_aggr(stat[:, 1, 0:2], stat[:, 0, 0:12]))
                inv_root(stat[:, 1, 1:2], 1.0, LN_EPS, 7 + 3 * which + t)
                ts(xs[:, t, :], xs[:, t, :], stat[:, 1, 0:1], stat[:, 1, 1:2], ALU.subtract, ALU.mult)
                tt(xs[:, t, :], xs[:, t, :], ln_rows[:, 2 * which, :], ALU.mult)
                tt(xs[:, t, :], xs[:, t, :], ln_rows[:, 2 * which + 1, :], ALU.add, name)

            dve.wait_ge(S("gat_ev"), 8)
            dve.wait_ge(S("ln_in"), 16 * 6)
            dve.wait_ge(S("x_in"), 64)
            for t in range(TILES):
                dve.wait_ge(S("wo_mm"), 2 * t + 2)
                if t == 0:
                    dve.wait_ge(S("wo_mm"), 6)
                layernorm(t, [bank[[4, 5, 6, 7, 0, 1][2 * t + j]][:, :] for j in range(2)], 0, "x1")
            modulate(6, 24, 32, [2, 3, 4, 5, 6, 7])

            dve.wait_ge(S("scores"), 1)
            cp(count_up, bank[7][:, P:2 * P])
            for t in range(TILES):
                ts(tok_id[:, t, 0:1], bank[7][:, 0:1], float(P * t - NOWHERE), None, ALU.add)
                ts(tok_id[:, t, 1:2], bank[7][:, 0:1], float(N_ACT), float(N_ACT * P * t - 1 - NOWHERE),
                   ALU.mult, ALU.add, "tok_id")
            for t in range(TILES):
                sc, choice, tmp, m = rt[:, t, :], rt[:, 3, :], rt[:, 4, :], chosen[:, t, :]
                tt(choice, sc, r_bias, ALU.add)
                for g in range(NG):
                    st.do(V.max(r8[:, 8 * g:8 * g + 8], choice[:, GE * g:GE * g + GE]), hold=(g == NG - 1))
                gs, gsel = g8[:, 0:8], g8[:, 8:16]
                v8 = r8.rearrange("p (g e) -> p g e", g=NG)
                tt(gs, v8[:, :, 0], v8[:, :, 1], ALU.add)
                st.do(V.max(g8[:, 16:24], gs))
                st.do(V.memset(g8[:, 20:24], 3.0 * BIG))
                st.do(V.match_replace(gsel, g8[:, 16:24], gs, -2.0 * BIG))
                ts(gsel, gsel, -2.0 * BIG, -BIG, ALU.not_equal, ALU.mult)
                tt(choice.rearrange("p (g e) -> p g e", g=NG), choice.rearrange("p (g e) -> p g e", g=NG),
                   over(gsel, GE), ALU.add)
                st.do(V.max(g8[:, 16:24], choice))
                st.do(V.match_replace(tmp, g8[:, 16:24], choice, -2.0 * BIG))
                ts(m, tmp, -2.0 * BIG, None, ALU.is_equal, name="chosen")
                tt(tmp, m, sc, ALU.mult)
                rsum(stat[:, 0, 0:1], tmp)
                ts(stat[:, 0, 0:1], stat[:, 0, 0:1], 1e-20, None, ALU.add)
                st.do(V.reciprocal(stat[:, 0, 1:2], stat[:, 0, 0:1]))
                ts(slot_rows[:, t, :, 2], tmp, stat[:, 0, 1:2], ROUTED_SCALE, ALU.mult, ALU.mult)
                st.do(V.tensor_tensor_scan(tmp, ones[:, 0:NE], m, 0.0, ALU.mult, ALU.add))
                ts(slot_rows[:, t, :, 1], tmp, tok_id[:, t, 1:2], None, ALU.add)
                ts(slot_rows[:, t, :, 0], m, 0.0, tok_id[:, t, 0:1], ALU.mult, ALU.add, "slot_rows")
                dve.wait_ge(S("s_silu"), t + 1)
                tt(act_t[:, t % 2, :], sil[:, t % 2, :], bank[6 + t % 2][:, DE:2 * DE], ALU.mult, "s_act")
            dve.wait_ge(S("pos_mm"), 1)
            stt(pos, bank[0][:, 0:3 * NE].rearrange("p (t e) -> p t e", t=3), 1.0, chosen, ALU.add, ALU.mult)
            ts(pos, pos, 1.0, None, ALU.subtract)
            st.do(V.tensor_reduce(stat[:, 0, 0:1], bank[0][:, 3 * NE:4 * NE], AX.X, ALU.max))
            cp(most[:, :], stat[:, 0, 0:1], "most")

            def routed(pre, n_task):
                def spread(i, u):
                    e = expert_of(pre, i, u)
                    for t in range(TILES):
                        last = V.tensor_scalar(onehot[:, u % 2, t, :], count_up, float(first_slot(pre, u)),
                                               pos[:, t, bass.ds(e, 1)], ALU.add, ALU.is_equal)
                    last.then_inc(S("r_hot"), 1)

                def ids(i, u):
                    dve.wait_ge(S("r_ids_mm"), i * ROUND + u + 1 + done(pre, "ids_mm"))
                    V.tensor_copy(slot_gate[:, u % ROUND:u % ROUND + 1], bank[6][:, 2:3])
                    V.tensor_scalar(slot_ids[:, u % ROUND, :], bank[6][:, 0:2], float(NOWHERE), None, ALU.add
                                    ).then_inc(S("r_ids"), 1)

                def turned(i, u):
                    dve.wait_ge(S("r_turn"), i * ROUND + u + 1 + done(pre, "turn"))
                    V.tensor_copy(hgT[:, u % 2, 4:8, :].rearrange("p k c -> p (k c)"), bank[1][:, :]
                                  ).then_inc(S("r_hgD"), 1)

                def out_half(i, u):
                    dve.wait_ge(S("r_dn_mm"), i * ROUND + u + 1 + done(pre, "dn_mm"))
                    if not (isinstance(i, int) and i * ROUND + u < 2):
                        dve.wait_ge(S(f"r_sc{u % 2}"), i * 48 + 16 * ((u - 2) // 2 + 1) + done(pre, "sc", u % 2))
                    V.tensor_copy(obuf[u % 2][:, 512:1024], bank[5][:, :]).then_inc(S("r_oD"), 1)

                def task(i, u):
                    n = i * ROUND + u if isinstance(i, int) else None
                    if n is None or n + 1 < n_task:
                        turned(i, u + 1)
                    if n is None or n + 3 < n_task:
                        spread(i, u + 3)
                    dve.wait_ge(S("r_silu"), i * ROUND + u + 1 + done(pre, "silu"))
                    dve.wait_ge(S("r_ids"), i * ROUND + u + 1 + done(pre, "ids"))
                    V.scalar_tensor_tensor(out=act_t[:, u % 2, :], in0=sil[:, u % 2, :],
                                           scalar=slot_gate[:, u:u + 1],
                                           in1=bank[[2, 3, 7][u % 3]][:, DE:2 * DE], op0=ALU.mult, op1=ALU.mult
                                           ).then_inc(S("r_act"), 1)
                    if n is None or n >= 1:
                        out_half(i, u - 1)
                    if n is None or n + 3 < n_task:
                        ids(i, u + 3)

                for u in range(3):
                    spread(0, u)
                    ids(0, u)
                turned(0, 0)
                rounds(dve, task, n_task)
                out_half((n_task - 1) // ROUND, (n_task - 1) % ROUND)

            routed("a", NE)
            with dve.If(dve.value_load(most[0:1, 0:1], min_val=0, max_val=T) > P):
                for i in range(2):
                    dve.wait_ge(S(f"r_sc{i}"), 16 * NE // 2)
                routed("b", 2 * NE)
            dve.wait_ge(S("y_sh"), 6)
            for j in range(2 * TILES):
                dve.wait_ge(S(f"ring{j % 3}"), 16 * (len(range(j % 3, N_RING, RING)) + j // 3 + 1))
                for i in range(4):
                    tt(y_sh[:, j // 2, :], y_sh[:, j // 2, :], y_in[:, j % 3, i, :], ALU.add,
                       "y_used" if i == 3 else None)
                if j % 2:
                    t = j // 2
                    layernorm(t, [y_sh[:, t, 0:512], y_sh[:, t, 512:1024]], 1, "y_ready")

        @block.tensor
        def _(pe):
            st = Steps(pe, "pe_chain")
            mm, tr = nc.tensor.matmul, nc.tensor.transpose

            def sig(ins, name):
                st.do(ins, name, hold=False)

            pe.wait_ge(S("pool_chain"), n_ident[0])
            pe.wait_ge(S("c_silu"), 1)
            for k in range(KC):
                last = tr(bank[1][:, 9 * k:9 * k + 9], c_sb[:, tok(k)], ident[0:9, 0:9])
            sig(last, "start_t")

            def turn_x(banks, name):
                for i in range(6):
                    t, k0 = i // 2, 4 * (i % 2)
                    for k in range(4):
                        last = tr(bank[banks[i]][:, tok(k)], xs[:, t, (k0 + k) * P:(k0 + k + 1) * P], ident[:, :])
                    sig(last, name)

            pe.wait_ge(S("start_ev"), 1)
            with pe.Fori(0, N_ADA // RING) as i:
                for u in range(RING):
                    pe.wait_ge(S(f"ring{u}"), i * 16 + 16)
                    for k in range(KC):
                        last = mm(bank[[3, 4, 6][u]][0:9, :], cT[:, k, :], ring[:, u, k, :],
                                  start=(k == 0), stop=(k == KC - 1))
                    last.then_inc(S("ada_mm"), 1)
                for u in range(RING):
                    pe.wait_ge(S("ada_row"), i * RING + u + 1)
                    for c in range(4):
                        last = mm(bank[5][:, bass.ds(i * 108 + 36 * u + 9 * c, 9)], mod_row[:, u, tok(c)],
                                  ident[0:9, 0:9], start=True, stop=True)
                    last.then_inc(S("ada_t"), 1)
            pe.wait_ge(S("pool_chain"), n_const[0])
            pe.wait_ge(S("par_in"), 16 * 8)
            tr(bank[0][:, 0:110], par_a, ident[0:110, 0:110])
            sig(tr(bank[0][:, 110:130], par_b, ident[0:20, 0:20]), "start_t")
            pe.wait_ge(S("past_in"), 16 * (RB + QB))
            tr(bank[2][:, 0:112], past_r, ident[0:112, 0:112])
            for a in range(3):
                last = tr(bank[2][:, 112 + 96 * a:112 + 96 * (a + 1)], past_q[:, a, :], ident[0:96, 0:96])
            sig(last, "start_t")
            pe.wait_ge(S("x_in"), 32)
            pe.wait_ge(S("start_ev"), 2)
            pe.wait_ge(S("past_ev"), 2)
            turn_x([0, 2, 3, 4, 6, 7], "x_turned")
            ring_n = [N_ADA // RING] * RING

            def ring_wait(n):
                u = n % RING
                ring_n[u] += 1
                pe.wait_ge(S(f"ring{u}"), 16 * ring_n[u])
                return u

            pe.wait_ge(S("hT"), 6)

            def project(n, u, c):
                if n >= 4:
                    pe.wait_ge(S("proj_ev"), n - 3)
                for k in range(KC):
                    last = mm(bank[4 + n % 4][:, 0:T], ring[:, u, k, tok(c)], hT[:, k, :],
                              start=(k == 0), stop=(k == KC - 1))
                sig(last, "proj_mm")

            def project_ring(j, blocks):
                u = (N_ADA + j) % RING
                if blocks[0] == 0:
                    ring_wait(N_ADA + j)
                first = sum(w // P for _, w in RING_IN[:4]) + 3 + 4 * (j - 5) if j > 4 else 4 * j
                for c in blocks:
                    project(first + c, u, c)

            for j in range(4):
                project_ring(j, range(RING_IN[j][1] // P))
            pe.wait_ge(S("row_in"), 16 * 9)
            for t in range(3):
                for k in range(KC):
                    last = mm(bank[3][:, 8 * t:8 * t + 8], hT[:, k, tok(t)], w_ab[:, k, :],
                              start=(k == 0), stop=(k == KC - 1))
            sig(last, "ab_mm")
            pe.wait_ge(S("lora_in"), 1)
            for b in range(PAIRS):
                for w in range(2):
                    if (b, w) == (1, 1):
                        pe.wait_ge(S("ab_ev"), 2)
                    if b >= 2:
                        pe.wait_ge(S("lora_ev"), 2 * (b - 2) + w + 1)
                    half = slice(64 * w, 64 * w + 64)
                    sig(mm(bank[2 * (b % 2) + w][:, 0:T], w2a2[half, tok(b)], rwp[half, 12, 0:T],
                           start=True, stop=True), "lora_mm")
            pe.wait_ge(S("sq"), 1)
            pe.wait_ge(S("lora_ev"), 5)
            for b in range(PAIRS):
                last = mm(bank[0][0:8, 0:T], half_sel[:, 6 - 2 * b:14 - 2 * b], sq[:, b, :],
                          start=(b == 0), stop=(b == PAIRS - 1))
            sig(last, "len_mm")
            u = ring_wait(N_ADA + 4)
            for t in range(3):
                n = NP_Z + t
                pe.wait_ge(S("proj_ev"), n - 3)
                for k in range(KC):
                    last = mm(bank[4 + n % 4][:, :], hT[:, k, tok(t)], ring[:, u, k, :],
                              start=(k == 0), stop=(k == KC - 1))
                sig(last, "proj_mm")
                if t == 1:
                    pe.wait_ge(S("len_inv"), 1)
                    pe.wait_ge(S("lora_ev"), 8)
                    for b in range(PAIRS):
                        sig(mm(bank[b][:, 0:T], head_rows[:, tok(b)], len_rows, start=True, stop=True), "len_all")
            pe.wait_ge(S("len_used"), PAIRS)
            for t in range(3):
                sig(mm(bank[1 + t][:, :], rwp[:, 13, tok(t)], g2_sb, start=True, stop=True), "gate_mm")
            project_ring(5, range(4))
            pe.wait_ge(S("bonus_in"), 1)
            for t in range(3):
                for b in range(PAIRS):
                    last = mm(bank[0][:, 8 * t + 2 * b:8 * t + 2 * b + 2], sq[:, 4 + b, tok(t)], head_sel[:, :],
                              start=True, stop=True)
            sig(last, "bonus_mm")
            project_ring(6, range(4))
            project_ring(7, range(3))
            pe.wait_ge(S("sq"), 2)
            pe.wait_ge(S("gate_ev"), 3)
            for b in range(8):
                last = mm(bank[1][0:8, 0:T], col_sel[:, 7 - b:15 - b], sq[:, b, :], start=(b == 0), stop=(b == 7))
            sig(last, "len_mm")
            project_ring(7, [3])
            pe.wait_ge(S("len_inv"), 2)
            pe.wait_ge(S("bonus_ev"), 1)
            for b in range(8):
                if b >= 4:
                    pe.wait_ge(S("len_used"), PAIRS + b - 3)
                sig(mm(bank[b % 4][:, 0:T], ident[0:8, b:b + 1].broadcast_to([8, P]), len_rows,
                       start=True, stop=True), "len_all")
            pe.wait_ge(S("len_used"), PAIRS + 8)
            pe.wait_ge(S("last_q"), QB)
            for w in range(4):
                if w < 3:
                    src = last_q[:, 4 * w:4 * w + 4, :, :].rearrange("p b s w -> p (b s w)")
                else:
                    src = last_r[:, :, :].rearrange("p b s -> p (b s)")
                sig(tr(bank[w][0:src.shape[1], 0:P], src, ident[:, :]), "last_t")
            pe.wait_ge(S("rwkv_in"), 16 * 16)
            pe.wait_ge(S("proj_ev"), NP_MG)
            for i in range(8):
                if i >= 4:
                    pe.wait_ge(S("z_ev"), i - 3)
                for b in range(PAIRS):
                    last = tr(bank[4 + i % 4][:, tok(b)], Zraw[:, i, b, :], ident[:, :])
                sig(last, "z_turned")
            pe.wait_ge(S("z_ev"), 8)
            pe.wait_ge(S("last_ev"), 4)
            pe.wait_ge(S("gdn_in"), 16)
            pe.wait_ge(S("F_ready"), 1)

            for q, t in enumerate(ORDER):
                kind = int(t == 2)
                if q:
                    pe.wait_ge(S("branch_done"), q)
                q_ = [qkv[:, h, tok(t)] for h in range(4)]
                k_ = [qkv[:, 4 + h, tok(t)] for h in range(4)]
                v_ = [qkv[:, 8 + h, tok(t)] for h in range(4)]
                pe.wait_ge(S("gb"), q + 1)
                for h in range(4):
                    mm(bank[6][:, tok(h)], gb[:, tok(h)], masks[:, kind, 1, :], start=True, stop=True)
                mm(bank[7][:, 0:4], masks[:, kind, 1, :], g_log[:, t, :], start=True, stop=True)
                mm(bank[7][:, 4:8], (same_seq if kind else ones)[:, :], g_log[:, t, :], start=True, stop=True)
                for h in range(4):
                    last = mm(bank[7][:, 8 + 8 * h:16 + 8 * h], gb[:, tok(h)],
                              seq_rows[:, :] if kind else ones[:, 0:8], start=True, stop=True)
                sig(last, "g_mm")
                pe.wait_ge(S("dt"), q + 1)
                for h in range(4):
                    mm(bank[6][:, tok(h)], k_[h], k_[h], start=True, stop=True)
                for h in range(4):
                    last = mm(bank[7][:, tok(h)], k_[h], q_[h], start=True, stop=True)
                sig(last, "kq_mm")
                pe.wait_ge(S("gdn_mat"), q + 1)
                for h in range(HB):
                    if h >= 2:
                        pe.wait_ge(S("rw_mat"), HB * q + h - 1)
                    half, b = slice(64 * (h % 2), 64 * (h % 2) + 64), h // 2
                    f3, f4 = F3[half, b, tok(t)], rwp[half, 4 + b, tok(t)]
                    f1, f2 = F1[half, b, tok(t)], rwp[half, b, tok(t)]
                    for i, (l_, r_) in enumerate(((f3, f1), (f3, f2), (f4, f1), (f4, f2))):
                        last = mm(bank[6 + h % 2][:, tok(i)], l_, r_, start=True, stop=True)
                    sig(last, "rw_mm")
                for l in range(LEVELS[q]):
                    for g in range(3):
                        n = INV0[q] + 3 * l + g
                        pe.wait_ge(S("inv_nl"), n + 1)
                        if l:
                            pe.wait_ge(S("inv_x"), n - 2)
                        for h in range(4):
                            if l:
                                last = mm(bank[g][:, tok(h)], NL[:, g][:, tok(h)], X[:, g][:, tok(h)],
                                          start=True, stop=True)
                            else:
                                last = tr(bank[g][:, tok(h)], NL[:, g][:, tok(h)], ident[:, :])
                        sig(last, "inv_t1")
                    for g in range(3 if l else 0):
                        n = INV0[q] + 3 * l + g
                        pe.wait_ge(S("inv_t1e"), n + 1 - 3 * (q + 1))
                        if l < LEVELS[q] - 1:
                            for h in range(4):
                                mm(bank[3 + g][:, tok(h)], XT[:, g][:, tok(h)], T1[:, g][:, tok(h)],
                                   start=True, stop=True)
                        for h in range(4):
                            last = mm(bank[g][:, tok(h)], T1[:, g][:, tok(h)], XT[:, g][:, tok(h)],
                                      start=True, stop=True)
                        sig(last, "inv_p")
                pe.wait_ge(S("inv_x"), INV0[q] + 3 * LEVELS[q])
                if t < 2:
                    for h in range(4):
                        mm(bank[0][:, tok(h)], k_[h], Sg[:, tok(h)], start=True, stop=True)
                    for h in range(4):
                        mm(bank[1][:, tok(h)], q_[h], Sg[:, tok(h)], start=True, stop=True)
                else:
                    for h in range(4):
                        pe.wait_ge(S("seq_in"), h + 1)
                        for w in range(2):
                            for s in range(NSEQ):
                                last = mm(bank[w][:, tok(h)], sm[:, h % 2, w, s, :], Ss[:, s, h, :],
                                          start=(s == 0), stop=(s == NSEQ - 1))
                        sig(last, "seq_mm")
                for h in range(4):
                    tr(bank[2][:, tok(h)], v_[h], ident[:, :])
                for h in range(4):
                    last = tr(bank[3][:, tok(h)], k_[h], ident[:, :])
                sig(last, "kv_t")
                pe.wait_ge(S("R"), q + 1)
                for h in range(4):
                    last = mm(bank[4][:, tok(h)], XT[:, 0][:, tok(h)], R[:, tok(h)], start=True, stop=True)
                sig(last, "yr_mm")
                pe.wait_ge(S("vn"), q + 1)
                if t < 2:
                    for h in range(4):
                        mm(bank[6][:, tok(h)], Kd[:, tok(h)], vn[:, tok(h)], start=True, stop=True)
                for h in range(4):
                    last = mm(bank[5][:, tok(h)], aT[:, tok(h)], vn[:, tok(h)], start=True, stop=True)
                sig(last, "av_mm")
                if t == 2:
                    for h in range(4):
                        pe.wait_ge(S("seq_rhs"), h + 1)
                        if h >= 2:
                            pe.wait_ge(S("seq_ev"), h - 1)
                        for j in range(2):
                            last = mm(bank[upd_bank(h, j)][:, :], Kd[:, tok(h)],
                                      sm[:, h % 2, 0, 4 * j:4 * j + 4, :].rearrange("p s v -> p (s v)"),
                                      start=True, stop=True)
                        sig(last, "seq_upd")
                pe.wait_ge(S("gdn_done"), q + 1)
                for i, src in enumerate((rwp[:, 8:12, :], F3, rwp[:, 4:8, :])):
                    for b in range(PAIRS):
                        last = tr(bank[[7, 0, 1][i]][:, tok(b)], src[:, b, tok(t)], ident[:, :])
                    sig(last, "rt_t")
                pe.wait_ge(S("rtok"), 3 * q + 3)

                def head_cols(h):
                    return slice(NB * h, NB * h + NB)

                xt_h = [XT[:, 1 + h // 4][:, tok(h % 4)] for h in range(HB)]
                if t < 2:
                    pe.wait_ge(S("zp"), q)
                for b in range(PAIRS):
                    if t < 2:
                        mm(bank[2][:, tok(b)], F1[:, b, tok(t)], Zp[:, tok(b)], start=True, stop=False)
                    else:
                        pe.wait_ge(S("seq_in"), HA + b + 1)
                        for s in range(NSEQ):
                            mm(bank[0][:, tok(b)], sm[:, b % 2, 1, s, :], Zs[:, s, b, :],
                               start=(s == 0), stop=(s == NSEQ - 1))
                        for s in range(NSEQ):
                            last = mm(bank[2][:, tok(b)], sm[:, b % 2, 0, s, :], Zs[:, s, b, :],
                                      start=(s == 0), stop=False)
                        sig(last, "seq_mm")
                    for h in (2 * b, 2 * b + 1):
                        last = mm(bank[2][:, head_cols(h)], MT[:, h, 2 * P:3 * P], vt[:, head_cols(h)],
                                  start=False, stop=(h % 2 == 1))
                sig(last, "w1_mm")
                pe.wait_ge(S("w1n"), q + 1)
                for h in range(HB):
                    last = mm(bank[3][:, head_cols(h)], xt_h[h], W1n[:, head_cols(h)], start=True, stop=True)
                sig(last, "sp_mm")
                pe.wait_ge(S("sp"), q + 1)
                if t < 2:
                    for b in range(PAIRS):
                        mm(bank[5][:, tok(b)], F3t[:, tok(b)], sp[:, tok(b)], start=True, stop=False)
                        mm(bank[5][:, tok(b)], F4t[:, tok(b)], vt[:, tok(b)], start=False, stop=True)
                for b in range(PAIRS):
                    if t < 2:
                        mm(bank[4][:, tok(b)], rwp[:, b, tok(t)], Zp[:, tok(b)], start=True, stop=False)
                    for h in (2 * b, 2 * b + 1):
                        hc = head_cols(h)
                        mm(bank[4][:, hc], MT[:, h, P:2 * P], sp[:, hc], start=(t == 2), stop=False)
                        last = mm(bank[4][:, hc], MT[:, h, 3 * P:4 * P], vt[:, hc], start=False,
                                  stop=(t == 2 or h % 2 == 1))
                sig(last, "ry_mm")
                if t == 2:
                    for b in range(PAIRS):
                        pe.wait_ge(S("seq_rhs"), HA + b + 1)
                        if b >= 2:
                            pe.wait_ge(S("seq_ev"), HA + b - 1)
                        for j in range(2):
                            for w, tk in enumerate((F3t, F4t)):
                                last = mm(bank[upd_bank(b, j)][:, :], tk[:, tok(b)],
                                          sm[:, b % 2, w, 4 * j:4 * j + 4, :].rearrange("p s v -> p (s v)"),
                                          start=(w == 0), stop=(w == 1))
                        sig(last, "seq_upd")
                    pe.wait_ge(S("seq_ev"), HA + PAIRS)
                    pe.wait_ge(S("branch_done"), 1)
                    for i in range(8):
                        if i >= 4:
                            pe.wait_ge(S("z_ev"), 8 + i - 3)
                        for b in range(PAIRS):
                            last = tr(bank[i % 4][:, tok(b)], Zs[:, i, b, :], ident[:, :])
                        sig(last, "z_turned")
                    pe.wait_ge(S("z_ev"), 16)
            pe.wait_ge(S("branch_done"), 3)
            for b in range(PAIRS):
                last = tr(bank[0][:, tok(b)], Zb[:, tok(b)], ident[:, :])
            sig(last, "z_turned")
            for i in range(6):
                if i >= 3:
                    pe.wait_ge(S("yT"), i - 2)
                src = (zs if i < 3 else gate)[:, i % 3, :]
                for b in range(4):
                    last = tr(bank[1 + i % 3][:, tok(b)], src[:, tok(b)], ident[:, :])
                sig(last, "y_t")
            n = NP_MG
            for j in range(4):
                u = ring_wait(N_ADA + len(RING_IN) + j)
                for c in range(4):
                    project(n, u, c)
                    n += 1
            pe.wait_ge(S("yT"), 6)
            pe.wait_ge(S("z_ev"), 17)
            ua = ring_wait(N_ADA + len(RING_IN) + 4)
            ub = ring_wait(N_ADA + len(RING_IN) + 5)
            for c in range(8):
                if c >= 2:
                    pe.wait_ge(S("merged"), c - 1)
                for w, u in enumerate((ua, ub)):
                    pv = flat(ring, 4096, 4096 * u).rearrange("p (k n) -> p k n", k=4)
                    for k in range(4):
                        last = mm(bank[2 * w + c % 2][:, 0:T], pv[:, k, tok(c)], yT[:, w, k, :],
                                  start=(k == 0), stop=(k == 3))
                    sig(last, "pab_mm")
            pe.wait_ge(S("proj_ev"), NP_END)
            for i in range(4):
                for b in range(4):
                    last = tr(bank[4 + i][0:9, tok(b)], modT[:, [16, 20, 40, 44][i] + b, :], ident[:, :])
                sig(last, "ga_t")
            pe.wait_ge(S("ga_r"), 4)
            pe.wait_ge(S("merged"), 8)
            for i in range(8):
                if i >= 4:
                    pe.wait_ge(S("gat_ev"), i - 3)
                sig(mm(bank[i % 4][:, :], req_rows[:, i // 4, :], ga_rows[:, 512 * (i % 4):512 * (i % 4) + 512],
                       start=True, stop=True), "gat_mm")
            pe.wait_ge(S("gat_ev"), 8)
            uo = [ring_wait(N_ADA + len(RING_IN) + 6 + i) for i in range(2)]
            for t in range(3):
                for i in range(2):
                    for k in range(KC):
                        last = mm(bank[[4, 5, 6, 7, 0, 1][2 * t + i]][:, :], merged[:, k, tok(t)], ring[:, uo[i], k, :],
                                  start=(k == 0), stop=(k == KC - 1))
                    sig(last, "wo_mm")
            pe.wait_ge(S("x1"), 3)
            turn_x([2, 3, 4, 5, 6, 7], "x_turned")
            pe.wait_ge(S("hT"), 12)
            for t in range(3):
                for k in range(KC):
                    last = mm(bank[6][:, NE * t:NE * t + NE], hT[:, k, tok(t)], rw_sb[:, k, :],
                              start=(k == 0), stop=(k == KC - 1))
            mm(bank[7][:, 0:1], masks[:, 0, 0, :], ones[:, 0:1], start=True, stop=True)
            last = mm(bank[7][:, P:2 * P], ones[:, :], masks[:, 0, 0, :], start=True, stop=True)
            sig(last, "route_mm")
            for i in range(6):
                for k in range(4):
                    last = tr(bank[i][:, tok(k)], hT[:, 4 * (i % 2) + k, tok(i // 2)], ident[:, :])
                sig(last, "x_turned")

            def s_gate_up(j):
                for k in range(KC):
                    last = mm(bank[6 + j % 2][:, :], hT[:, k, tok(j)], ring[:, 0, k, :],
                              start=(k == 0), stop=(k == KC - 1))
                sig(last, "sgu_mm")

            def s_turn(j):
                pe.wait_ge(S("s_act"), j + 1)
                for k in range(2):
                    last = tr(bank[6 + j % 2][:, tok(k)], act_t[:, j % 2, tok(k)], ident[:, :])
                sig(last, "s_turn")

            def s_down(j):
                pe.wait_ge(S("s_actT"), j + 1)
                for i in range(2):
                    for k in range(2):
                        last = mm(bank[2 * (1 + j % 2) + i][:, :], actT[:, j % 2, tok(k)],
                                  wd_ring[:, 0, k, 512 * i:512 * i + 512], start=(k == 0), stop=(k == 1))
                sig(last, "sdn_mm")

            pe.wait_ge(S("r_gu0"), 32)
            pe.wait_ge(S("scores"), 1)
            s_gate_up(0)
            pe.wait_ge(S("tok_id"), TILES)
            s_gate_up(1)
            s_turn(0)
            pe.wait_ge(S("s_actT"), 1)
            s_gate_up(2)
            pe.wait_ge(S("r_wd0"), 16)
            pe.wait_ge(S("h2_tok"), 6)
            s_down(0)
            s_turn(1)
            s_down(1)
            pe.wait_ge(S("chosen"), TILES)
            for t in range(TILES + 1):
                for t2 in range(min(t + 1, TILES)):
                    last = mm(bank[0][:, NE * t:NE * t + NE], masks[:, 0, 0, :] if t2 == t else ones[:, :],
                              chosen[:, t2, :], start=(t2 == 0), stop=(t2 == min(t, TILES - 1)))
            sig(last, "pos_mm")
            s_turn(2)
            pe.wait_ge(S("y_sh"), 2)
            s_down(2)
            pe.wait_ge(S("slot_rows"), TILES)
            pe.wait_ge(S("most"), 1)
            pe.wait_ge(S("y_sh"), 6)

            def routed(pre, n_task):
                def turn_in(i, u):
                    pe.wait_ge(S(f"r_xg{u % 2}"), i * 48 + 16 * (u // 2 + 1) + done(pre, "xg", u % 2))
                    if not (isinstance(i, int) and i * ROUND + u < 1):
                        pe.wait_ge(S("r_hgA"), i * ROUND + u + done(pre, "hgA"))
                        pe.wait_ge(S("r_hgD"), i * ROUND + u + done(pre, "hgD"))
                    for k in range(KC):
                        last = tr(bank[k // 4][:, tok(k % 4)], xt[:, u % 2, tok(k)], ident[:, :])
                    last.then_inc(S("r_turn"), 1)

                def find(i, u):
                    e = expert_of(pre, i, u)
                    pe.wait_ge(S("r_hot"), i * ROUND + u + 1 + done(pre, "hot"))
                    if not (isinstance(i, int) and i * ROUND + u < 1):
                        pe.wait_ge(S("r_ids"), i * ROUND + u + done(pre, "ids"))
                    for t in range(TILES):
                        last = mm(bank[6][:, 0:3], onehot[:, u % 2, t, :],
                                  slot_rows[:, t, bass.ds(e, 1), :].rearrange("p e c -> p (e c)"),
                                  start=(t == 0), stop=(t == TILES - 1))
                    last.then_inc(S("r_ids_mm"), 1)

                def down(i, u):
                    slot = weight_slot(pre, u)
                    pe.wait_ge(S("r_actT"), i * ROUND + u + 1 + done(pre, "actT"))
                    pe.wait_ge(S(f"r_wd{slot}"), i * 32 + 16 * (u // 3 + 1) + done(pre, "wd", slot))
                    if not (isinstance(i, int) and i * ROUND + u < 1):
                        pe.wait_ge(S("r_oA"), i * ROUND + u + done(pre, "oA"))
                        pe.wait_ge(S("r_oD"), i * ROUND + u + done(pre, "oD"))
                    for j in range(2):
                        for k in range(2):
                            last = mm(bank[4 + j][:, :], actT[:, u % 2, tok(k)],
                                      wd_ring[:, slot, k, 512 * j:512 * j + 512], start=(k == 0), stop=(k == 1))
                    last.then_inc(S("r_dn_mm"), 1)

                def task(i, u):
                    n = i * ROUND + u if isinstance(i, int) else None
                    slot, gu = weight_slot(pre, u), bank[[2, 3, 7][u % 3]]
                    if n is None or n + 1 < n_task:
                        turn_in(i, u + 1)
                    pe.wait_ge(S(f"r_gu{slot}"), i * 64 + 32 * (u // 3 + 1) + done(pre, "gu", slot))
                    pe.wait_ge(S("r_hgA"), i * ROUND + u + 1 + done(pre, "hgA"))
                    pe.wait_ge(S("r_hgD"), i * ROUND + u + 1 + done(pre, "hgD"))
                    if n is None or n >= 3:
                        pe.wait_ge(S("r_actT"), i * ROUND + u - 2 + done(pre, "actT"))
                    for k in range(KC):
                        last = mm(gu[:, :], hgT[:, u % 2, k, :], ring[:, slot, k, :],
                                  start=(k == 0), stop=(k == KC - 1))
                    last.then_inc(S("r_gu_mm"), 1)
                    if n is None or n >= 1:
                        down(i, u - 1)
                    pe.wait_ge(S("r_act"), i * ROUND + u + 1 + done(pre, "act"))
                    for k in range(2):
                        last = tr(gu[:, tok(k)], act_t[:, u % 2, tok(k)], ident[:, :])
                    last.then_inc(S("r_ta"), 1)
                    if n is None or n + 3 < n_task:
                        find(i, u + 3)

                for u in range(3):
                    find(0, u)
                turn_in(0, 0)
                rounds(pe, task, n_task)
                down((n_task - 1) // ROUND, (n_task - 1) % ROUND)

            routed("a", NE)
            with pe.If(pe.value_load(most[0:1, 0:1], min_val=0, max_val=T) > P):
                for i in range(2):
                    pe.wait_ge(S(f"r_sc{i}"), 16 * NE // 2)
                routed("b", 2 * NE)


_INS = ['x_prompt', 'x_sample', 'c_prompt', 'c_sample', 'state_gdn_conv', 'state_gdn', 'state_rwkv_shift',
        'state_rwkv', 'w_ada', 'b_ada', 'w_in', 'conv_w', 'a_log', 'dt_bias', 'gdn_norm_w', 'mu_shift', 'w0',
        'w2', 'a0', 'a2', 'g2', 'k_k', 'k_a', 'r_k', 'lnx_g', 'lnx_b', 'p_a', 'p_b', 'w_o', 'ln1_g', 'ln1_b',
        'router_w', 'router_bias', 'we_gate', 'we_up', 'we_down', 'ws_gate', 'ws_up', 'ws_down', 'ln2_g', 'ln2_b']
_OUTS = [(1, SEQ, D), (NSEQ, LS, D), (1, 1, 3, QKV), (1, 1, HA, P, P), (1, 1, 1, SHIFT_W), (1, 1, HB, NB, NB),
         (1, NSEQ, 3, QKV), (1, NSEQ, HA, P, P), (1, NSEQ, 1, SHIFT_W), (1, NSEQ, HB, NB, NB)]


def kernel(**inputs):
    import numpy as _np
    import concourse.bacc as _bacc
    from concourse.bass_utils import run_bass_kernel_spmd as _run

    nc = _bacc.Bacc("TRN2", target_bir_lowering=False, num_devices=1)
    arrays, args = {}, []
    for name in _INS:
        a = _np.ascontiguousarray(inputs[name])
        arrays[f"in_{name}_dram"] = a
        args.append(nc.dram_tensor(f"in_{name}_dram", a.shape, mybir.dt.from_np(a.dtype), kind="ExternalInput").ap())
    for i, shape in enumerate(_OUTS):
        args.append(nc.dram_tensor(f"out_{i}_dram", shape, F32, kind="ExternalOutput").ap())
    hybrid_kernel(nc, *args)
    r = _run(nc, [arrays], core_ids=[0])
    return tuple(r.results[0][f"out_{i}_dram"] for i in range(len(_OUTS)))
```

```python
import concourse.bass as bass
from concourse import mybir
from contextlib import ExitStack

F32 = mybir.dt.float32
I32 = mybir.dt.int32
ALU = mybir.AluOpType
ACT = mybir.ActivationFunctionType
AX = mybir.AxisListType

P = 128
D = 1024
KC = D // P
SEQ = 256
NSEQ, LS = 8, 16
TILES = 3
T = TILES * P
HA = 4
HB, NB = 8, 64
PAIRS = HB // 2
DB = HB * NB
QKV = 3 * HA * P
QB = QKV // P
SHIFT_W = 3 * DB + 64 + 64 + 128
RB = SHIFT_W // P
OFF_ALPHA = QKV
OFF_Z = QKV + 2 * HA
OFF_RWKV = OFF_Z + HA * P
OFF_MERGE = OFF_RWKV + SHIFT_W
NE, NG, DE = 64, 8, 256
GE = NE // NG
ROUTED_SCALE = 2.5
DN_ALPHA = 2 ** 0.25
LN_EPS, GN_EPS, RMS_EPS, L2_EPS = 1e-5, 64e-5, 1e-6, 1e-6
EXP_NEG_HALF = 0.6065306597126334
QW = 3 + SEQ + NSEQ * (LS + 3)
RW = 1 + SEQ + NSEQ * (LS + 1)
ORDER = [2, 0, 1]
LEVELS = [4, 7, 7]
INV0 = [3 * sum(LEVELS[:q]) for q in range(TILES)]
RING = 3
BIG = 1e30
NOWHERE = 65536
N_ACT = 8
ROUND = 6
C_ADA, C_CONV, C_MU, C_W0, C_A0, C_KK, C_KA, C_RK = 0, 48, 96, 110, 114, 118, 122, 126


def hybrid_kernel(nc, x_prompt, x_sample, c_prompt, c_sample, state_gdn_conv, state_gdn,
                  state_rwkv_shift, state_rwkv, w_ada, b_ada, w_in, conv_w, a_log, dt_bias,
                  gdn_norm_w, mu_shift, w0, w2, a0, a2, g2, k_k, k_a, r_k, lnx_g, lnx_b, p_a, p_b,
                  w_o, ln1_g, ln1_b, router_w, router_bias, we_gate, we_up, we_down, ws_gate,
                  ws_up, ws_down, ln2_g, ln2_b,
                  y_p, y_s, conv_p, gdn_p, shift_p, rwkv_p, conv_s, gdn_s, shift_s, rwkv_s):
    ctx = ExitStack()
    with ctx:
        def sb(name, shape):
            return ctx.enter_context(nc.sbuf_tensor(name, shape, F32))

        sems = {}

        def S(name):
            if name not in sems:
                sems[name] = ctx.enter_context(nc.semaphore(name))
            return sems[name]

        class Steps:

            def __init__(self, eng, own):
                self.eng, self.own, self.n = eng, own, {}

            def do(self, ins, name=None, hold=True):
                name = name or self.own
                self.n[name] = self.n.get(name, 0) + 1
                ins.then_inc(S(name), 1)
                if hold:
                    self.eng.wait_ge(S(name), self.n[name])

        def flat(t, n, off=0):
            names = "abcd"[:len(t.shape) - 1]
            ap = t[tuple([slice(None)] * len(t.shape))]
            if len(names) > 1:
                ap = ap.rearrange(f"p {' '.join(names)} -> p ({' '.join(names)})")
            return ap[:, off:off + n]

        ident = sb("ident", [P, P])
        ones = sb("ones", [P, P])
        blk64 = sb("blk64", [P, P])
        lvl = sb("lvl", [P, 7, P])
        masks = sb("masks", [P, 2, 2, P])
        same_seq = sb("same_seq", [P, P])
        seq_cols = sb("seq_cols", [P, NSEQ, P])
        seq_rows = sb("seq_rows", [P, NSEQ])
        head_sel = sb("head_sel", [P, 2])
        req_rows = sb("req_rows", [9, 2, P])
        par = sb("par", [P, 130])
        a_neg = sb("a_neg", [P, HA])
        dtb = sb("dtb", [P, HA])
        gnw = sb("gnw", [P, P])
        lnx = sb("lnx", [P, 2, DB])
        w_ab = sb("w_ab", [P, KC, 2 * HA])
        hT = sb("hT", [P, KC, T])
        cT = sb("cT", [P, KC, 9])
        modT = sb("modT", [P, 48, 9])
        qkv = sb("qkv", [P, QB, QW])
        rwp = sb("rwp", [P, RB, RW])
        zs = sb("zs", [P, TILES, DB])
        gate = sb("gate", [P, TILES, DB])
        ring = sb("ring", [P, RING, KC, 512])
        last_q = sb("last_q", [P, QB, 9, 3])
        last_r = sb("last_r", [P, RB, 9])
        ab = sb("ab", [P, TILES, 2 * HA])
        g_log = sb("g_log", [P, TILES, HA])
        beta = sb("beta", [P, TILES, HA])
        sp_tmp = sb("sp_tmp", [P, 3, TILES, HA])
        F13 = sb("F13", [P, 2, PAIRS, T])
        F1, F3 = F13[:, 0], F13[:, 1]
        c_mid = sb("c_mid", [P, PAIRS, 2])
        e_mid = sb("e_mid", [P, PAIRS, 2])
        e_tot = sb("e_tot", [P, PAIRS, 2])
        e_seq = sb("e_seq", [P, PAIRS, NSEQ])
        bonus = sb("bonus", [P, TILES, HB])
        NT = sb("NT", [P, 512])
        aT = sb("aT", [P, 512])
        MT = sb("MT", [P, HB, 512])
        inv = sb("inv", [P, 4, 3, 512])
        X, XT, T1, NL = inv[:, 0], inv[:, 1], inv[:, 2], inv[:, 3]
        xs = sb("xs", [P, TILES, D])
        states = sb("states", [P, 1024])
        Sg = states[:, 0:512]
        Zb = states[:, 512:1024]
        gc = sb("gc", [P, 40])
        eg = sb("eg", [P, 40])
        neg_eg = sb("neg_eg", [P, HA])
        stat = sb("stat", [P, 3, 16])
        slot_ids = ctx.enter_context(nc.sbuf_tensor("slot_ids", [P, ROUND, 2], I32))
        slot_gate = sb("slot_gate", [P, ROUND])
        most = ctx.enter_context(nc.sbuf_tensor("most", [P, 1], I32))
        tok_id = sb("tok_id", [P, TILES, 2])
        h_rows = nc.dram_tensor("h_rows", [T, D], F32).ap()
        y_rows = nc.dram_tensor("y_rows", [T * N_ACT, D], F32).ap()

        c_sb = flat(gate, D)[0:9, :]
        mod_part = flat(MT, RING * 512, 1024)[0:105, :].rearrange("p (u n) -> p u n", u=RING)
        part_sel = flat(MT, 9, 928)[0:105, :]
        col_sel = flat(MT, 15, 896)
        half_sel = flat(MT, 14, 912)
        past_r = flat(MT, P)[0:112, :]
        past_q = flat(MT, 3 * P, P).rearrange("p (a c) -> p a c", a=3)[0:96]
        conv_acc = flat(MT, 2 * T, 1024).rearrange("p (a t) -> p a t", a=2)
        shift_tmp = flat(MT, T)
        keep = flat(MT, T, 512)
        par_a = flat(MT, P, 3584)[0:110, :]
        par_b = flat(MT, P, 3712)[0:20, :]
        cum = flat(inv, PAIRS * T).rearrange("p (b t) -> p b t", b=PAIRS)
        kkn = flat(inv, PAIRS * T, PAIRS * T).rearrange("p (b t) -> p b t", b=PAIRS)
        sq = flat(inv, 2 * PAIRS * T, 2 * PAIRS * T).rearrange("p (b t) -> p b t", b=8)
        w2a2 = flat(MT, DB, 2560)
        g2_sb = flat(MT, DB, 3072)
        rs_tmp = flat(MT, 2 * T, 1792).rearrange("p (a t) -> p a t", a=2)
        DT = flat(xs, 512)
        Vt, R, vn, Kd, Ot = [flat(xs, 512, 512 * i) for i in range(1, 6)]
        gb = Ot
        vt, F3t, F4t, Zp, W1n, sp = [flat(xs, 512, 512 * i) for i in range(6)]
        Ss = flat(ring, 4096).rearrange("p (s h v) -> p s h v", s=NSEQ, h=HA)
        Zs = flat(ring, 4096, 4096).rearrange("p (s b v) -> p s b v", s=NSEQ, b=PAIRS)
        Zraw = flat(ring, 4096, 8192).rearrange("p (s b v) -> p s b v", s=NSEQ, b=PAIRS)
        sm = flat(ring, 4096, 8192).rearrange("p (a w s c) -> p a w s c", a=2, w=2, s=NSEQ)
        zout = flat(MT, 512)
        head_rows = NT[0:8, :]
        len_rows = flat(MT, T, 1792 + T)[0:8, :]
        last_out = flat(inv, 512, 4096)
        yT = flat(inv, 2 * PAIRS * T).rearrange("p (w b t) -> p w b t", w=2, b=4)
        ga_rows = flat(inv, 2048, 3072)[0:9, :]
        sg = flat(ring, 16 * T).rearrange("p (b t) -> p b t", b=16)
        mg_w = [flat(ring, 2048, 16 * T + 2048 * i).rearrange("p (k n) -> p k n", k=KC) for i in range(3)]
        pab = [flat(t, 4096).rearrange("p (k n) -> p k n", k=4) for t in (rwp, qkv)]
        w_o_sb = [flat(ring, 4096, 8192).rearrange("p (k n) -> p k n", k=KC),
                  flat(rwp, 4096).rearrange("p (k n) -> p k n", k=KC)]
        merged = flat(MT, 8 * T).rearrange("p (b t) -> p b t", b=8)
        mtmp = flat(MT, 2 * T, 8 * T).rearrange("p (a t) -> p a t", a=2)
        ga_tok = [t.rearrange("p (k n) -> p k n", k=2) for t in (flat(ring, 2 * D, 16 * T), flat(rwp, 2 * D))]
        ln_rows = flat(qkv, 4096).rearrange("p (a n) -> p a n", a=4)
        rw_sb = flat(rwp, 512, 4096).rearrange("p (a n) -> p a n", a=KC)
        r_bias = flat(rwp, NE, 4608)
        lt = flat(zs, 1024)
        wd_ring = flat(inv, 6144).rearrange("p (a k n) -> p a k n", a=3, k=2)
        h2_tok = flat(MT, 3 * D).rearrange("p (t n) -> p t n", t=3)
        xt = flat(MT, 2 * D).rearrange("p (a n) -> p a n", a=2)
        hgT = flat(MT, 2 * D, 2 * D).rearrange("p (a k c) -> p a k c", a=2, k=KC)
        obuf = [flat(zs, D), flat(gate, D)]
        sil = flat(zs, 2 * DE, D).rearrange("p (a n) -> p a n", a=2)
        act_t = flat(gate, 2 * DE, D).rearrange("p (a n) -> p a n", a=2)
        actT = flat(rwp, 2 * DE, 4672).rearrange("p (a n) -> p a n", a=2)
        onehot = flat(qkv, 2 * TILES * P, 4096).rearrange("p (a t c) -> p a t c", a=2, t=TILES)
        slot_rows = flat(states, TILES * NE * 3).rearrange("p (t e c) -> p t e c", t=TILES, c=3)
        pos = flat(states, TILES * NE, 576).rearrange("p (t e) -> p t e", t=TILES)
        count_up = flat(states, P, 768)
        rt = flat(NT, 5 * NE).rearrange("p (a e) -> p a e", a=5)
        r8 = flat(NT, 64, 5 * NE)
        g8 = flat(NT, 32, 5 * NE + 64)
        chosen = flat(aT, TILES * NE).rearrange("p (t e) -> p t e", t=TILES)
        y_sh = flat(F13, 3 * D).rearrange("p (t n) -> p t n", t=TILES)
        y_in = flat(ring, 3 * 4096).rearrange("p (a j n) -> p a j n", a=3, j=4)

        bank = [ctx.enter_context(nc.psum_tensor(f"bank{i}", [P, 512], F32)) for i in range(8)]

        def rw_bank(h):
            return bank[[6, 7, 4, 5][h % 4]]

        MG_STEPS = {(1, "g"): [0], (1, "kq"): [1], (1, "kv"): [7], (1, "av"): [2, 3], (1, "ry"): [6, 7, 2],
                    (2, "g"): [0], (2, "kq"): [1], (2, "kv"): [7], (2, "av"): [2, 3], (2, "ry"): [6, 7, 2]}
        mg_n = 0
        for key, banks in MG_STEPS.items():
            MG_STEPS[key] = [(mg_n + i, bk) for i, bk in enumerate(banks)]
            mg_n += len(banks)
        GA_STEPS = [(which, kind, j) for which in range(2) for kind in range(2) for j in range(2)]

        def ga_bank(i):
            return [0, 1, 2, 3, 6, 7, 6, 7][i]

        def level_half(ap, l, odd):
            return ap.rearrange("p (b two x) -> p b two x", two=2, x=1 << l)[:, :, odd, :]

        def upd_bank(h, j):
            return (6 if h % 2 == 0 else 2) + j

        def seqs(ap, n=LS):
            return ap.rearrange("p (s t) -> p s t", s=NSEQ)

        def tok(t):
            return slice(t * P, (t + 1) * P)

        def col(c):
            return par[:, c:c + 1]

        w_in_v = w_in[0].rearrange("(k p) n -> p k n", p=P)
        w_ada_v = w_ada[0].rearrange("(k p) n -> p k n", p=P)
        w_o_v = w_o[0].rearrange("(k p) n -> p k n", p=P)
        RING_IN = [(OFF_RWKV, 512), (OFF_RWKV + 512, 512), (OFF_RWKV + 1024, 512), (OFF_RWKV + 1536, 256),
                   (OFF_Z, 512), (0, 512), (512, 512), (1024, 512)]
        N_ADA = 12
        N_ADA1 = 4
        RING_SEQ = [("ada", i) for i in range(N_ADA1)]
        for i in range(4):
            RING_SEQ += [("in", i), ("ada", N_ADA1 + 2 * i), ("ada", N_ADA1 + 2 * i + 1)]
        RING_SEQ += [("in", i) for i in range(4, 8)]

        def ring_use(n):
            kind, i = RING_SEQ[n]
            return ("ada_mm", i + 1) if kind == "ada" else ("proj_mm", [4, 8, 12, 14, 17, 21, 25, 29][i])

        def ada_bank(n):
            return bank[[3, 4, 6][n % 3] if n < N_ADA1 else n % 3]

        RING_BASE = [len(range(i, N_ADA + len(RING_IN), RING)) for i in range(RING)]
        RING_MG = [RING_BASE[i] + len(range(i, 8, 3)) for i in range(RING)]
        RING_END = [RING_MG[0] + 2, RING_MG[1] + 1, RING_MG[2] + 1]
        NP_Z, NP_QKV, NP_MG, NP_END = RB, RB + 3, RB + QB + 3, RB + QB + 3 + 16

        def rounds(eng, task, n_task):
            full = (n_task - 3) // ROUND
            for u in range(ROUND):
                task(0, u)
            with eng.Fori(1, full) as i:
                for u in range(ROUND):
                    task(i, u)
            for n in range(full * ROUND, n_task):
                task(n // ROUND, n % ROUND)

        def expert_of(pre, i, u):
            return i * ROUND + u if pre == "a" else i * (ROUND // 2) + u // 2

        def first_slot(pre, u):
            return 0 if pre == "a" else P * (1 + u % 2)

        def weight_slot(pre, u):
            return (u + 1) % 3 if pre == "a" else u % 3

        def done(pre, name, k=0):
            shared = {"gu": 32, "wd": 16}.get(name, 0) if k == 0 else 0
            if pre == "a":
                return shared
            if name in ("xg", "sc"):
                return 16 * NE // 2
            if name in ("gu", "wd"):
                return shared + {"gu": 32, "wd": 16}[name] * sum(weight_slot("a", n) == k for n in range(NE))
            return NE

        block = ctx.enter_context(nc.Block())
        n_const, n_ident = [0], [0]

        @block.gpsimd
        def _(pool):
            st = Steps(pool, "pool_chain")

            def fill(ap, value):
                st.do(pool.memset(ap, value))

            def where(ap, pattern, base, cm, op=ALU.is_ge, other=0.0):
                st.do(pool.affine_select(out=ap, in_=ap, compare_op=op, fill=other, base=base,
                                         pattern=pattern, channel_multiplier=cm))

            def diagonal(ap, lead, n, width):
                where(ap, lead + [[-width, n], [0, width]], 0, 1)
                where(ap, lead + [[width, n], [0, width]], width - 1, -1)

            fill(ident[:, :], 0.0)
            where(ident[:, :], [[-1, P]], 0, 1, ALU.not_equal, 1.0)
            fill(flat(MT, RING * 512, 1024), 0.0)
            fill(flat(MT, 64, 896), 0.0)
            for j in range(4):
                where(part_sel, [[-1, 9]], -32 * j, 1, ALU.not_equal, 1.0)
            n_ident[0] = st.n["pool_chain"]
            fill(ones[:, :], 1.0)
            fill(blk64[:, :], 1.0)
            diagonal(blk64[:, :].rearrange("p (a b) -> p a b", a=2), [], 2, 64)
            fill(qkv[:, :, 0:3], 0.0)
            fill(rwp[:, :, 0:1], 0.0)
            fill(req_rows[:, :, :], 1.0)
            where(req_rows[:, 0, :], [[0, P]], 0, -1)
            where(req_rows[:, 1, :], [[1, P]], LS, -LS)
            where(req_rows[:, 1, :], [[-1, P]], -1, LS)
            fill(keep, 1.0)
            fill(keep[:, 0:SEQ:P], 0.0)
            fill(keep[:, SEQ:T:LS], 0.0)
            fill(head_sel[:, :], 1.0)
            where(head_sel[:, :], [[-64, 2]], 0, 1)
            where(head_sel[:, :], [[64, 2]], 63, -1)
            fill(col_sel[:, 7:8], 1.0)
            fill(head_rows, 0.0)
            where(head_rows.rearrange("p (h c) -> p h c", h=HB), [[-1, HB], [0, NB]], 0, 1, ALU.not_equal, 1.0)
            fill(half_sel[:, 6:8], 1.0)
            where(half_sel[:, 6:8], [[-64, 2]], 0, 1)
            where(half_sel[:, 6:8], [[64, 2]], 63, -1)
            fill(lvl[:, :, :], 1.0)
            for i in range(7):
                n = 1 << i
                v = lvl[:, i, :].rearrange("p (b two x) -> p b two x", two=2, x=n)
                fill(v[:, :, 0, :], 0.0)
                where(v[:, :, 1, :], [[-2 * n, 64 // n], [0, n]], 0, 1)
                where(v[:, :, 1, :], [[2 * n, 64 // n], [0, n]], n - 1, -1)
            fill(masks[:, :, :, :], 1.0)
            for kind in range(2):
                where(masks[:, kind, 0, :], [[1, P]], 0, -1, ALU.is_gt)
                where(masks[:, kind, 1, :], [[1, P]], 0, -1)
            diagonal(masks[:, 1, :, :].rearrange("p a (b c) -> p a b c", b=NSEQ), [[0, 2]], NSEQ, LS)
            fill(same_seq[:, :], 1.0)
            diagonal(same_seq[:, :].rearrange("p (b c) -> p b c", b=NSEQ), [], NSEQ, LS)
            fill(seq_cols[:, :, :], 1.0)
            where(seq_cols[:, :, :], [[-LS, NSEQ], [1, P]], 0, 0)
            where(seq_cols[:, :, :], [[LS, NSEQ], [-1, P]], LS - 1, 0)
            fill(seq_rows[:, :], 1.0)
            where(seq_rows[:, :], [[-LS, NSEQ]], 0, 1)
            where(seq_rows[:, :], [[LS, NSEQ]], LS - 1, -1)
            fill(Sg[:, :], 0.0)
            fill(Zb[:, :], 0.0)
            n_const[0] = st.n["pool_chain"]
            pool.wait_ge(S("proj_mm"), NP_MG)
            pool.wait_ge(S("ab_mm"), 1)
            st.do(pool.memset(flat(ring, 4096, 8192), 0.0), "zraw_clear")
            for q in range(3):
                for l in range(LEVELS[q]):
                    for g in range(3):
                        n = INV0[q] + 3 * l + g
                        if l == 0 and g == 0:
                            pool.wait_ge(S("gdn_mat"), q + 1)
                        if l == 0 and g > 0:
                            pool.wait_ge(S("rw_mat"), HB * q + 4 * g)
                        if n >= 3:
                            pool.wait_ge(S("inv_t1"), n - 2)
                        if l == 1:
                            pool.wait_ge(S("inv_x"), n - 2)
                        src = NT[:, :] if g == 0 else MT[:, 4 * (g - 1):4 * g, 0:P]
                        if g == 0:
                            src = src.rearrange("p (h i) -> p h i", h=4)
                        st.do(pool.tensor_tensor(NL[:, g].rearrange("p (h i) -> p h i", h=4), src,
                                                 lvl[:, l, :].unsqueeze(1).broadcast_to([P, 4, P]),
                                                 ALU.mult), "inv_nl", hold=False)

            pool.wait_ge(S("h_out"), 32 + 16)
            st.do(pool.memset(flat(MT, 2 * D), 0.0))

            def mark():
                pool.sem_inc(S("dma_go"))

            def routed(pre, n_task):
                def gather(i, u):
                    pool.wait_ge(S("r_ids"), i * ROUND + u + 1 + done(pre, "ids"))
                    if not (isinstance(i, int) and i * ROUND + u < 2):
                        pool.wait_ge(S("r_turn"), i * ROUND + u - 1 + done(pre, "turn"))
                    mark()
                    pool.indirect_dma_start(xt[:, u % 2, :], None, h_rows,
                                            bass.IndirectOffsetOnAxis(slot_ids[:, u % ROUND, 0:1], 0),
                                            bounds_check=T - 1, oob_is_err=False
                                            ).then_inc(S(f"r_xg{u % 2}"), 16)

                def scatter(i, u):
                    pool.wait_ge(S("r_oA"), i * ROUND + u + 1 + done(pre, "oA"))
                    pool.wait_ge(S("r_oD"), i * ROUND + u + 1 + done(pre, "oD"))
                    mark()
                    pool.indirect_dma_start(y_rows, bass.IndirectOffsetOnAxis(slot_ids[:, u % ROUND, 1:2], 0),
                                            obuf[u % 2], None, bounds_check=N_ACT * T - 1, oob_is_err=False
                                            ).then_inc(S(f"r_sc{u % 2}"), 16)

                def task(i, u):
                    n = i * ROUND + u if isinstance(i, int) else None
                    if n is None or n + 3 < n_task:
                        gather(i, u + 3)
                    if n is None or n >= 1:
                        scatter(i, u - 1)

                for u in range(3):
                    gather(0, u)
                rounds(pool, task, n_task)
                scatter((n_task - 1) // ROUND, (n_task - 1) % ROUND)
                for par_ in range(2):
                    pool.wait_ge(S(f"r_sc{par_}"), 16 * (n_task // 2) + done(pre, "sc", par_))

            routed("a", NE)
            pool.wait_ge(S("most"), 1)
            with pool.If(pool.value_load(most[0:1, 0:1], min_val=0, max_val=T) > P):
                for i in range(2):
                    pool.wait_ge(S(f"r_sc{i}"), 16 * NE // 2)
                routed("b", 2 * NE)
            st.do(pool.memset(stat[:, 2, 0:1], 0.0), "routed")

        @block.sync
        def _(sp_):
            def load(dst, src, name):
                sp_.dma_start(dst, src).then_inc(S(name), 16)

            load(c_sb[0:1, :], c_prompt, "c_in")
            load(c_sb[1:9, :], c_sample, "c_in")

            def ring_load(n):
                if n >= RING:
                    name, value = ring_use(n - RING)
                    sp_.wait_ge(S(name), value)
                kind, i = RING_SEQ[n]
                c0, w = (512 * i, 512) if kind == "ada" else RING_IN[i]
                load(ring[:, n % RING, :, 0:w], (w_ada_v if kind == "ada" else w_in_v)[:, :, c0:c0 + w], f"ring{n % RING}")

            for n in range(RING):
                ring_load(n)
            load(xs[:, 0:2, :], x_prompt[0].rearrange("(t p) d -> p t d", p=P), "x_in")
            load(xs[:, 2, :], x_sample.rearrange("s t d -> (s t) d"), "x_in")
            for b in range(RB):
                load(past_r[NSEQ * b:NSEQ * (b + 1), :], state_rwkv_shift[0, :, 0, tok(b)], "past_in")
            for b in range(QB):
                load(past_q[24 * (b % 4):24 * (b % 4 + 1), b // 4, :],
                     state_gdn_conv[0, :, :, tok(b)].rearrange("s w c -> (s w) c"), "past_in")
            for n in range(RING, len(RING_SEQ)):
                ring_load(n)

            sp_.wait_ge(S("proj_mm"), NP_MG)
            load(Ss, state_gdn[0].rearrange("s h k v -> k s h v"), "gdn_in")
            sp_.wait_ge(S("zraw_clear"), 1)
            for h in range(2):
                for s in range(NSEQ):
                    load(Zraw[64 * h:64 * h + 64, s, :, 64 * h:64 * h + 64],
                         state_rwkv[0, s, h:HB:2].rearrange("b v k -> v b k"), "rwkv_in")
            for w in range(4):
                sp_.wait_ge(S("last_ev"), w + 1)
                if w < 3:
                    for j in range(4):
                        b, r = 4 * w + j, 27 * j
                        sp_.dma_start(conv_p[0, 0, :, tok(b)], last_out[r:r + 3, tok(w)]).then_inc(S("out"), 16)
                        sp_.dma_start(conv_s[0, :, :, tok(b)].rearrange("s w c -> (s w) c"),
                                      last_out[r + 3:r + 27, tok(w)]).then_inc(S("out"), 16)
                else:
                    for b in range(RB):
                        sp_.dma_start(shift_p[0, 0, :, tok(b)], last_out[9 * b:9 * b + 1, tok(w)]).then_inc(S("out"), 16)
                        sp_.dma_start(shift_s[0, :, 0, tok(b)], last_out[9 * b + 1:9 * b + 9, tok(w)]).then_inc(S("out"), 16)
            n_out = 16 * (24 + 28)
            sp_.wait_ge(S("out"), n_out)
            sp_.wait_ge(S("seq_ev"), HA)
            sp_.dma_start(gdn_s[0].rearrange("s h k v -> k s h v"), Ss).then_inc(S("out"), 16)
            sp_.wait_ge(S("z_ev"), 16)
            for h in range(2):
                for s in range(NSEQ):
                    sp_.dma_start(rwkv_s[0, s, h:HB:2].rearrange("b v k -> v b k"),
                                  Zraw[64 * h:64 * h + 64, s, :, 64 * h:64 * h + 64]).then_inc(S("out"), 16)
            n_out += 16 * 17
            sp_.wait_ge(S("out"), n_out)
            for i in range(8):
                if i >= 3:
                    sp_.wait_ge(S("proj_mm"), NP_MG + 2 * (i - 3) + 2)
                load(mg_w[i % 3], w_in_v[:, :, OFF_MERGE + 256 * i:OFF_MERGE + 256 * (i + 1)], f"ring{i % 3}")
            sp_.wait_ge(S("branch_done"), 3)
            for i in range(2):
                sp_.wait_ge(S(f"ring{i}"), 16 * RING_MG[i])
            load(pab[0], p_a[0].rearrange("(k p) n -> p k n", p=P), "ring0")
            load(pab[1], p_b[0].rearrange("(k p) n -> p k n", p=P), "ring1")
            sp_.dma_start(gdn_p[0, 0].rearrange("h k v -> k h v"),
                          Sg[:, :].rearrange("p (h v) -> p h v", h=4)).then_inc(S("out"), 16)
            sp_.wait_ge(S("z_ev"), 17)
            for h in range(2):
                sp_.dma_start(rwkv_p[0, 0, h:HB:2].rearrange("b v k -> v b k"),
                              zout.rearrange("p (b k) -> p b k", b=4)[64 * h:64 * h + 64, :, 64 * h:64 * h + 64]
                              ).then_inc(S("out"), 16)
            n_out += 48
            sp_.wait_ge(S("proj_mm"), NP_END)
            load(w_o_sb[0], w_o_v[:, :, 0:512], "ring2")
            load(xs[:, 0:2, :], x_prompt[0].rearrange("(t p) d -> p t d", p=P), "x_in")
            load(xs[:, 2, :], x_sample.rearrange("s t d -> (s t) d"), "x_in")
            load(r_bias, router_bias[0].partition_broadcast(P), "ln_in")
            load(rw_sb, router_w[0].rearrange("(k p) n -> p k n", p=P), "ln_in")
            sp_.wait_ge(S("pa_mm"), 8)
            load(w_o_sb[1], w_o_v[:, :, 512:1024], "ring0")
            sp_.wait_ge(S("pb_mm"), 8)
            for i, v in enumerate((ln1_g, ln1_b, ln2_g, ln2_b)):
                load(ln_rows[:, i, :], v[0].partition_broadcast(P), "ln_in")

            def col_w(w):
                return w.rearrange("(k p) n -> p k n", p=P)

            def dyn(w, e):
                return w[0, bass.ds(e, 1)].rearrange("e (k p) n -> p (e k) n", p=P)

            sp_.wait_ge(S("merged"), 8)
            load(ring[:, 0, :, 0:DE], col_w(ws_gate[0]), "r_gu0")
            load(ring[:, 0, :, DE:2 * DE], col_w(ws_up[0]), "r_gu0")
            load(wd_ring[:, 0], col_w(ws_down[0]), "r_wd0")

            def routed(pre, n_task):
                def task(i, u):
                    n = i * ROUND + u if isinstance(i, int) else None
                    slot, e = weight_slot(pre, u), expert_of(pre, i, u)
                    if n is None or n >= 3:
                        sp_.wait_ge(S("r_gu_mm"), i * ROUND + u - 2 + done(pre, "gu_mm"))
                    elif pre == "a" and n == 0:
                        sp_.wait_ge(S("x1"), 3)
                        sp_.wait_ge(S("gat_mm"), 8)
                    elif pre == "a" and n == 2:
                        sp_.wait_ge(S("sgu_mm"), 3)
                    elif pre == "b":
                        sp_.wait_ge(S("r_gu_mm"), NE)
                    sp_.dma_start(ring[:, slot, :, 0:DE], dyn(we_gate, e)).then_inc(S(f"r_gu{slot}"), 16)
                    sp_.dma_start(ring[:, slot, :, DE:2 * DE], dyn(we_up, e)).then_inc(S(f"r_gu{slot}"), 16)
                    if n is None or n >= 3:
                        sp_.wait_ge(S("r_dn_mm"), i * ROUND + u - 2 + done(pre, "dn_mm"))
                    elif pre == "a" and n == 2:
                        sp_.wait_ge(S("sdn_mm"), 3)
                    elif pre == "b":
                        sp_.wait_ge(S("r_dn_mm"), NE)
                    sp_.dma_start(wd_ring[:, slot], dyn(we_down, e)).then_inc(S(f"r_wd{slot}"), 16)

                rounds(sp_, task, n_task)

            routed("a", NE)
            sp_.wait_ge(S("most"), 1)
            with sp_.If(sp_.value_load(most[0:1, 0:1], min_val=0, max_val=T) > P):
                for i in range(2):
                    sp_.wait_ge(S(f"r_sc{i}"), 16 * NE // 2)
                routed("b", 2 * NE)
            sp_.wait_ge(S("routed"), 1)
            y_v = y_rows.rearrange("(t p j) d -> t p j d", p=P, j=N_ACT)
            for j in range(2 * TILES):
                if j >= 3:
                    sp_.wait_ge(S("ys_mm"), j - 2)
                if j == 4:
                    sp_.wait_ge(S("y_used"), 1)
                load(y_in[:, j % 3], y_v[j // 2][:, 4 * (j % 2):4 * (j % 2) + 4, :], f"ring{j % 3}")
            for t in range(TILES):
                sp_.wait_ge(S("y_ready"), t + 1)
                dst = y_p[0, tok(t), :] if t < 2 else y_s.rearrange("s t d -> (s t) d")
                sp_.dma_start(dst, xs[:, t, :]).then_inc(S("out"), 16)
            sp_.wait_ge(S("out"), n_out + 48)

        @block.scalar
        def _(act):
            st = Steps(act, "act_chain")

            def load(dst, src, name):
                act.dma_start(dst, src).then_inc(S(name), 16)

            def f(out, in_, func, name=None, hold=True, **kw):
                st.do(act.activation(out, in_, func, **kw), name, hold)

            def lengths(n):
                act.wait_ge(S("len_mm"), n)
                f(len_rows, bank[n - 1][0:8, 0:T], ACT.Sqrt, "len_ev", hold=False, bias=L2_EPS)

            def root(ap, k):
                act.wait_ge(S("var_in"), k)
                f(ap, ap, ACT.Sqrt, "var_root", hold=False)

            act.wait_ge(S("c_in"), 32)
            f(c_sb, c_sb, ACT.Silu, "c_silu")
            load(par_a[C_ADA:C_ADA + 48, :], b_ada[0].rearrange("(b c) -> b c", c=P), "par_in")
            load(par_a[C_CONV:C_CONV + 48, :], conv_w[0].rearrange("w (b c) -> (w b) c", c=P), "par_in")
            load(par_a[C_MU:C_MU + RB, :], mu_shift[0].rearrange("(b c) -> b c", c=P), "par_in")
            for i, v in enumerate((w0[0], a0[0], k_k[0], k_a[0], r_k[0].rearrange("h n -> (h n)"))):
                load(par_b[4 * i:4 * i + 4, :], v.rearrange("(b c) -> b c", c=P), "par_in")
            load(a_neg[:, :], a_log[0].partition_broadcast(P), "row_in")
            load(dtb[:, :], dt_bias[0].partition_broadcast(P), "row_in")
            load(gnw[:, :], gdn_norm_w[0].partition_broadcast(P), "row_in")
            load(lnx[:, 0, :], lnx_g[0].partition_broadcast(P), "row_in")
            load(lnx[:, 1, :], lnx_b[0].partition_broadcast(P), "row_in")
            def mod_rows(n):
                act.wait_ge(S("ada_mm"), n + 1)
                if n >= RING:
                    act.wait_ge(S("ada_t"), n - RING + 1)
                for j in range(4):
                    rows = slice(32 * j, 32 * j + 9)
                    f(mod_part[rows, n % RING, :], ada_bank(n)[rows, :], ACT.Copy,
                      "ada_row" if j == 3 else "act_chain", hold=False)

            act.wait_ge(S("pool_chain"), n_ident[0])
            for n in range(N_ADA1):
                mod_rows(n)
            load(w2a2[0:64, :], w2[0], "row_in")
            load(w2a2[64:128, :], a2[0], "row_in")
            load(g2_sb, g2[0], "row_in")
            load(w_ab[:, :, :], w_in_v[:, :, OFF_ALPHA:OFF_Z], "row_in")
            def projected(n):
                act.wait_ge(S("proj_mm"), n + 1)
                b = bank[4 + n % 4]
                row, pad = (rwp[:, n, :], 1) if n < RB else (qkv[:, n - NP_QKV, :], 3)
                f(row[:, pad:pad + SEQ], b[:, 0:SEQ], ACT.Copy, hold=False)
                f(row[:, pad + SEQ:].rearrange("p (s t) -> p s t", s=NSEQ)[:, :, pad:], seqs(b[:, SEQ:T]),
                  ACT.Copy, "proj_ev", hold=False)

            def conv_silu(j):
                act.wait_ge(S("conv_sum"), j + 1)
                f(qkv[:, j, 0:T], conv_acc[:, j % 2, :], ACT.Silu, "conv_silu", hold=False)

            def merge_gates(steps):
                for b, bk in steps:
                    act.wait_ge(S("proj_mm"), NP_MG + b + 1)
                    f(sg[:, b, :], bank[bk][:, 0:T], ACT.Sigmoid, "proj_ev", hold=False)

            def mg(q, key):
                merge_gates(MG_STEPS.get((q, key), []))

            act.wait_ge(S("past_ev"), 2)
            for n in range(RB):
                projected(n)
                if n % 4 == 3 or n == RB - 1:
                    mod_rows(N_ADA1 + 2 * (n // 4))
                    mod_rows(N_ADA1 + 2 * (n // 4) + 1)
            act.wait_ge(S("mixed"), RB)
            f(rwp[0:64, 12, 0:T], rwp[0:64, 12, 0:T], ACT.Tanh)
            f(rwp[:, 13, 0:T], rwp[:, 13, 0:T], ACT.Sigmoid, "lora_in")
            for b in range(PAIRS):
                for w, (dst, c) in enumerate(((F1, C_W0), (F3, C_A0))):
                    act.wait_ge(S("lora_mm"), 2 * b + w + 1)
                    f(dst[:, b, :], bank[2 * (b % 2) + w][:, 0:T], ACT.Sigmoid, "lora_ev", hold=False,
                      bias=col(c + b))
            lengths(1)
            for t in range(3):
                act.wait_ge(S("proj_mm"), NP_Z + t + 1)
                f(zs[:, t, :], bank[4 + (NP_Z + t) % 4][:, :], ACT.Silu, "proj_ev", hold=False)
                if t == 0:
                    act.wait_ge(S("decay"), 1)
                    f(e_mid[:, :, :], c_mid[:, :, :], ACT.Exp)
                    f(e_tot[:, :, :], e_tot[:, :, :], ACT.Exp)
                    f(e_seq[:, :, :], e_seq[:, :, :], ACT.Exp, None)
                    f(F1[:, :, :], F1[:, :, :], ACT.Exp, "e_factor")
            for t in range(3):
                act.wait_ge(S("gate_mm"), t + 1)
                f(gate[:, t, :], bank[1 + t][:, :], ACT.Copy, "gate_ev", hold=False)
            act.wait_ge(S("ab_ev"), 2)
            f(beta[:, :, :], ab[:, :, HA:2 * HA], ACT.Sigmoid, "beta")
            act.wait_ge(S("row_in"), 16 * 9)
            f(a_neg[:, :], a_neg[:, :], ACT.Exp)
            f(sp_tmp[:, 2], sp_tmp[:, 1], ACT.Exp)
            f(sp_tmp[:, 2], sp_tmp[:, 2], ACT.Ln, "sp_ln", bias=1.0)
            act.wait_ge(S("kb"), 1)
            f(sq[:, 0:4, :], cum, ACT.Exp, scale=-1.0, name="e_factor")
            f(cum, cum, ACT.Exp, "e_factor")
            for j in range(QB):
                projected(NP_QKV + j)
                if j >= 2:
                    conv_silu(j - 2)
            lengths(2)
            conv_silu(QB - 2)
            conv_silu(QB - 1)
            for w in range(4):
                act.wait_ge(S("last_t"), w + 1)
                f(last_out[0:[108, 108, 108, 126][w], tok(w)], bank[w][0:[108, 108, 108, 126][w], 0:P],
                  ACT.Copy, "last_ev", hold=False)
            for i in range(8):
                act.wait_ge(S("z_turned"), i + 1)
                f(flat(ring, 512, 4096 + 512 * i), bank[4 + i % 4][:, :], ACT.Copy, "z_ev", hold=False)

            for q, t in enumerate(ORDER):
                act.wait_ge(S("gc"), q + 1)
                f(eg[:, :], gc[:, :], ACT.Exp, "decay_exp", hold=False)
                act.wait_ge(S("dt"), q + 1)
                f(DT, DT, ACT.Exp, "decay_exp", hold=False)
                if q == 1:
                    act.wait_ge(S("out"), 16 * (52 + 17))
                mg(q, "g")
                mg(q, "kq")
                for l in range(1, LEVELS[q]):
                    for g in range(3):
                        n = INV0[q] + 3 * l + g
                        act.wait_ge(S("inv_t1"), n + 1)
                        if (q, l, g) == (0, 1, 2):
                            act.wait_ge(S("out"), 16 * 52)
                        f(T1[:, g], bank[g][:, :], ACT.Copy, "inv_t1e", hold=False)
                act.wait_ge(S("kv_t"), q + 1)
                f(Vt, bank[2][:, :], ACT.Copy, "vt_a", hold=False)
                mg(q, "kv")
                root(stat[:, 0, 0:4], 2 * q + 1)
                mg(q, "av")
                for i, dst in enumerate((vt, F3t, F4t)):
                    act.wait_ge(S("rt_t"), 3 * q + i + 1)
                    f(dst, bank[[7, 0, 1][i]][:, :], ACT.Copy, "rtok", hold=False)
                act.wait_ge(S("w1_mm"), q + 1)
                f(W1n, bank[2][:, :], ACT.Copy, "w1n", hold=False, scale=-1.0)
                act.wait_ge(S("sp_mm"), q + 1)
                act.wait_ge(S("gdn_done"), q + 1)
                f(sp, bank[3][:, :], ACT.Copy, "sp", hold=False)
                mg(q, "ry")
                if t < 2:
                    root(stat[:, 1, 0:8], 2 * q + 2)
                else:
                    for i in range(8):
                        if i == 4:
                            root(stat[:, 1, 0:8], 2 * q + 2)
                        act.wait_ge(S("z_turned"), 8 + i + 1)
                        f(flat(ring, 512, 8192 + 512 * i), bank[i % 4][:, :], ACT.Copy, "z_ev", hold=False)
            act.wait_ge(S("z_turned"), 17)
            f(zout, bank[0][:, :], ACT.Copy, "z_ev", hold=False)
            for i in range(4):
                act.wait_ge(S("ga_t"), i + 1)
                f(ga_rows[:, 512 * i:512 * i + 512], bank[[4, 5, 6, 4][i]][0:9, :], ACT.Copy, "ga_r", hold=False)
            act.wait_ge(S("merged"), 8)
            for i, (which, kind, j) in enumerate(GA_STEPS):
                if i == 4:
                    root(stat[:, 1, 1:2], 7)
                    root(stat[:, 1, 1:2], 8)
                act.wait_ge(S("gat_mm"), i + 1)
                f(ga_tok[which][:, kind, 512 * j:512 * j + 512], bank[ga_bank(i)][:, :], ACT.Copy, "gat_ev", hold=False)
            root(stat[:, 1, 1:2], 9)
            act.wait_ge(S("route_mm"), 1)
            f(rt[:, 0:3, :], bank[6][:, 0:3 * NE].rearrange("p (t e) -> p t e", t=3), ACT.Sigmoid, "scores", hold=False)

            for i in range(6):
                act.wait_ge(S("x_turned"), 12 + i + 1)
                f(h2_tok[:, i // 2, 512 * (i % 2):512 * (i % 2) + 512], bank[i][:, :], ACT.Copy, "h2_tok", hold=False)
            act.wait_ge(S("h2_tok"), 6)
            for t in range(3):
                load(h_rows[tok(t), :], h2_tok[:, t, :], "h_out")
            for j in range(3):
                act.wait_ge(S("sgu_mm"), j + 1)
                f(sil[:, j % 2, :], bank[6 + j % 2][:, 0:DE], ACT.Silu, "s_silu", hold=False)
                if j:
                    act.wait_ge(S("s_turn"), j)
                    f(actT[:, (j - 1) % 2, :], bank[6 + (j - 1) % 2][:, 0:2 * P], ACT.Copy, "s_actT", hold=False)
                    if j == 2:
                        act.wait_ge(S("sdn_mm"), 1)
                        for i in range(2):
                            f(y_sh[:, 0, 512 * i:512 * i + 512], bank[2 + i][:, :], ACT.Copy, "y_sh", hold=False)
            act.wait_ge(S("s_turn"), 3)
            f(actT[:, 0, :], bank[6][:, 0:2 * P], ACT.Copy, "s_actT", hold=False)
            for t in range(1, 3):
                act.wait_ge(S("sdn_mm"), t + 1)
                for i in range(2):
                    f(y_sh[:, t, 512 * i:512 * i + 512], bank[2 * (1 + t % 2) + i][:, :], ACT.Copy, "y_sh", hold=False)

            def routed(pre, n_task):
                def turned(i, u):
                    act.wait_ge(S("r_turn"), i * ROUND + u + 1 + done(pre, "turn"))
                    act.activation(hgT[:, u % 2, 0:4, :].rearrange("p k c -> p (k c)"), bank[0][:, :], ACT.Copy
                                   ).then_inc(S("r_hgA"), 1)

                def out_half(i, u):
                    act.wait_ge(S("r_dn_mm"), i * ROUND + u + 1 + done(pre, "dn_mm"))
                    if not (isinstance(i, int) and i * ROUND + u < 2):
                        act.wait_ge(S(f"r_sc{u % 2}"), i * 48 + 16 * ((u - 2) // 2 + 1) + done(pre, "sc", u % 2))
                    act.activation(obuf[u % 2][:, 0:512], bank[4][:, :], ACT.Copy).then_inc(S("r_oA"), 1)

                def task(i, u):
                    n = i * ROUND + u if isinstance(i, int) else None
                    if n is None or n + 1 < n_task:
                        turned(i, u + 1)
                    act.wait_ge(S("r_gu_mm"), i * ROUND + u + 1 + done(pre, "gu_mm"))
                    act.activation(sil[:, u % 2, :], bank[[2, 3, 7][u % 3]][:, 0:DE], ACT.Silu
                                   ).then_inc(S("r_silu"), 1)
                    if n is None or n >= 1:
                        out_half(i, u - 1)
                    act.wait_ge(S("r_ta"), i * ROUND + u + 1 + done(pre, "ta"))
                    act.activation(actT[:, u % 2, :], bank[[2, 3, 7][u % 3]][:, 0:2 * P], ACT.Copy
                                   ).then_inc(S("r_actT"), 1)

                turned(0, 0)
                rounds(act, task, n_task)
                out_half((n_task - 1) // ROUND, (n_task - 1) % ROUND)

            routed("a", NE)
            act.wait_ge(S("most"), 1)
            with act.If(act.value_load(most[0:1, 0:1], min_val=0, max_val=T) > P):
                for i in range(2):
                    act.wait_ge(S(f"r_sc{i}"), 16 * NE // 2)
                routed("b", 2 * NE)
            for t in range(3):
                root(stat[:, 1, 1:2], 10 + t)

        @block.vector
        def _(dve):
            st = Steps(dve, "dve_chain")
            V = nc.vector

            def tt(out, a, b, op, name=None, hold=True):
                st.do(V.tensor_tensor(out, a, b, op), name, hold)

            def ts(out, a, s1, s2, op0, op1=None, name=None, hold=True):
                if op1 is None:
                    st.do(V.tensor_scalar(out, a, s1, None, op0), name, hold)
                else:
                    st.do(V.tensor_scalar(out, a, s1, s2, op0, op1), name, hold)

            def stt(out, a, s, b, op0, op1, name=None, hold=True):
                st.do(V.scalar_tensor_tensor(out=out, in0=a, scalar=s, in1=b, op0=op0, op1=op1), name, hold)

            def cp(out, a, name=None, hold=True):
                st.do(V.tensor_copy(out, a), name, hold)

            def rsum(out, a, name=None):
                st.do(V.tensor_reduce(out, a, AX.X, ALU.add), name)

            def over(ap, n):
                return ap.unsqueeze(2).broadcast_to([P, ap.shape[1], n])

            def inv_root(ap, scale, eps, k):
                ts(ap, ap, scale, eps, ALU.mult, ALU.add, "var_in")
                dve.wait_ge(S("var_root"), k)
                st.do(V.reciprocal(ap, ap))

            dve.wait_ge(S("start_t"), 1)
            cp(cT[:, :, :], bank[1][:, 0:72].rearrange("p (k r) -> p k r", r=9), "start_ev")
            dve.wait_ge(S("pool_chain"), n_const[0])
            dve.wait_ge(S("start_t"), 2)
            cp(par[:, :], bank[0][:, 0:130], "start_ev")
            dve.wait_ge(S("start_t"), 3)
            cp(rwp[:, :, 1 + SEQ:].rearrange("p b (s t) -> p b s t", s=NSEQ)[:, :, :, 0],
               bank[2][:, 0:112].rearrange("p (b s) -> p b s", s=NSEQ), "past_ev")
            qs = qkv[:, :, 3 + SEQ:].rearrange("p b (s t) -> p b s t", s=NSEQ)
            for w in range(3):
                cp(qs[:, :, :, w], bank[2][:, 112:400].rearrange("p (b s w) -> p b s w", s=NSEQ, w=3)[:, :, :, w],
                   "past_ev" if w == 2 else None)
            def mod_blocks(src, b0, b1, plus_one):
                tt(modT[:, b0:b1, :], src[:, 9 * b0:9 * b1].rearrange("p (b r) -> p b r", r=9),
                   over(par[:, b0:b1], 9), ALU.add)
                for b in plus_one:
                    ts(modT[:, b:b + 8, :], modT[:, b:b + 8, :], 1.0, None, ALU.add, name="mod_ev")

            dve.wait_ge(S("ada_t"), N_ADA1)
            mod_blocks(bank[5], 0, 16, [8])

            def modulate(before, shift, scale, banks, tiles=range(TILES)):
                for i in range(6):
                    t, k0 = i // 2, 4 * (i % 2)
                    if t not in tiles:
                        continue
                    dve.wait_ge(S("x_turned"), before + i + 1)
                    src = bank[banks[i]][:, :].rearrange("p (k t) -> p k t", k=4)
                    out = hT[:, k0:k0 + 4, tok(t)]
                    sc, sh = modT[:, scale + k0:scale + k0 + 4, :], modT[:, shift + k0:shift + k0 + 4, :]
                    if t < 2:
                        sc, sh = over(sc[:, :, 0], P), over(sh[:, :, 0], P)
                    else:
                        src, out = [v.rearrange("p k (s t) -> p k s t", s=NSEQ) for v in (src, out)]
                        sc, sh = [v[:, :, 1:9].unsqueeze(3).broadcast_to([P, 4, NSEQ, LS]) for v in (sc, sh)]
                    tt(out, src, sc, ALU.mult)
                    tt(out, out, sh, ALU.add, "hT")

            modulate(0, 0, 8, [0, 2, 3, 4, 6, 7])

            for b in range(RB):
                dve.wait_ge(S("proj_ev"), b + 1)
                row = rwp[:, b, :]
                srow = row[:, 1 + SEQ:].rearrange("p (s t) -> p s t", s=NSEQ)
                cp(last_r[:, b, 0:1], row[:, SEQ:SEQ + 1])
                cp(last_r[:, b, 1:9], srow[:, :, LS])
                tt(shift_tmp[:, 0:SEQ], row[:, 0:SEQ], row[:, 1:1 + SEQ], ALU.subtract)
                tt(seqs(shift_tmp[:, SEQ:T]), srow[:, :, 0:LS], srow[:, :, 1:], ALU.subtract)
                ts(shift_tmp, shift_tmp, col(C_MU + b), None, ALU.mult)
                tt(shift_tmp[:, 0:SEQ], shift_tmp[:, 0:SEQ], row[:, 1:1 + SEQ], ALU.add)
                tt(seqs(shift_tmp[:, SEQ:T]), seqs(shift_tmp[:, SEQ:T]), srow[:, :, 1:], ALU.add)
                cp(row[:, 0:T], shift_tmp, "mixed")
            dve.wait_ge(S("ada_t"), N_ADA)
            mod_blocks(bank[3], 16, 48, [16, 32, 40])
            dve.wait_ge(S("ab_mm"), 1)
            cp(ab[:, :, :], bank[7][:, 0:24].rearrange("p (t c) -> p t c", t=3))
            dve.wait_ge(S("row_in"), 16 * 9)
            tt(sp_tmp[:, 0], ab[:, :, 0:HA], dtb[:, :].unsqueeze(1).broadcast_to([P, 3, HA]), ALU.add)
            ts(sp_tmp[:, 1], sp_tmp[:, 0], -1.0, None, ALU.mult)
            tt(sp_tmp[:, 1], sp_tmp[:, 0], sp_tmp[:, 1], ALU.min, "ab_ev")
            st.do(V.memset(stat[:, 0, 0:1], 0.0), "ab_ev")
            r_, k_ = rwp[:, 0:4, 0:T], rwp[:, 4:8, 0:T]
            for b in range(PAIRS):
                ts(kkn[:, b, :], k_[:, b, :], col(C_KK + b), None, ALU.mult)
            tt(sq[:, 0:4, :], kkn, kkn, ALU.mult, "sq")
            dve.wait_ge(S("lora_ev"), 8)
            ts(F1[:, :, :], F1[:, :, :], -EXP_NEG_HALF, None, ALU.mult)
            for b in range(PAIRS):
                st.do(V.tensor_tensor_scan(cum[:, b, :], keep, F1[:, b, :], 0.0, ALU.mult, ALU.add))
            cp(e_seq[:, :, :], cum[:, :, SEQ + LS - 1:T:LS])
            cp(c_mid[:, :, :], cum[:, :, 63:SEQ:P])
            tt(e_tot[:, :, :], cum[:, :, P - 1:SEQ:P], c_mid[:, :, :], ALU.subtract)
            for t in range(2):
                tt(cum[:, :, tok(t)], cum[:, :, tok(t)], over(c_mid[:, :, t], P), ALU.subtract)
            tt(F1[:, :, :], cum, F1[:, :, :], ALU.subtract, "decay")
            dve.wait_ge(S("len_ev"), 1)
            st.do(V.reciprocal(len_rows, len_rows), "len_inv")
            for b in range(PAIRS):
                dve.wait_ge(S("len_all"), b + 1)
                tt(kkn[:, b, :], kkn[:, b, :], bank[b][:, 0:T], ALU.mult, "len_used")
            for b in range(PAIRS):
                tmp = rs_tmp[:, 0, :]
                ts(tmp, F3[:, b, :], 1.0, col(C_KA + b), ALU.subtract, ALU.mult)
                stt(k_[:, b, :], tmp, 1.0, k_[:, b, :], ALU.add, ALU.mult)
            tt(F3[:, :, :], F3[:, :, :], kkn, ALU.mult)
            for b in range(PAIRS):
                stt(sq[:, 4 + b, :], r_[:, b, :], col(C_RK + b), k_[:, b, :], ALU.mult, ALU.mult,
                    "bonus_in" if b == 3 else None)
            dve.wait_ge(S("e_factor"), 1)
            tt(F1[:, :, :], F1[:, :, :], kkn, ALU.mult, "kb")
            dve.wait_ge(S("e_factor"), 2)
            tt(F3[:, :, :], F3[:, :, :], sq[:, 0:4, :], ALU.mult)
            tt(k_, k_, sq[:, 0:4, :], ALU.mult)
            dve.wait_ge(S("e_factor"), 3)
            tt(r_, r_, cum, ALU.mult, "F_ready")
            for b in range(QB):
                if b == 9:
                    dve.wait_ge(S("bonus_mm"), 1)
                    cp(bonus[:, :, :], bank[0][:, 0:24].rearrange("p (t h) -> p t h", t=3), "bonus_ev")
                    dve.wait_ge(S("conv_silu"), 8)
                    tt(sq, qkv[:, 0:8, 0:T], qkv[:, 0:8, 0:T], ALU.mult, "sq")
                dve.wait_ge(S("proj_ev"), NP_QKV + b + 1)
                row = qkv[:, b, :]
                srow = row[:, 3 + SEQ:].rearrange("p (s t) -> p s t", s=NSEQ)
                cp(last_q[:, b, 0, :], row[:, SEQ:SEQ + 3])
                cp(last_q[:, b, 1:9, :], srow[:, :, LS:LS + 3], "last_q")
                acc = conv_acc[:, b % 2, :]
                if b >= 2:
                    dve.wait_ge(S("conv_silu"), b - 1)
                for w in range(4):
                    c = col(C_CONV + QB * w + b)
                    if w == 0:
                        ts(acc[:, 0:SEQ], row[:, w:w + SEQ], c, None, ALU.mult)
                        ts(seqs(acc[:, SEQ:T]), srow[:, :, w:w + LS], c, None, ALU.mult)
                    else:
                        stt(acc[:, 0:SEQ], row[:, w:w + SEQ], c, acc[:, 0:SEQ], ALU.mult, ALU.add)
                        stt(seqs(acc[:, SEQ:T]), srow[:, :, w:w + LS], c, seqs(acc[:, SEQ:T]), ALU.mult, ALU.add,
                            "conv_sum" if w == 3 else None)
            dve.wait_ge(S("len_ev"), 2)
            st.do(V.reciprocal(len_rows, len_rows), "len_inv")
            for b in range(8):
                dve.wait_ge(S("len_all"), PAIRS + b + 1)
                stt(qkv[:, b, 0:T], qkv[:, b, 0:T], P ** -0.5 if b < 4 else 1.0, bank[b % 4][:, 0:T],
                    ALU.mult, ALU.mult, "len_used")
            dve.wait_ge(S("sp_ln"), 1)
            ts(sp_tmp[:, 0], sp_tmp[:, 0], 0.0, None, ALU.max)
            tt(sp_tmp[:, 0], sp_tmp[:, 0], sp_tmp[:, 2], ALU.add)
            tt(g_log[:, :, :], sp_tmp[:, 0], a_neg[:, :].unsqueeze(1).broadcast_to([P, 3, HA]), ALU.mult)
            ts(g_log[:, :, :], g_log[:, :, :], -1.0, None, ALU.mult)

            for q, t in enumerate(ORDER):
                kind = int(t == 2)
                cp(gb.rearrange("p (h i) -> p h i", h=4), over(g_log[:, t, :], P), "gb")
                dve.wait_ge(S("g_mm"), q + 1)
                cp(gc[:, 0:4], bank[7][:, 0:4])
                tt(gc[:, 4:8], bank[7][:, 4:8], gc[:, 0:4], ALU.subtract)
                cp(gc[:, 8:40], bank[7][:, 8:40], "gc")
                for h in range(4):
                    ts(DT[:, tok(h)], bank[6][:, tok(h)], gc[:, h:h + 1], 0.0, ALU.subtract, ALU.min,
                       "dt" if h == 3 else None)
                dve.wait_ge(S("decay_exp"), 2 * q + 2)
                dve.wait_ge(S("decay_exp"), 2 * q + 1)
                ts(neg_eg[:, :], eg[:, 0:4], -1.0, None, ALU.mult)
                dve.wait_ge(S("kq_mm"), q + 1)
                dve.wait_ge(S("beta"), 1)
                tt(NT[:, :].rearrange("p (h i) -> p h i", h=4), bank[6][:, :].rearrange("p (h i) -> p h i", h=4),
                   over(beta[:, t, :], P), ALU.mult)
                tt(NT[:, :], NT[:, :], DT, ALU.mult)
                tt(aT[:, :], bank[7][:, :], DT, ALU.mult)
                a4 = aT[:, :].rearrange("p (h i) -> p h i", h=4)
                tt(a4, a4, masks[:, kind, 1, :].unsqueeze(1).broadcast_to([P, 4, P]), ALU.mult, "gdn_mat")
                for h in range(HB):
                    dve.wait_ge(S("rw_mm"), HB * q + h + 1)
                    tt(MT[:, h, :].rearrange("p (a i) -> p a i", a=2),
                       rw_bank(h)[:, :].rearrange("p (a i) -> p a i", a=2),
                       masks[:, kind].rearrange("p a i -> p (a i)").unsqueeze(1).broadcast_to([P, 2, 2 * P]),
                       ALU.mult, "rw_mat", hold=False)
                for l in range(LEVELS[q]):
                    for g in range(3):
                        n = INV0[q] + 3 * l + g
                        four = "p (h i) -> p h i"
                        x_g, xt_g = X[:, g].rearrange(four, h=4), XT[:, g].rearrange(four, h=4)
                        if l == 0:
                            idb = ident[:, :].unsqueeze(1).broadcast_to([P, 4, P])
                            dve.wait_ge(S("inv_t1"), n + 1)
                            tt(x_g, idb, bank[g][:, :].rearrange(four, h=4), ALU.subtract, hold=False)
                            dve.wait_ge(S("inv_nl"), n + 1)
                            tt(xt_g, idb, NL[:, g].rearrange(four, h=4), ALU.subtract, "inv_x", hold=False)
                            continue
                        dve.wait_ge(S("inv_p"), n + 1 - 3 * (q + 1))
                        packed = "p (b x) -> p b x"
                        if l < LEVELS[q] - 1:
                            xe = level_half(X[:, g], l, 0)
                            tt(xe, xe, bank[3 + g][:, 0:256].rearrange(packed, x=1 << l), ALU.subtract, hold=False)
                        xo = level_half(XT[:, g], l, 1)
                        tt(xo, xo, bank[g][:, 0:256].rearrange(packed, x=1 << l), ALU.subtract, "inv_x", hold=False)
                if t == 2:
                    for h in range(HA):
                        if h >= 2:
                            dve.wait_ge(S("seq_mm"), h - 1)
                        for w in range(2):
                            src = qkv[:, 4 * (1 - w) + h, tok(2)]
                            tt(sm[:, h % 2, w], src.unsqueeze(1).broadcast_to([P, NSEQ, P]), seq_cols[:, :, :],
                               ALU.mult, "seq_in" if w else None, hold=False)
                dve.wait_ge(S("kv_t"), q + 1)
                four = "p (h i) -> p h i"
                tt(Kd.rearrange(four, h=4), bank[3][:, :].rearrange(four, h=4), over(eg[:, 4:8], P), ALU.mult)
                tt(Ot.rearrange(four, h=4), bank[1][:, :].rearrange(four, h=4), over(eg[:, 0:4], P), ALU.mult)
                dve.wait_ge(S("vt_a"), q + 1)
                for h in range(4):
                    stt(R[:, tok(h)], bank[0][:, tok(h)], neg_eg[:, h:h + 1], Vt[:, tok(h)], ALU.mult, ALU.add,
                        "R" if h == 3 else None)
                dve.wait_ge(S("yr_mm"), q + 1)
                tt(vn.rearrange(four, h=4), bank[4][:, :].rearrange(four, h=4), over(beta[:, t, :], P), ALU.mult, "vn")
                dve.wait_ge(S("av_mm"), q + 1)
                tt(Ot, Ot, bank[5][:, :], ALU.add)
                if t < 2:
                    for h in range(4):
                        stt(Sg[:, tok(h)], Sg[:, tok(h)], eg[:, 8 + 8 * h:9 + 8 * h], bank[6][:, tok(h)],
                            ALU.mult, ALU.add)
                else:
                    def by_seq(h):
                        if h >= 2:
                            dve.wait_ge(S("seq_upd"), h - 1)
                        tt(sm[:, h % 2, 0], vn[:, tok(h)].unsqueeze(1).broadcast_to([P, NSEQ, P]),
                           over(seq_rows[:, :], P), ALU.mult, "seq_rhs", hold=False)

                    by_seq(0)
                    for h in range(4):
                        if h < 3:
                            by_seq(h + 1)
                        tt(Ss[:, :, h, :], Ss[:, :, h, :], over(eg[:, 8 + 8 * h:16 + 8 * h], P), ALU.mult)
                        dve.wait_ge(S("seq_upd"), h + 1)
                        for j in range(2):
                            sl = Ss[:, 4 * j:4 * j + 4, h, :]
                            tt(sl, sl, bank[upd_bank(h, j)][:, :].rearrange("p (s v) -> p s v", s=4), ALU.add,
                               "seq_ev" if j else None, hold=False)
                if t < 2:
                    tt(Zp.rearrange(four, h=4), Zb[:, :].rearrange(four, h=4), over(e_mid[:, :, t], P), ALU.mult, "zp")
                else:
                    def pair_in(b):
                        if b >= 2:
                            dve.wait_ge(S("seq_mm"), HA + b - 1)
                        for w, src in enumerate((F1[:, b, tok(2)], rwp[:, b, tok(2)])):
                            tt(sm[:, b % 2, w], src.unsqueeze(1).broadcast_to([P, NSEQ, P]), seq_cols[:, :, :],
                               ALU.mult, "seq_in" if w else None, hold=False)

                    pair_in(0)
                    pair_in(1)
                O2 = T1[:, 2]
                tt(O2, Ot, Ot, ALU.mult)
                rsum(stat[:, 0, 0:4], O2.rearrange(four, h=4))
                inv_root(stat[:, 0, 0:4], 1.0 / P, RMS_EPS, 2 * q + 1)
                tt(Ot.rearrange(four, h=4), Ot.rearrange(four, h=4), over(stat[:, 0, 0:4], P), ALU.mult)
                tt(Ot.rearrange(four, h=4), Ot.rearrange(four, h=4),
                   gnw[:, :].unsqueeze(1).broadcast_to([P, 4, P]), ALU.mult)
                tt(zs[:, t, :], zs[:, t, :], Ot, ALU.mult, "gdn_done")
                if t == 2:
                    pair_in(2)
                    pair_in(3)
                dve.wait_ge(S("ry_mm"), q + 1)
                Y, Y2 = T1[:, 0], T1[:, 1]
                cp(Y, bank[4][:, :])
                if t < 2:
                    tt(Zb[:, :].rearrange(four, h=4), bank[5][:, :].rearrange(four, h=4),
                       blk64[:, :].unsqueeze(1).broadcast_to([P, 4, P]), ALU.mult)
                    tt(Zb[:, :], Zb[:, :], Zp, ALU.add)
                    tt(Zb[:, :].rearrange(four, h=4), Zb[:, :].rearrange(four, h=4), over(e_tot[:, :, t], P),
                       ALU.mult)
                else:
                    tt(Y, Y, bank[0][:, :], ALU.add)
                    def pair_by_seq(b):
                        if b >= 2:
                            dve.wait_ge(S("seq_upd"), HA + b - 1)
                        for w, src in enumerate((sp, vt)):
                            tt(sm[:, b % 2, w], src[:, tok(b)].unsqueeze(1).broadcast_to([P, NSEQ, P]),
                               over(seq_rows[:, :], P), ALU.mult, "seq_rhs" if w else None, hold=False)

                    upd = flat(inv, 1024).rearrange("p (s v) -> p s v", s=NSEQ)
                    pair_by_seq(0)
                    for b in range(PAIRS):
                        if b < PAIRS - 1:
                            pair_by_seq(b + 1)
                        dve.wait_ge(S("seq_upd"), HA + b + 1)
                        for j in range(2):
                            tt(upd[:, 4 * j:4 * j + 4, :],
                               bank[upd_bank(b, j)][:, :].rearrange("p (s v) -> p s v", s=4),
                               blk64[:, :].unsqueeze(1).broadcast_to([P, 4, P]), ALU.mult)
                        tt(upd, upd, Zs[:, :, b, :], ALU.add)
                        tt(Zs[:, :, b, :], upd, over(e_seq[:, b, :], P), ALU.mult, "seq_ev")
                eight = "p (h v) -> p h v"
                Yh, Y2h = Y.rearrange(eight, h=8), Y2.rearrange(eight, h=8)
                mu8, rs8 = stat[:, 0, 0:8], stat[:, 1, 0:8]
                rsum(mu8, Yh)
                ts(mu8, mu8, 1.0 / NB, None, ALU.mult)
                tt(Yh, Yh, over(mu8, NB), ALU.subtract)
                tt(Y2, Y, Y, ALU.mult)
                rsum(rs8, Y2h)
                inv_root(rs8, 1.0 / NB, GN_EPS, 2 * q + 2)
                tt(Yh, Yh, over(rs8, NB), ALU.mult)
                tt(Y, Y, lnx[:, 0, :], ALU.mult)
                tt(Y, Y, lnx[:, 1, :], ALU.add)
                tt(Y2h, vt.rearrange(eight, h=8), over(bonus[:, t, :], NB), ALU.mult)
                tt(Y, Y, Y2, ALU.add)
                dve.wait_ge(S("gate_ev"), 3)
                tt(gate[:, t, :], gate[:, t, :], Y, ALU.mult, "branch_done")

            for i in range(6):
                dve.wait_ge(S("y_t"), i + 1)
                cp(yT[:, i // 3, :, tok(i % 3)], bank[[7, 2, 3][i % 3]][:, :].rearrange("p (b t) -> p b t", b=4), "yT")
            dve.wait_ge(S("proj_ev"), NP_END)
            dve.wait_ge(S("out"), 16 * (52 + 17 + 3))
            for c in range(8):
                dve.wait_ge(S("pa_mm"), c + 1)
                tt(mtmp[:, 0], bank[[0, 1, 4, 5][c % 4]][:, 0:T], sg[:, c, :], ALU.mult)
                dve.wait_ge(S("pb_mm"), c + 1)
                tt(mtmp[:, 1], bank[2 + c % 2][:, 0:T], sg[:, 8 + c, :], ALU.mult)
                tt(merged[:, c, :], mtmp[:, 0], mtmp[:, 1], ALU.add, "merged")

            def layernorm(t, src_banks, which, name, rest=None):
                kind = int(t == 2)
                for j in range(2):
                    half = slice(512 * j, 512 * j + 512)
                    src = src_banks[j]
                    if rest is not None:
                        tt(lt[:, half], src, rest[:, half], ALU.add, "y_used" if j else None)
                        src = lt[:, half]
                    tt(lt[:, half], src, ga_tok[which][:, kind, 512 * j:512 * j + 512],
                       ALU.mult)
                    stt(xs[:, t, half], xs[:, t, half], DN_ALPHA, lt[:, half], ALU.mult, ALU.add)
                    st.do(V.bn_stats(stat[:, 0, 6 * j:6 * j + 6], xs[:, t, half]))
                st.do(V.bn_aggr(stat[:, 1, 0:2], stat[:, 0, 0:12]))
                inv_root(stat[:, 1, 1:2], 1.0, LN_EPS, 7 + 3 * which + t)
                ts(xs[:, t, :], xs[:, t, :], stat[:, 1, 0:1], stat[:, 1, 1:2], ALU.subtract, ALU.mult)
                tt(xs[:, t, :], xs[:, t, :], ln_rows[:, 2 * which, :], ALU.mult)
                tt(xs[:, t, :], xs[:, t, :], ln_rows[:, 2 * which + 1, :], ALU.add, name)

            dve.wait_ge(S("gat_ev"), 4)
            dve.wait_ge(S("ln_in"), 16 * 6)
            dve.wait_ge(S("x_in"), 64)
            for t in range(TILES):
                dve.wait_ge(S("wo_mm"), 2 * t + 2)
                layernorm(t, [bank[[4, 5, 6, 7, 0, 1][2 * t + j]][:, :] for j in range(2)], 0, "x1")
                if t:
                    modulate(6, 24, 32, [2, 3, 4, 5, 6, 7], [t - 1])
            modulate(6, 24, 32, [2, 3, 4, 5, 6, 7], [2])

            dve.wait_ge(S("scores"), 1)
            cp(count_up, bank[7][:, P:2 * P])
            for t in range(TILES):
                ts(tok_id[:, t, 0:1], bank[7][:, 0:1], float(P * t - NOWHERE), None, ALU.add)
                ts(tok_id[:, t, 1:2], bank[7][:, 0:1], float(N_ACT), float(N_ACT * P * t - 1 - NOWHERE),
                   ALU.mult, ALU.add, "tok_id")
            for t in range(TILES):
                sc, choice, tmp, m = rt[:, t, :], rt[:, 3, :], rt[:, 4, :], chosen[:, t, :]
                tt(choice, sc, r_bias, ALU.add)
                for g in range(NG):
                    st.do(V.max(r8[:, 8 * g:8 * g + 8], choice[:, GE * g:GE * g + GE]), hold=(g == NG - 1))
                gs, gsel = g8[:, 0:8], g8[:, 8:16]
                v8 = r8.rearrange("p (g e) -> p g e", g=NG)
                tt(gs, v8[:, :, 0], v8[:, :, 1], ALU.add)
                st.do(V.max(g8[:, 16:24], gs))
                st.do(V.memset(g8[:, 20:24], 3.0 * BIG))
                st.do(V.match_replace(gsel, g8[:, 16:24], gs, -2.0 * BIG))
                ts(gsel, gsel, -2.0 * BIG, -BIG, ALU.not_equal, ALU.mult)
                tt(choice.rearrange("p (g e) -> p g e", g=NG), choice.rearrange("p (g e) -> p g e", g=NG),
                   over(gsel, GE), ALU.add)
                st.do(V.max(g8[:, 16:24], choice))
                st.do(V.match_replace(tmp, g8[:, 16:24], choice, -2.0 * BIG))
                ts(m, tmp, -2.0 * BIG, None, ALU.is_equal, name="chosen")
                tt(tmp, m, sc, ALU.mult)
                rsum(stat[:, 0, 0:1], tmp)
                ts(stat[:, 0, 0:1], stat[:, 0, 0:1], 1e-20, None, ALU.add)
                st.do(V.reciprocal(stat[:, 0, 1:2], stat[:, 0, 0:1]))
                ts(slot_rows[:, t, :, 2], tmp, stat[:, 0, 1:2], ROUTED_SCALE, ALU.mult, ALU.mult)
                st.do(V.tensor_tensor_scan(tmp, ones[:, 0:NE], m, 0.0, ALU.mult, ALU.add))
                ts(slot_rows[:, t, :, 1], tmp, tok_id[:, t, 1:2], None, ALU.add)
                ts(slot_rows[:, t, :, 0], m, 0.0, tok_id[:, t, 0:1], ALU.mult, ALU.add, "slot_rows")
                dve.wait_ge(S("s_silu"), t + 1)
                tt(act_t[:, t % 2, :], sil[:, t % 2, :], bank[6 + t % 2][:, DE:2 * DE], ALU.mult, "s_act")
            dve.wait_ge(S("pos_mm"), 1)
            stt(pos, bank[0][:, 0:3 * NE].rearrange("p (t e) -> p t e", t=3), 1.0, chosen, ALU.add, ALU.mult)
            ts(pos, pos, 1.0, None, ALU.subtract)
            st.do(V.tensor_reduce(stat[:, 0, 0:1], bank[0][:, 3 * NE:4 * NE], AX.X, ALU.max))
            cp(most[:, :], stat[:, 0, 0:1], "most")

            def routed(pre, n_task):
                def spread(i, u):
                    e = expert_of(pre, i, u)
                    for t in range(TILES):
                        last = V.tensor_scalar(onehot[:, u % 2, t, :], count_up, float(first_slot(pre, u)),
                                               pos[:, t, bass.ds(e, 1)], ALU.add, ALU.is_equal)
                    last.then_inc(S("r_hot"), 1)

                def ids(i, u):
                    dve.wait_ge(S("r_ids_mm"), i * ROUND + u + 1 + done(pre, "ids_mm"))
                    V.tensor_copy(slot_gate[:, u % ROUND:u % ROUND + 1], bank[6][:, 2:3])
                    V.tensor_scalar(slot_ids[:, u % ROUND, :], bank[6][:, 0:2], float(NOWHERE), None, ALU.add
                                    ).then_inc(S("r_ids"), 1)

                def turned(i, u):
                    dve.wait_ge(S("r_turn"), i * ROUND + u + 1 + done(pre, "turn"))
                    V.tensor_copy(hgT[:, u % 2, 4:8, :].rearrange("p k c -> p (k c)"), bank[1][:, :]
                                  ).then_inc(S("r_hgD"), 1)

                def out_half(i, u):
                    dve.wait_ge(S("r_dn_mm"), i * ROUND + u + 1 + done(pre, "dn_mm"))
                    if not (isinstance(i, int) and i * ROUND + u < 2):
                        dve.wait_ge(S(f"r_sc{u % 2}"), i * 48 + 16 * ((u - 2) // 2 + 1) + done(pre, "sc", u % 2))
                    V.tensor_copy(obuf[u % 2][:, 512:1024], bank[5][:, :]).then_inc(S("r_oD"), 1)

                def task(i, u):
                    n = i * ROUND + u if isinstance(i, int) else None
                    if n is None or n + 1 < n_task:
                        turned(i, u + 1)
                    if n is None or n + 3 < n_task:
                        spread(i, u + 3)
                    dve.wait_ge(S("r_silu"), i * ROUND + u + 1 + done(pre, "silu"))
                    dve.wait_ge(S("r_ids"), i * ROUND + u + 1 + done(pre, "ids"))
                    V.scalar_tensor_tensor(out=act_t[:, u % 2, :], in0=sil[:, u % 2, :],
                                           scalar=slot_gate[:, u:u + 1],
                                           in1=bank[[2, 3, 7][u % 3]][:, DE:2 * DE], op0=ALU.mult, op1=ALU.mult
                                           ).then_inc(S("r_act"), 1)
                    if n is None or n >= 1:
                        out_half(i, u - 1)
                    if n is None or n + 3 < n_task:
                        ids(i, u + 3)

                for u in range(3):
                    spread(0, u)
                    ids(0, u)
                turned(0, 0)
                rounds(dve, task, n_task)
                out_half((n_task - 1) // ROUND, (n_task - 1) % ROUND)

            routed("a", NE)
            with dve.If(dve.value_load(most[0:1, 0:1], min_val=0, max_val=T) > P):
                for i in range(2):
                    dve.wait_ge(S(f"r_sc{i}"), 16 * NE // 2)
                routed("b", 2 * NE)
            dve.wait_ge(S("y_sh"), 6)
            for t in range(TILES):
                j = 2 * t + 1
                dve.wait_ge(S(f"ring{j % 3}"), 16 * (RING_END[j % 3] + j // 3 + 1))
                rest = y_in[:, j % 3, 2, :]
                tt(rest, rest, y_in[:, j % 3, 3, :], ALU.add)
                dve.wait_ge(S("ys_mm"), j + 1)
                layernorm(t, [bank[2 * t][:, :], bank[2 * t + 1][:, :]], 1, "y_ready", rest)

        @block.tensor
        def _(pe):
            st = Steps(pe, "pe_chain")
            mm, tr = nc.tensor.matmul, nc.tensor.transpose

            def sig(ins, name):
                st.do(ins, name, hold=False)

            pe.wait_ge(S("pool_chain"), n_ident[0])
            pe.wait_ge(S("c_silu"), 1)
            for k in range(KC):
                last = tr(bank[1][:, 9 * k:9 * k + 9], c_sb[:, tok(k)], ident[0:9, 0:9])
            sig(last, "start_t")

            def turn_x(banks, name, tiles=range(TILES)):
                for i in range(6):
                    t, k0 = i // 2, 4 * (i % 2)
                    if t not in tiles:
                        continue
                    for k in range(4):
                        last = tr(bank[banks[i]][:, tok(k)], xs[:, t, (k0 + k) * P:(k0 + k + 1) * P], ident[:, :])
                    sig(last, name)

            pe.wait_ge(S("start_ev"), 1)
            ring_n = [0] * RING

            def ring_wait(n):
                u = n % RING
                ring_n[u] += 1
                pe.wait_ge(S(f"ring{u}"), 16 * ring_n[u])
                return u

            def modulation(n, n_ring):
                u = ring_wait(n_ring)
                for k in range(KC):
                    last = mm(ada_bank(n)[32 * (k % 4):32 * (k % 4) + 9, :], cT[:, k, :], ring[:, u, k, :],
                              start=(k < 4), stop=(k >= 4))
                sig(last, "ada_mm")

            def turn_modulation(n):
                pe.wait_ge(S("ada_row"), n + 1)
                for c in range(4):
                    last = mm(bank[5 if n < N_ADA1 else 3][:, 36 * n + 9 * c:36 * n + 9 * c + 9],
                              mod_part[:, n % RING, tok(c)], part_sel, start=True, stop=True)
                sig(last, "ada_t")

            for n in range(N_ADA1):
                modulation(n, n)
                if n:
                    turn_modulation(n - 1)
            turn_modulation(N_ADA1 - 1)
            pe.wait_ge(S("pool_chain"), n_const[0])
            pe.wait_ge(S("par_in"), 16 * 8)
            tr(bank[0][:, 0:110], par_a, ident[0:110, 0:110])
            sig(tr(bank[0][:, 110:130], par_b, ident[0:20, 0:20]), "start_t")
            pe.wait_ge(S("past_in"), 16 * (RB + QB))
            tr(bank[2][:, 0:112], past_r, ident[0:112, 0:112])
            for a in range(3):
                last = tr(bank[2][:, 112 + 96 * a:112 + 96 * (a + 1)], past_q[:, a, :], ident[0:96, 0:96])
            sig(last, "start_t")
            pe.wait_ge(S("x_in"), 32)
            pe.wait_ge(S("start_ev"), 2)
            pe.wait_ge(S("past_ev"), 2)
            turn_x([0, 2, 3, 4, 6, 7], "x_turned")
            pe.wait_ge(S("hT"), 6)

            def project(n, u, c):
                if n >= 4:
                    pe.wait_ge(S("proj_ev"), n - 3)
                for k in range(KC):
                    last = mm(bank[4 + n % 4][:, 0:T], ring[:, u, k, tok(c)], hT[:, k, :],
                              start=(k == 0), stop=(k == KC - 1))
                sig(last, "proj_mm")

            def project_ring(j, blocks):
                n_ring = RING_SEQ.index(("in", j))
                u = n_ring % RING
                if blocks[0] == 0:
                    ring_wait(n_ring)
                first = sum(w // P for _, w in RING_IN[:4]) + 3 + 4 * (j - 5) if j > 4 else 4 * j
                for c in blocks:
                    project(first + c, u, c)

            for j in range(4):
                project_ring(j, range(RING_IN[j][1] // P))
                n = N_ADA1 + 2 * j
                modulation(n, RING_SEQ.index(("ada", n)))
                modulation(n + 1, RING_SEQ.index(("ada", n + 1)))
                turn_modulation(n)
                turn_modulation(n + 1)
            pe.wait_ge(S("row_in"), 16 * 9)
            pe.wait_ge(S("proj_ev"), RB)
            for t in range(3):
                for k in range(KC):
                    last = mm(bank[7][:, 8 * t:8 * t + 8], hT[:, k, tok(t)], w_ab[:, k, :],
                              start=(k == 0), stop=(k == KC - 1))
            sig(last, "ab_mm")
            pe.wait_ge(S("lora_in"), 1)
            for b in range(PAIRS):
                for w in range(2):
                    if (b, w) == (1, 1):
                        pe.wait_ge(S("mod_ev"), 4)
                    if b >= 2:
                        pe.wait_ge(S("lora_ev"), 2 * (b - 2) + w + 1)
                    half = slice(64 * w, 64 * w + 64)
                    sig(mm(bank[2 * (b % 2) + w][:, 0:T], w2a2[half, tok(b)], rwp[half, 12, 0:T],
                           start=True, stop=True), "lora_mm")
            pe.wait_ge(S("sq"), 1)
            pe.wait_ge(S("lora_ev"), 5)
            for b in range(PAIRS):
                last = mm(bank[0][0:8, 0:T], half_sel[:, 6 - 2 * b:14 - 2 * b], sq[:, b, :],
                          start=(b == 0), stop=(b == PAIRS - 1))
            sig(last, "len_mm")
            u = ring_wait(N_ADA + 4)
            for t in range(3):
                n = NP_Z + t
                pe.wait_ge(S("proj_ev"), n - 3)
                if t == 1:
                    pe.wait_ge(S("ab_ev"), 2)
                for k in range(KC):
                    last = mm(bank[4 + n % 4][:, :], hT[:, k, tok(t)], ring[:, u, k, :],
                              start=(k == 0), stop=(k == KC - 1))
                sig(last, "proj_mm")
                if t == 1:
                    pe.wait_ge(S("len_inv"), 1)
                    pe.wait_ge(S("lora_ev"), 8)
                    for b in range(PAIRS):
                        sig(mm(bank[b][:, 0:T], head_rows[:, tok(b)], len_rows, start=True, stop=True), "len_all")
            pe.wait_ge(S("len_used"), PAIRS)
            for t in range(3):
                sig(mm(bank[1 + t][:, :], rwp[:, 13, tok(t)], g2_sb, start=True, stop=True), "gate_mm")
            project_ring(5, range(4))
            pe.wait_ge(S("bonus_in"), 1)
            for t in range(3):
                for b in range(PAIRS):
                    last = mm(bank[0][:, 8 * t + 2 * b:8 * t + 2 * b + 2], sq[:, 4 + b, tok(t)], head_sel[:, :],
                              start=True, stop=True)
            sig(last, "bonus_mm")
            project_ring(6, range(4))
            project_ring(7, range(3))
            pe.wait_ge(S("sq"), 2)
            pe.wait_ge(S("gate_ev"), 3)
            for b in range(8):
                last = mm(bank[1][0:8, 0:T], col_sel[:, 7 - b:15 - b], sq[:, b, :], start=(b == 0), stop=(b == 7))
            sig(last, "len_mm")
            project_ring(7, [3])
            pe.wait_ge(S("len_inv"), 2)
            pe.wait_ge(S("bonus_ev"), 1)
            for b in range(8):
                if b >= 4:
                    pe.wait_ge(S("len_used"), PAIRS + b - 3)
                sig(mm(bank[b % 4][:, 0:T], ident[0:8, b:b + 1].broadcast_to([8, P]), len_rows,
                       start=True, stop=True), "len_all")
            pe.wait_ge(S("len_used"), PAIRS + 8)
            pe.wait_ge(S("last_q"), QB)
            for w in range(4):
                if w < 3:
                    src = last_q[:, 4 * w:4 * w + 4, :, :].rearrange("p b s w -> p (b s w)")
                else:
                    src = last_r[:, :, :].rearrange("p b s -> p (b s)")
                sig(tr(bank[w][0:src.shape[1], 0:P], src, ident[:, :]), "last_t")
            pe.wait_ge(S("rwkv_in"), 16 * 16)
            pe.wait_ge(S("proj_ev"), NP_MG)
            for i in range(8):
                if i >= 4:
                    pe.wait_ge(S("z_ev"), i - 3)
                for b in range(PAIRS):
                    last = tr(bank[4 + i % 4][:, tok(b)], Zraw[:, i, b, :], ident[:, :])
                sig(last, "z_turned")
            pe.wait_ge(S("z_ev"), 8)
            pe.wait_ge(S("last_ev"), 4)
            pe.wait_ge(S("gdn_in"), 16)
            pe.wait_ge(S("F_ready"), 1)

            mg_done = [0]

            def merge_gates(steps):
                for b, bk in steps:
                    i = b // 2
                    if b % 2 == 0:
                        pe.wait_ge(S(f"ring{i % 3}"), 16 * (RING_BASE[i % 3] + i // 3 + 1))
                    for k in range(KC):
                        last = mm(bank[bk][:, 0:T], mg_w[i % 3][:, k, tok(b % 2)], hT[:, k, :],
                                  start=(k == 0), stop=(k == KC - 1))
                    sig(last, "proj_mm")
                    mg_done[0] = NP_MG + b + 1

            def mg(q, key):
                merge_gates(MG_STEPS.get((q, key), []))

            def mg_left():
                if mg_done[0]:
                    pe.wait_ge(S("proj_ev"), mg_done[0])

            for q, t in enumerate(ORDER):
                kind = int(t == 2)
                if q:
                    pe.wait_ge(S("branch_done"), q)
                mg_left()
                q_ = [qkv[:, h, tok(t)] for h in range(4)]
                k_ = [qkv[:, 4 + h, tok(t)] for h in range(4)]
                v_ = [qkv[:, 8 + h, tok(t)] for h in range(4)]
                pe.wait_ge(S("gb"), q + 1)
                for h in range(4):
                    mm(bank[6][:, tok(h)], gb[:, tok(h)], masks[:, kind, 1, :], start=True, stop=True)
                mm(bank[7][:, 0:4], masks[:, kind, 1, :], g_log[:, t, :], start=True, stop=True)
                mm(bank[7][:, 4:8], (same_seq if kind else ones)[:, :], g_log[:, t, :], start=True, stop=True)
                for h in range(4):
                    last = mm(bank[7][:, 8 + 8 * h:16 + 8 * h], gb[:, tok(h)],
                              seq_rows[:, :] if kind else ones[:, 0:8], start=True, stop=True)
                sig(last, "g_mm")
                mg(q, "g")
                pe.wait_ge(S("dt"), q + 1)
                for h in range(4):
                    mm(bank[6][:, tok(h)], k_[h], k_[h], start=True, stop=True)
                for h in range(4):
                    last = mm(bank[7][:, tok(h)], k_[h], q_[h], start=True, stop=True)
                sig(last, "kq_mm")
                mg(q, "kq")
                pe.wait_ge(S("gdn_mat"), q + 1)
                for b in range(PAIRS):
                    if b >= 2:
                        pe.wait_ge(S("rw_mat"), HB * q + 2 * b - 2)
                    for i in range(4):
                        for j in range(2):
                            half = slice(64 * j, 64 * j + 64)
                            l_ = (F3[half, b, tok(t)], rwp[half, 4 + b, tok(t)])[i // 2]
                            r_ = (F1[half, b, tok(t)], rwp[half, b, tok(t)])[i % 2]
                            last = mm(rw_bank(2 * b + j)[:, tok(i)], l_, r_, start=True, stop=True)
                            if i == 3:
                                sig(last, "rw_mm")
                mg_left()
                for l in range(LEVELS[q]):
                    for g in range(3):
                        n = INV0[q] + 3 * l + g
                        pe.wait_ge(S("inv_nl"), n + 1)
                        if l:
                            pe.wait_ge(S("inv_x"), n - 2)
                        for h in range(4):
                            if l:
                                last = mm(bank[g][:, tok(h)], NL[:, g][:, tok(h)], X[:, g][:, tok(h)],
                                          start=True, stop=True)
                            else:
                                last = tr(bank[g][:, tok(h)], NL[:, g][:, tok(h)], ident[:, :])
                        sig(last, "inv_t1")
                    for g in range(3 if l else 0):
                        n = INV0[q] + 3 * l + g
                        pe.wait_ge(S("inv_t1e"), n + 1 - 3 * (q + 1))
                        if l < LEVELS[q] - 1:
                            for h in range(4):
                                mm(bank[3 + g][:, 64 * h:64 * h + 64], XT[:, g][:, tok(h)],
                                   level_half(T1[:, g][:, tok(h)], l, 0), start=True, stop=True)
                        for h in range(4):
                            last = mm(bank[g][:, 64 * h:64 * h + 64], T1[:, g][:, tok(h)],
                                      level_half(XT[:, g][:, tok(h)], l, 1), start=True, stop=True)
                        sig(last, "inv_p")
                pe.wait_ge(S("inv_x"), INV0[q] + 3 * LEVELS[q])
                if t < 2:
                    for h in range(4):
                        mm(bank[0][:, tok(h)], k_[h], Sg[:, tok(h)], start=True, stop=True)
                    for h in range(4):
                        mm(bank[1][:, tok(h)], q_[h], Sg[:, tok(h)], start=True, stop=True)
                else:
                    for h in range(4):
                        pe.wait_ge(S("seq_in"), h + 1)
                        for w in range(2):
                            for s in range(NSEQ):
                                last = mm(bank[w][:, tok(h)], sm[:, h % 2, w, s, :], Ss[:, s, h, :],
                                          start=(s == 0), stop=(s == NSEQ - 1))
                        sig(last, "seq_mm")
                for h in range(4):
                    tr(bank[2][:, tok(h)], v_[h], ident[:, :])
                for h in range(4):
                    last = tr(bank[3][:, tok(h)], k_[h], ident[:, :])
                sig(last, "kv_t")
                mg(q, "kv")
                pe.wait_ge(S("R"), q + 1)
                for h in range(4):
                    last = mm(bank[4][:, tok(h)], XT[:, 0][:, tok(h)], R[:, tok(h)], start=True, stop=True)
                sig(last, "yr_mm")
                pe.wait_ge(S("vn"), q + 1)
                if t < 2:
                    for h in range(4):
                        mm(bank[6][:, tok(h)], Kd[:, tok(h)], vn[:, tok(h)], start=True, stop=True)
                for h in range(4):
                    last = mm(bank[5][:, tok(h)], aT[:, tok(h)], vn[:, tok(h)], start=True, stop=True)
                sig(last, "av_mm")
                if t == 2:
                    for h in range(4):
                        pe.wait_ge(S("seq_rhs"), h + 1)
                        if h >= 2:
                            pe.wait_ge(S("seq_ev"), h - 1)
                        for j in range(2):
                            last = mm(bank[upd_bank(h, j)][:, :], Kd[:, tok(h)],
                                      sm[:, h % 2, 0, 4 * j:4 * j + 4, :].rearrange("p s v -> p (s v)"),
                                      start=True, stop=True)
                        sig(last, "seq_upd")
                mg(q, "av")
                mg_left()
                if t == 2:
                    pe.wait_ge(S("seq_ev"), HA)
                for i, src in enumerate((rwp[:, 8:12, :], F3, rwp[:, 4:8, :])):
                    for b in range(PAIRS):
                        last = tr(bank[[7, 0, 1][i]][:, tok(b)], src[:, b, tok(t)], ident[:, :])
                    sig(last, "rt_t")
                pe.wait_ge(S("rtok"), 3 * q + 3)

                def head_cols(h):
                    return slice(NB * h, NB * h + NB)

                xt_h = [XT[:, 1 + h // 4][:, tok(h % 4)] for h in range(HB)]
                if t < 2:
                    pe.wait_ge(S("zp"), q)
                for b in range(PAIRS):
                    if t < 2:
                        mm(bank[2][:, tok(b)], F1[:, b, tok(t)], Zp[:, tok(b)], start=True, stop=False)
                    else:
                        pe.wait_ge(S("seq_in"), HA + b + 1)
                        for s in range(NSEQ):
                            mm(bank[0][:, tok(b)], sm[:, b % 2, 1, s, :], Zs[:, s, b, :],
                               start=(s == 0), stop=(s == NSEQ - 1))
                        for s in range(NSEQ):
                            last = mm(bank[2][:, tok(b)], sm[:, b % 2, 0, s, :], Zs[:, s, b, :],
                                      start=(s == 0), stop=False)
                        sig(last, "seq_mm")
                    for h in (2 * b, 2 * b + 1):
                        last = mm(bank[2][:, head_cols(h)], MT[:, h, 2 * P:3 * P], vt[:, head_cols(h)],
                                  start=False, stop=(h % 2 == 1))
                sig(last, "w1_mm")
                pe.wait_ge(S("w1n"), q + 1)
                for h in range(HB):
                    last = mm(bank[3][:, head_cols(h)], xt_h[h], W1n[:, head_cols(h)], start=True, stop=True)
                sig(last, "sp_mm")
                pe.wait_ge(S("sp"), q + 1)
                if t < 2:
                    for b in range(PAIRS):
                        mm(bank[5][:, tok(b)], F3t[:, tok(b)], sp[:, tok(b)], start=True, stop=False)
                        mm(bank[5][:, tok(b)], F4t[:, tok(b)], vt[:, tok(b)], start=False, stop=True)
                for b in range(PAIRS):
                    if t < 2:
                        mm(bank[4][:, tok(b)], rwp[:, b, tok(t)], Zp[:, tok(b)], start=True, stop=False)
                    for h in (2 * b, 2 * b + 1):
                        hc = head_cols(h)
                        mm(bank[4][:, hc], MT[:, h, P:2 * P], sp[:, hc], start=(t == 2), stop=False)
                        last = mm(bank[4][:, hc], MT[:, h, 3 * P:4 * P], vt[:, hc], start=False,
                                  stop=(t == 2 or h % 2 == 1))
                sig(last, "ry_mm")
                mg(q, "ry")
                if t == 2:
                    for b in range(PAIRS):
                        pe.wait_ge(S("seq_rhs"), HA + b + 1)
                        if b >= 2:
                            pe.wait_ge(S("seq_ev"), HA + b - 1)
                        for j in range(2):
                            for w, tk in enumerate((F3t, F4t)):
                                last = mm(bank[upd_bank(b, j)][:, :], tk[:, tok(b)],
                                          sm[:, b % 2, w, 4 * j:4 * j + 4, :].rearrange("p s v -> p (s v)"),
                                          start=(w == 0), stop=(w == 1))
                        sig(last, "seq_upd")
                    pe.wait_ge(S("seq_ev"), HA + PAIRS)
                    for i in range(8):
                        if i >= 4:
                            pe.wait_ge(S("z_ev"), 8 + i - 3)
                        for b in range(PAIRS):
                            last = tr(bank[i % 4][:, tok(b)], Zs[:, i, b, :], ident[:, :])
                        sig(last, "z_turned")
                    pe.wait_ge(S("z_ev"), 16)
            pe.wait_ge(S("branch_done"), 3)
            mg_left()
            for b in range(PAIRS):
                last = tr(bank[0][:, tok(b)], Zb[:, tok(b)], ident[:, :])
            sig(last, "z_turned")
            for i in range(6):
                if i >= 3:
                    pe.wait_ge(S("yT"), i - 2)
                src = (zs if i < 3 else gate)[:, i % 3, :]
                for b in range(4):
                    last = tr(bank[[7, 2, 3][i % 3]][:, tok(b)], src[:, tok(b)], ident[:, :])
                sig(last, "y_t")
            pe.wait_ge(S("z_ev"), 17)
            for i in range(4):
                for b in range(4):
                    last = tr(bank[[4, 5, 6, 4][i]][0:9, tok(b)], modT[:, [16, 20, 40, 44][i] + b, :], ident[:, :])
                sig(last, "ga_t")
                if i == 2:
                    pe.wait_ge(S("ga_r"), 1)
            pe.wait_ge(S("yT"), 6)
            mg_left()
            pe.wait_ge(S("ga_r"), 4)
            pe.wait_ge(S("ring0"), 16 * (RING_MG[0] + 1))

            def by_p(w, c, bk):
                for k in range(4):
                    last = mm(bank[bk][:, 0:T], pab[w][:, k, tok(c)], yT[:, w, k, :], start=(k == 0), stop=(k == 3))
                sig(last, "pb_mm" if w else "pa_mm")

            for c in range(4):
                by_p(0, c, [0, 1, 4, 5][c])
            pe.wait_ge(S("ring1"), 16 * (RING_MG[1] + 1))
            for c in range(8):
                if c >= 2:
                    pe.wait_ge(S("merged"), c - 1)
                by_p(1, c, 2 + c % 2)
                if c < 4:
                    pe.wait_ge(S("merged"), c + 1)
                    by_p(0, c + 4, [0, 1, 4, 5][c])
            pe.wait_ge(S("merged"), 8)

            def spread(i):
                which, kind, j = GA_STEPS[i]
                if i >= 6:
                    pe.wait_ge(S("gat_ev"), i - 1)
                sig(mm(bank[ga_bank(i)][:, :], req_rows[:, kind, :], ga_rows[:, 512 * (2 * which + j):][:, 0:512],
                       start=True, stop=True), "gat_mm")

            for i in range(4):
                spread(i)
            pe.wait_ge(S("ring2"), 16 * (RING_MG[2] + 1))
            pe.wait_ge(S("ring0"), 16 * (RING_MG[0] + 2))
            for t in range(3):
                if t == 1:
                    pe.wait_ge(S("gat_ev"), 4)
                for i in range(2):
                    for k in range(KC):
                        last = mm(bank[[4, 5, 6, 7, 0, 1][2 * t + i]][:, :], merged[:, k, tok(t)], w_o_sb[i][:, k, :],
                                  start=(k == 0), stop=(k == KC - 1))
                    sig(last, "wo_mm")
                if t:
                    pe.wait_ge(S("x1"), t)
                    turn_x([2, 3, 4, 5, 6, 7], "x_turned", [t - 1])
            for i in range(4, 8):
                spread(i)
            pe.wait_ge(S("gat_ev"), 8)
            pe.wait_ge(S("x1"), 3)
            turn_x([2, 3, 4, 5, 6, 7], "x_turned", [2])
            pe.wait_ge(S("hT"), 12)
            for t in range(3):
                for k in range(KC):
                    last = mm(bank[6][:, NE * t:NE * t + NE], hT[:, k, tok(t)], rw_sb[:, k, :],
                              start=(k == 0), stop=(k == KC - 1))
            mm(bank[7][:, 0:1], masks[:, 0, 0, :], ones[:, 0:1], start=True, stop=True)
            last = mm(bank[7][:, P:2 * P], ones[:, :], masks[:, 0, 0, :], start=True, stop=True)
            sig(last, "route_mm")
            for i in range(6):
                for k in range(4):
                    last = tr(bank[i][:, tok(k)], hT[:, 4 * (i % 2) + k, tok(i // 2)], ident[:, :])
                sig(last, "x_turned")

            def s_gate_up(j):
                for k in range(KC):
                    last = mm(bank[6 + j % 2][:, :], hT[:, k, tok(j)], ring[:, 0, k, :],
                              start=(k == 0), stop=(k == KC - 1))
                sig(last, "sgu_mm")

            def s_turn(j):
                pe.wait_ge(S("s_act"), j + 1)
                for k in range(2):
                    last = tr(bank[6 + j % 2][:, tok(k)], act_t[:, j % 2, tok(k)], ident[:, :])
                sig(last, "s_turn")

            def s_down(j):
                pe.wait_ge(S("s_actT"), j + 1)
                for i in range(2):
                    for k in range(2):
                        last = mm(bank[2 * (1 + j % 2) + i][:, :], actT[:, j % 2, tok(k)],
                                  wd_ring[:, 0, k, 512 * i:512 * i + 512], start=(k == 0), stop=(k == 1))
                sig(last, "sdn_mm")

            pe.wait_ge(S("r_gu0"), 32)
            pe.wait_ge(S("scores"), 1)
            s_gate_up(0)
            pe.wait_ge(S("tok_id"), TILES)
            s_gate_up(1)
            s_turn(0)
            pe.wait_ge(S("s_actT"), 1)
            s_gate_up(2)
            pe.wait_ge(S("r_wd0"), 16)
            pe.wait_ge(S("h2_tok"), 6)
            s_down(0)
            s_turn(1)
            s_down(1)
            pe.wait_ge(S("chosen"), TILES)
            for t in range(TILES + 1):
                for t2 in range(min(t + 1, TILES)):
                    last = mm(bank[0][:, NE * t:NE * t + NE], masks[:, 0, 0, :] if t2 == t else ones[:, :],
                              chosen[:, t2, :], start=(t2 == 0), stop=(t2 == min(t, TILES - 1)))
            sig(last, "pos_mm")
            s_turn(2)
            pe.wait_ge(S("y_sh"), 2)
            s_down(2)
            pe.wait_ge(S("slot_rows"), TILES)
            pe.wait_ge(S("most"), 1)
            pe.wait_ge(S("y_sh"), 6)

            def routed(pre, n_task):
                def turn_in(i, u):
                    pe.wait_ge(S(f"r_xg{u % 2}"), i * 48 + 16 * (u // 2 + 1) + done(pre, "xg", u % 2))
                    if not (isinstance(i, int) and i * ROUND + u < 1):
                        pe.wait_ge(S("r_hgA"), i * ROUND + u + done(pre, "hgA"))
                        pe.wait_ge(S("r_hgD"), i * ROUND + u + done(pre, "hgD"))
                    for k in range(KC):
                        last = tr(bank[k // 4][:, tok(k % 4)], xt[:, u % 2, tok(k)], ident[:, :])
                    last.then_inc(S("r_turn"), 1)

                def find(i, u):
                    e = expert_of(pre, i, u)
                    pe.wait_ge(S("r_hot"), i * ROUND + u + 1 + done(pre, "hot"))
                    if not (isinstance(i, int) and i * ROUND + u < 1):
                        pe.wait_ge(S("r_ids"), i * ROUND + u + done(pre, "ids"))
                    for t in range(TILES):
                        last = mm(bank[6][:, 0:3], onehot[:, u % 2, t, :],
                                  slot_rows[:, t, bass.ds(e, 1), :].rearrange("p e c -> p (e c)"),
                                  start=(t == 0), stop=(t == TILES - 1))
                    last.then_inc(S("r_ids_mm"), 1)

                def down(i, u):
                    slot = weight_slot(pre, u)
                    pe.wait_ge(S("r_actT"), i * ROUND + u + 1 + done(pre, "actT"))
                    pe.wait_ge(S(f"r_wd{slot}"), i * 32 + 16 * (u // 3 + 1) + done(pre, "wd", slot))
                    if not (isinstance(i, int) and i * ROUND + u < 1):
                        pe.wait_ge(S("r_oA"), i * ROUND + u + done(pre, "oA"))
                        pe.wait_ge(S("r_oD"), i * ROUND + u + done(pre, "oD"))
                    for j in range(2):
                        for k in range(2):
                            last = mm(bank[4 + j][:, :], actT[:, u % 2, tok(k)],
                                      wd_ring[:, slot, k, 512 * j:512 * j + 512], start=(k == 0), stop=(k == 1))
                    last.then_inc(S("r_dn_mm"), 1)

                def task(i, u):
                    n = i * ROUND + u if isinstance(i, int) else None
                    slot, gu = weight_slot(pre, u), bank[[2, 3, 7][u % 3]]
                    if n is None or n + 1 < n_task:
                        turn_in(i, u + 1)
                    pe.wait_ge(S(f"r_gu{slot}"), i * 64 + 32 * (u // 3 + 1) + done(pre, "gu", slot))
                    pe.wait_ge(S("r_hgA"), i * ROUND + u + 1 + done(pre, "hgA"))
                    pe.wait_ge(S("r_hgD"), i * ROUND + u + 1 + done(pre, "hgD"))
                    if n is None or n >= 3:
                        pe.wait_ge(S("r_actT"), i * ROUND + u - 2 + done(pre, "actT"))
                    for k in range(KC):
                        last = mm(gu[:, :], hgT[:, u % 2, k, :], ring[:, slot, k, :],
                                  start=(k == 0), stop=(k == KC - 1))
                    last.then_inc(S("r_gu_mm"), 1)
                    if n is None or n >= 1:
                        down(i, u - 1)
                    pe.wait_ge(S("r_act"), i * ROUND + u + 1 + done(pre, "act"))
                    for k in range(2):
                        last = tr(gu[:, tok(k)], act_t[:, u % 2, tok(k)], ident[:, :])
                    last.then_inc(S("r_ta"), 1)
                    if n is None or n + 3 < n_task:
                        find(i, u + 3)

                for u in range(3):
                    find(0, u)
                turn_in(0, 0)
                rounds(pe, task, n_task)
                down((n_task - 1) // ROUND, (n_task - 1) % ROUND)

            routed("a", NE)
            with pe.If(pe.value_load(most[0:1, 0:1], min_val=0, max_val=T) > P):
                for i in range(2):
                    pe.wait_ge(S(f"r_sc{i}"), 16 * NE // 2)
                routed("b", 2 * NE)
            pe.wait_ge(S("routed"), 1)
            pe.wait_ge(S("y_sh"), 6)
            for j in range(2 * TILES):
                t, rows = j // 2, range(4 - 2 * (j % 2))
                pe.wait_ge(S(f"ring{j % 3}"), 16 * (RING_END[j % 3] + j // 3 + 1))
                for i in range(2):
                    half = slice(512 * i, 512 * i + 512)
                    if j % 2 == 0:
                        mm(bank[2 * t + i][:, :], ident[:, :], y_sh[:, t, half], start=True, stop=False)
                    for k in rows:
                        last = mm(bank[2 * t + i][:, :], ident[:, :], y_in[:, j % 3, k, half],
                                  start=False, stop=(j % 2 == 1 and k == rows[-1]))
                sig(last, "ys_mm")


_INS = ['x_prompt', 'x_sample', 'c_prompt', 'c_sample', 'state_gdn_conv', 'state_gdn', 'state_rwkv_shift',
        'state_rwkv', 'w_ada', 'b_ada', 'w_in', 'conv_w', 'a_log', 'dt_bias', 'gdn_norm_w', 'mu_shift', 'w0',
        'w2', 'a0', 'a2', 'g2', 'k_k', 'k_a', 'r_k', 'lnx_g', 'lnx_b', 'p_a', 'p_b', 'w_o', 'ln1_g', 'ln1_b',
        'router_w', 'router_bias', 'we_gate', 'we_up', 'we_down', 'ws_gate', 'ws_up', 'ws_down', 'ln2_g', 'ln2_b']
_OUTS = [(1, SEQ, D), (NSEQ, LS, D), (1, 1, 3, QKV), (1, 1, HA, P, P), (1, 1, 1, SHIFT_W), (1, 1, HB, NB, NB),
         (1, NSEQ, 3, QKV), (1, NSEQ, HA, P, P), (1, NSEQ, 1, SHIFT_W), (1, NSEQ, HB, NB, NB)]


def kernel(**inputs):
    import numpy as _np
    import concourse.bacc as _bacc
    from concourse.bass_utils import run_bass_kernel_spmd as _run

    nc = _bacc.Bacc("TRN2", target_bir_lowering=False, num_devices=1)
    arrays, args = {}, []
    for name in _INS:
        a = _np.ascontiguousarray(inputs[name])
        arrays[f"in_{name}_dram"] = a
        args.append(nc.dram_tensor(f"in_{name}_dram", a.shape, mybir.dt.from_np(a.dtype), kind="ExternalInput").ap())
    for i, shape in enumerate(_OUTS):
        args.append(nc.dram_tensor(f"out_{i}_dram", shape, F32, kind="ExternalOutput").ap())
    hybrid_kernel(nc, *args)
    r = _run(nc, [arrays], core_ids=[0])
    return tuple(r.results[0][f"out_{i}_dram"] for i in range(len(_OUTS)))
```
